# Optimizing a Trainium2 kernel written in Bass

```python
import math
import jax, jax.numpy as jnp
from jax import lax
import numpy as np

D_MODEL = 2048
BATCH = 1
SEQ = 1024
DEPTH = 2

CHUNK = 64
D_MIX = D_MODEL
POOL_WINDOWS = (2, 4, 8, 16)
A_WIDTH = D_MIX // 4
A_GROUP = A_WIDTH // len(POOL_WINDOWS)
B_WIDTH = D_MIX // 2
B_HEAD_DIM = 64
B_HEADS = B_WIDTH // B_HEAD_DIM
B_KV_HEADS = 2
B_WINDOW = 128
B_WINDOW_CHUNKS = B_WINDOW // CHUNK
ROPE_THETA = 500000.0
ROPE_DIM = B_HEAD_DIM // 4
C_WIDTH = D_MIX - A_WIDTH - B_WIDTH
C_HEAD_DIM = 64
C_HEADS = C_WIDTH // C_HEAD_DIM
C_LEFT_CHUNKS = 8
C_BAND_CHUNKS = C_LEFT_CHUNKS + 1
C_MAX_REL = 128
SPLIT_SIZES = (A_WIDTH, A_WIDTH,
               B_WIDTH, B_KV_HEADS * B_HEAD_DIM, B_KV_HEADS * B_HEAD_DIM, B_WIDTH,
               C_WIDTH, C_WIDTH, C_WIDTH, C_WIDTH)
D_IN = sum(SPLIT_SIZES)
VALUE_SLOTS = (0, 4, 8)
DEEPNORM_ALPHA = (2.0 * DEPTH) ** 0.25
DEEPNORM_BETA = (8.0 * DEPTH) ** -0.25
LN_EPS = 1e-5
NEG_INF = -1e30

kernel_name = "hybrid_pool_swa_chunkrel_deepnorm"

def _split_points():
    pts, acc = [], 0
    for s in SPLIT_SIZES[:-1]:
        acc += s
        pts.append(acc)
    return pts

def _layer_norm(x, g, b):
    xf = x.astype(jnp.float32)
    mu = jnp.mean(xf, axis=-1, keepdims=True)
    var = jnp.mean(jnp.square(xf - mu), axis=-1, keepdims=True)
    y = (xf - mu) * lax.rsqrt(var + LN_EPS) * g.astype(jnp.float32) + b.astype(jnp.float32)
    return y.astype(x.dtype)

def pool_mixer(v, group_w, scale):
    bsz, seq, _ = v.shape
    vf = v.astype(jnp.float32)
    cs = jnp.pad(jnp.cumsum(vf, axis=1), ((0, 0), (1, 0), (0, 0)))
    t = jnp.arange(seq, dtype=jnp.float32)
    outs = []
    for gi, w in enumerate(POOL_WINDOWS):
        c = cs[..., gi * A_GROUP:(gi + 1) * A_GROUP]
        upper = c[:, 1:]
        lower = jnp.pad(c[:, :seq - w + 1], ((0, 0), (w - 1, 0), (0, 0)))
        count = jnp.minimum(t + 1.0, float(w))[None, :, None]
        pooled = (upper - lower) / count
        outs.append(pooled - vf[..., gi * A_GROUP:(gi + 1) * A_GROUP])
    y = jnp.stack(outs, axis=2).astype(v.dtype)
    y = jnp.einsum('bsgc,gcd->bsgd', y, group_w).reshape(bsz, seq, A_WIDTH)
    return y * scale

def rope_partial(x, pos):
    half = ROPE_DIM // 2
    inv = ROPE_THETA ** (-jnp.arange(half, dtype=jnp.float32) / half)
    ang = pos.astype(jnp.float32)[:, None] * inv[None, :]
    cos = jnp.cos(ang)[None, :, None, :]
    sin = jnp.sin(ang)[None, :, None, :]
    xr = x[..., :ROPE_DIM].astype(jnp.float32)
    x1, x2 = xr[..., :half], xr[..., half:]
    rot = jnp.concatenate([x1 * cos - x2 * sin, x2 * cos + x1 * sin], axis=-1)
    return jnp.concatenate([rot.astype(x.dtype), x[..., ROPE_DIM:]], axis=-1)

def _chunk_band(t, n_band):
    nc = t.shape[1]
    tp = jnp.pad(t, ((0, 0), (n_band - 1, 0), (0, 0), (0, 0), (0, 0)))
    return jnp.concatenate([tp[:, i:i + nc] for i in range(n_band)], axis=2)

def _band_valid(nc, n_band):
    key_chunk = jnp.arange(nc)[:, None] + jnp.arange(n_band)[None, :] - (n_band - 1)
    return jnp.repeat(key_chunk >= 0, CHUNK, axis=1)

def swa_sink_attention(q, k, v, sinks):
    bsz, seq = q.shape[:2]
    nc = seq // CHUNK
    grp = B_HEADS // B_KV_HEADS
    pos = jnp.arange(seq)
    q = rope_partial(q.reshape(bsz, seq, B_HEADS, B_HEAD_DIM), pos)
    k = rope_partial(k.reshape(bsz, seq, B_KV_HEADS, B_HEAD_DIM), pos)
    qc = q.reshape(bsz, nc, CHUNK, B_KV_HEADS, grp, B_HEAD_DIM)
    kb = _chunk_band(k.reshape(bsz, nc, CHUNK, B_KV_HEADS, B_HEAD_DIM), B_WINDOW_CHUNKS)
    vb = _chunk_band(v.reshape(bsz, nc, CHUNK, B_KV_HEADS, B_HEAD_DIM), B_WINDOW_CHUNKS)
    s = jnp.einsum('bnqhgd,bnkhd->bnhgqk', qc, kb).astype(jnp.float32) * (B_HEAD_DIM ** -0.5)
    valid = _band_valid(nc, B_WINDOW_CHUNKS)
    s = jnp.where(valid[None, :, None, None, None, :], s, NEG_INF)
    sink = jnp.broadcast_to(sinks.astype(jnp.float32).reshape(1, 1, B_KV_HEADS, grp, 1, 1),
                            s.shape[:-1] + (1,))
    p = jax.nn.softmax(jnp.concatenate([s, sink], axis=-1), axis=-1)[..., :-1]
    o = jnp.einsum('bnhgqk,bnkhd->bnqhgd', p.astype(vb.dtype), vb)
    return o.reshape(bsz, seq, B_WIDTH)

def chunk_relbias_attention(q, k, v, rel_bias):
    bsz, seq = q.shape[:2]
    nc = seq // CHUNK
    qc = q.reshape(bsz, nc, CHUNK, C_HEADS, C_HEAD_DIM)
    kb = _chunk_band(k.reshape(bsz, nc, CHUNK, C_HEADS, C_HEAD_DIM), C_BAND_CHUNKS)
    vb = _chunk_band(v.reshape(bsz, nc, CHUNK, C_HEADS, C_HEAD_DIM), C_BAND_CHUNKS)
    s = jnp.einsum('bnqhd,bnkhd->bnhqk', qc, kb).astype(jnp.float32) * (C_HEAD_DIM ** -0.5)
    q_in_band = (C_BAND_CHUNKS - 1) * CHUNK + jnp.arange(CHUNK)
    rel = q_in_band[:, None] - jnp.arange(C_BAND_CHUNKS * CHUNK)[None, :]
    idx = jnp.clip(rel, -C_MAX_REL, C_MAX_REL) + C_MAX_REL
    bias = rel_bias.astype(jnp.float32)[:, idx]
    s = s + bias[None, None]
    valid = _band_valid(nc, C_BAND_CHUNKS)
    s = jnp.where(valid[None, :, None, None, :], s, NEG_INF)
    p = jax.nn.softmax(s, axis=-1)
    o = jnp.einsum('bnhqk,bnkhd->bnqhd', p.astype(vb.dtype), vb)
    return o.reshape(bsz, seq, C_WIDTH)

def hybrid_layer(x, w_in, a_group_w, a_scale, b_sinks, c_rel_bias, w_out, ln_gain, ln_bias):
    h = jnp.einsum('bsd,de->bse', x, w_in)
    a_v, a_gate, b_q, b_k, b_v, b_gate, c_q, c_k, c_v, c_gate = jnp.split(h, _split_points(), axis=-1)
    a_out = pool_mixer(a_v, a_group_w, a_scale) * jax.nn.silu(a_gate)
    b_out = swa_sink_attention(b_q, b_k, b_v, b_sinks) * jax.nn.silu(b_gate)
    c_out = chunk_relbias_attention(c_q, c_k, c_v, c_rel_bias) * jax.nn.silu(c_gate)
    mix = jnp.concatenate([a_out, b_out, c_out], axis=-1)
    y = jnp.einsum('bse,ed->bsd', mix, w_out)
    return _layer_norm(DEEPNORM_ALPHA * x + y, ln_gain, ln_bias)

def setup_inputs(seed: int = 0) -> dict:
    key = jax.random.key(seed)
    ks = jax.random.split(key, 9)
    x = jax.random.normal(ks[0], (BATCH, SEQ, D_MODEL), jnp.float32)
    col_scale = []
    for i, s in enumerate(SPLIT_SIZES):
        col_scale.append(np.full((s,), DEEPNORM_BETA if i in VALUE_SLOTS else 1.0, np.float32))
    col_scale = jnp.asarray(np.concatenate(col_scale))
    w_in = jax.random.normal(ks[1], (DEPTH, D_MODEL, D_IN), jnp.float32) * (D_MODEL ** -0.5) * col_scale
    a_group_w = jax.random.normal(ks[2], (DEPTH, len(POOL_WINDOWS), A_GROUP, A_GROUP), jnp.float32) * (A_GROUP ** -0.5)
    a_scale = 1.0 + 0.1 * jax.random.normal(ks[3], (DEPTH, A_WIDTH), jnp.float32)
    b_sinks = 0.5 * jax.random.normal(ks[4], (DEPTH, B_HEADS), jnp.float32)
    c_rel_bias = 0.5 * jax.random.normal(ks[5], (DEPTH, C_HEADS, 2 * C_MAX_REL + 1), jnp.float32)
    w_out = jax.random.normal(ks[6], (DEPTH, D_MIX, D_MODEL), jnp.float32) * (D_MIX ** -0.5) * DEEPNORM_BETA
    ln_gain = 1.0 + 0.05 * jax.random.normal(ks[7], (DEPTH, D_MODEL), jnp.float32)
    ln_bias = 0.02 * jax.random.normal(ks[8], (DEPTH, D_MODEL), jnp.float32)
    return {"x": x, "w_in": w_in, "a_group_w": a_group_w, "a_scale": a_scale,
            "b_sinks": b_sinks, "c_rel_bias": c_rel_bias, "w_out": w_out,
            "ln_gain": ln_gain, "ln_bias": ln_bias}

def reference(x, w_in, a_group_w, a_scale, b_sinks, c_rel_bias, w_out, ln_gain, ln_bias):
    for l in range(DEPTH):
        x = hybrid_layer(x, w_in[l], a_group_w[l], a_scale[l], b_sinks[l], c_rel_bias[l],
                         w_out[l], ln_gain[l], ln_bias[l])
    return x


_drawn_inputs = setup_inputs


def setup_inputs(seed=0):
    import zlib

    import numpy as np

    out = dict(_drawn_inputs(seed))
    spreads = {}
    factors = {'a_scale': 8.0, 'b_sinks': 8.0, 'c_rel_bias': 8.0}
    for name, (base, spread) in spreads.items():
        noise = np.random.default_rng([zlib.crc32(name.encode()), seed]).standard_normal(out[name].shape)
        drawn = base * np.exp(spread * noise) if base else spread * noise
        out[name] = __import__('jax').numpy.asarray(drawn.astype(out[name].dtype))
    for name, factor in factors.items():
        out[name] = (out[name] * factor).astype(out[name].dtype)
    return out
```

```python
from contextlib import ExitStack

import numpy as np

import concourse.bass as bass
from concourse import mybir

F32 = mybir.dt.float32
F32R = mybir.dt.float32r
ALU = mybir.AluOpType
ACT = mybir.ActivationFunctionType
AX = mybir.AxisListType.X
ds = bass.ds

P = 128
D = 2048
SEQ = 1024
DEPTH = 2
HALF = 512
STEPS = DEPTH * (SEQ // HALF)
KT = D // P
HD = 64
A_WIDTH = D // 4
A_GROUPS = 4
WINDOWS = (2, 4, 8, 16)
B_WIDTH = D // 2
B_HEADS = B_WIDTH // HD
B_TILES = B_HEADS // 2
C_WIDTH = D - A_WIDTH - B_WIDTH
C_PAIRS = C_WIDTH // P
CHUNK = 64
C_KEYS = 640
NEAR = 256
MAX_REL = 128
ROPE_DIM = HD // 4
ROPE_THETA = 500000.0
SCALE = float(HD) ** -0.5
ALPHA = (2.0 * DEPTH) ** 0.25
LN_EPS = 1e-5
NEG_INF = -1e30
QT = HALF // P

UNIT = 512
RING = 4
AHEAD = 3
U_C = 24
U_KV = 8
U_B = 8
U_N = 16
KV0 = C_PAIRS * U_C
B0 = KV0 + U_KV
O0 = B0 + B_TILES * U_B
U_STEP = O0 + 4 * U_N

MIX_A, MIX_B, MIX_C = 0, A_GROUPS, A_GROUPS + B_TILES
MIX_ORDER = list(range(MIX_B)) + list(range(MIX_C, KT)) + list(range(MIX_B, MIX_C))

MIXES = 2 * C_PAIRS + B_TILES
ROTS = 1 + B_TILES
QS = C_PAIRS + ROTS
TZ = 384

SWAP = [i + 8 if i < 8 else i - 8 if i < 16 else i for i in range(32)]


def build(nc, x, wall, a_gw, a_scale, sinks, rel_rev, ln_gain, ln_bias, rope_cos, rope_sin,
          pool_coef, pool_inv, out):
    with ExitStack() as ctx:
        def sb(name, shape, dt=F32):
            return ctx.enter_context(nc.sbuf_tensor(name, shape, dt))

        def psum(name, shape):
            return ctx.enter_context(nc.psum_tensor(name, shape, F32))

        def sem(name):
            return ctx.enter_context(nc.semaphore(name))

        x1 = nc.dram_tensor("x1_scratch", (SEQ, D), F32, kind="Internal").ap()
        res_d = nc.dram_tensor("res_scratch", (4, P, QT, 512), F32, kind="Internal").ap()
        hist_d = nc.dram_tensor("hist_scratch", (C_PAIRS, P, 4, 512), F32, kind="Internal").ap()
        tz_d = nc.dram_tensor("bias_rows_scratch", (DEPTH * 8, P * TZ), F32, kind="Internal").ap()

        xh = sb("xh", [P, KT, HALF], F32R)
        xl = sb("xl", [P, KT, HALF], F32R)
        mixh = sb("mixh", [P, KT, HALF], F32R)
        mixl = sb("mixl", [P, KT, HALF], F32R)
        raw = sb("raw", [P, RING, UNIT])
        wh = sb("wh", [P, RING, UNIT], F32R)
        wl = sb("wl", [P, RING, UNIT], F32R)
        bkh = sb("bkh", [P, P + HALF], F32R)
        bkl = sb("bkl", [P, P + HALF], F32R)
        bvh = sb("bvh", [P, 1 + QT, P], F32R)
        bvl = sb("bvl", [P, 1 + QT, P], F32R)
        bqh = sb("bqh", [P, HALF], F32R)
        bql = sb("bql", [P, HALF], F32R)
        pth = sb("pth", [P, 5, 2, P], F32R)
        ptl = sb("ptl", [P, 5, 2, P], F32R)
        prob = sb("prob", [P, 2, C_KEYS])
        res = sb("res", [P, QT, 512])
        gate = sb("gate", [P, HALF])
        tmp = sb("tmp", [P, HALF])
        av = sb("av", [P, 16 + HALF])
        s0 = sb("s0", [P, 16 + HALF])
        s1 = sb("s1", [P, 16 + HALF])
        brope = sb("brope", [P, 2, 512])
        gw = sb("gw", [P, P])
        gwh = sb("gwh", [P, P], F32R)
        gwl = sb("gwl", [P, P], F32R)
        ident = sb("ident", [P, P])
        a_tail = sb("a_tail", [P, A_GROUPS, 16])
        coef = sb("coef", [P, A_GROUPS, 4])
        inv16 = sb("inv16", [P, A_GROUPS, 16])
        coef1 = sb("coef1", [P, 4])
        inv1 = sb("inv1", [P, 16])
        scale_s = sb("scale_s", [P, DEPTH, A_GROUPS])
        scale1 = sb("scale1", [P, 1])
        sink_s = sb("sink_s", [P, DEPTH, B_TILES, 2])
        sink1 = sb("sink1", [P, 2, 2])
        nmax = sb("nmax", [P, 4, 2])
        mx = sb("mx", [P, 4, 2])
        psums = sb("psums", [P, 4, 2])
        esink = sb("esink", [P, 4, 2])
        rinv = sb("rinv", [P, 4, 2])
        stats = sb("stats", [P, QT, 4, 6])
        mv = sb("mv", [P, QT, 2])
        veps = sb("veps", [P, QT])
        sq = sb("sq", [P, QT])
        sq2 = sb("sq2", [P, QT])
        rstd = sb("rstd", [P, QT])

        ck_h, ck_l = (m[:, MIX_B:MIX_B + 2, :].rearrange("p a n -> p (a n)") for m in (mixh, mixl))
        cv_h, cv_l = (m[:, MIX_B + 2:MIX_B + 4, :].rearrange("p a (b n) -> p (a b) n", n=P) for m in (mixh, mixl))
        cq_h, cq_l = (m[:, MIX_B + 4, :] for m in (mixh, mixl))
        ya_h, ya_l = (m[:, MIX_B + 5, :] for m in (mixh, mixl))

        acc = [psum("acc0", [P, 512]), psum("acc1", [P, 512])]
        sc = [psum("sc0", [P, 1024]), psum("sc1", [P, 1024])]
        pv = psum("pv", [P, 1024])
        pv4 = pv[:, :].rearrange("p (j h q) -> p j h q", j=QT, h=2)
        even_banks = [acc[0][:, :], acc[1][:, :], sc[0][:, 0:512], sc[0][:, 512:1024]]
        odd_banks = [sc[1][:, 0:512], sc[1][:, 512:1024], pv[:, 0:512], pv[:, 512:1024]]

        w_raw = [sem(f"w_raw{i}") for i in range(RING)]
        w_hi = sem("w_hi")
        w_lo = sem("w_lo")
        w_used = sem("w_used")
        vn_full = sem("vn_full")
        a_full = sem("a_full")
        ident_ok = sem("ident_ok")
        const_in = sem("const_in")
        xin = [sem("xin0"), sem("xin1")]
        tr_full = sem("tr_full")
        xh_ok = sem("xh_ok")
        xl_ok = sem("xl_ok")
        av_ok = sem("av_ok")
        ay_ok = sem("ay_ok")
        ayh_ok = sem("ayh_ok")
        ayl_ok = sem("ayl_ok")
        gw_in = sem("gw_in")
        gwh_ok = sem("gwh_ok")
        gwl_ok = sem("gwl_ok")
        vt_ok = sem("vt_ok")
        vh_ok = sem("vh_ok")
        v_ok = sem("v_ok")
        kh_ok = sem("kh_ok")
        k_ok = sem("k_ok")
        qh_ok = sem("qh_ok")
        q_ok = sem("q_ok")
        bq_ok = sem("bq_ok")
        rope_raw = sem("rope_raw")
        rope_ok = sem("rope_ok")
        hist_out = sem("hist_out")
        hist_in = sem("hist_in")
        bias_in = sem("bias_in")
        bias_ok = sem("bias_ok")
        rope_in = sem("rope_in")
        cs_full = sem("cs_full")
        cs_max = sem("cs_max")
        cs_exp = sem("cs_exp")
        cs_prob = sem("cs_prob")
        ct_full = sem("ct_full")
        ct_hi = sem("ct_hi")
        ct_lo = sem("ct_lo")
        c_pv = sem("c_pv")
        bs_full = sem("bs_full")
        bs_max = sem("bs_max")
        bs_exp = sem("bs_exp")
        bs_prob = sem("bs_prob")
        bt_full = sem("bt_full")
        bt_hi = sem("bt_hi")
        bt_lo = sem("bt_lo")
        b_pv = sem("b_pv")
        tanh_ok = sem("tanh_ok")
        gate_ok = sem("gate_ok")
        prod_ok = sem("prod_ok")
        mixh_ok = sem("mixh_ok")
        mixl_ok = sem("mixl_ok")
        out_full = sem("out_full")
        out_free = sem("out_free")
        res_in = sem("res_in")
        res_out = sem("res_out")
        res_ok = sem("res_ok")
        ln_var = sem("ln_var")
        ln_sqrt = sem("ln_sqrt")
        ln_in = sem("ln_in")
        ln_ok = sem("ln_ok")
        ln_out = sem("ln_out")
        tzr_in = sem("tzr_in")
        tzr_ok = sem("tzr_ok")
        tz_out = sem("tz_out")
        hist_mv = sem("hist_mv")
        sp_step = sem("sp_step")
        dve = sem("dve_step")


        def layer(it):
            return it // 2

        def half(it):
            return it % 2

        def x_rows(it):
            src = x if layer(it) == 0 else x1
            return src[half(it) * HALF:(half(it) + 1) * HALF, :]

        def unit(it, r):
            return r + it * U_STEP

        block = ctx.enter_context(nc.Block())

        @block.sync
        def _(sp):
            sp.sem_inc(res_out, 16)

            def wait_alone(semaphore, value):
                sp.wait_ge(semaphore, value)
                sp.sem_inc(sp_step, 1)

            def load_unit(it, r, slot):
                sp.wait_ge(w_lo, unit(it, r) + 1)
                sp.dma_start(raw[:, slot, :], wall[layer(it), ds(r, 1)].rearrange("o p n -> (o p) n")
                             ).then_inc(w_raw[slot], 16)

            def load_ln(it, n):
                sp.wait_ge(res_out, 64 * (it + 1) + 16)
                sp.dma_start(res[:], res_d[ds(n, 1)].rearrange("o p t n -> (o p) t n")).then_inc(ln_in, 16)
                for slot, v in enumerate((ln_gain, ln_bias)):
                    sp.dma_start(prob[:, slot, 0:512], v[layer(it), ds(n, 1), :].to_broadcast([P, 512])
                                 ).then_inc(ln_in, 16)

            def store_ln(it, n):
                wait_alone(ln_ok, n + (4 * it + 1))
                dst = (x1 if layer(it) == 0 else out)[half(it) * HALF:(half(it) + 1) * HALF, :]
                sp.dma_start(dst.rearrange("(t p) (c n) -> c p t n", p=P, n=512)[ds(n, 1)]
                             .rearrange("o p t n -> (o p) t n"), res[:]).then_inc(ln_out, 16)
                wait_alone(ln_out, n * 16 + (64 * it + 16))

            for g in range(2):
                sp.dma_start(prob[:, g, 0:512], x[0:P, g * 512:(g + 1) * 512]).then_inc(xin[g], 16)
            for r in range(RING):
                load_unit(0, r, r)
            sp.dma_start(tmp[0:DEPTH * 8, 127:127 + 257], rel_rev).then_inc(tzr_in, 16)
            sp.dma_start(coef[:], pool_coef).then_inc(const_in, 16)
            sp.dma_start(inv16[:], pool_inv).then_inc(const_in, 16)
            sp.dma_start(scale_s[:], a_scale).then_inc(const_in, 16)
            sp.dma_start(sink_s[:].rearrange("p a b c -> p (a b c)"),
                         sinks.to_broadcast([P, DEPTH * B_HEADS])).then_inc(const_in, 16)
            for g in range(2, 16):
                sp.wait_ge(tr_full, g - 1)
                sp.dma_start(prob[:, g % 2, 0:512],
                             x[(g // 4) * P:(g // 4 + 1) * P, (g % 4) * 512:(g % 4 + 1) * 512]
                             ).then_inc(xin[g % 2], 16)
            sp.wait_ge(tzr_ok, 1)
            sp.dma_start(tz_d.rearrange("h (q c) -> h q c", c=TZ),
                         tmp[0:DEPTH * 8, 0:TZ].rearrange("h (o c) -> h o c", o=1).to_broadcast([DEPTH * 8, P, TZ])
                         ).then_inc(tz_out, 16)
            sp.wait_ge(tz_out, 16)

            for it in range(STEPS):
                with sp.Fori(0, C_PAIRS) as p:
                    for s in range(U_C):
                        if s == 4:
                            sp.wait_ge(gwl_ok, p + (C_PAIRS * it + 1))
                            sp.dma_start(gw[:], a_gw[layer(it), ds(p, 1)].rearrange("o c d -> (o c) d")
                                         ).then_inc(gw_in, 16)
                        if s == 9 and half(it):
                            sp.wait_ge(w_used, unit(it, p * U_C) + (1 + RING))
                            for n, m in enumerate((mixh, mixl)):
                                sp.dma_start(m[:, MIX_B:MIX_B + 3:2, :].bitcast(F32),
                                             hist_d[ds(p, 1), :, 2 * n:2 * n + 2, :].rearrange("o p a n -> (o p) a n")
                                             ).then_inc(hist_in, 16)
                        if s == 10:
                            sp.wait_ge(bias_ok, p + (C_PAIRS * it + 1))
                            if it:
                                sp.wait_ge(rope_ok, (B_TILES + 1) * it)
                            sp.dma_start(brope[:, 0, :].rearrange("p (h n) -> p h n", h=2),
                                         tz_d[ds(2 * p + 8 * layer(it), 2), 127:127 + P * (TZ - 1)]
                                         .rearrange("h (q c) -> q h c", c=TZ - 1)[:, :, 0:NEAR]).then_inc(bias_in, 16)
                        if s == 12 and it:
                            sp.wait_ge(w_used, unit(it, p * U_C) + (1 + RING))
                            load_ln(it - 1, p)
                        if s == 22 and it:
                            store_ln(it - 1, p)
                        if s == 23 and not half(it):
                            wait_alone(k_ok, p + (C_PAIRS * it + 1))
                            wait_alone(v_ok, p + ((C_PAIRS + 1) * it + 1))
                            for n, m in enumerate((mixh, mixl)):
                                sp.dma_start(hist_d[ds(p, 1), :, 2 * n:2 * n + 2, :].rearrange("o p a n -> (o p) a n"),
                                             m[:, MIX_B + 1:MIX_B + 4:2, :].bitcast(F32)).then_inc(hist_out, 16)
                        if it == 0:
                            load_unit(it, p * U_C + (s + RING), s % RING)
                        else:
                            load_unit(it, p * U_C + s, s % RING)
                for s in range(U_KV):
                    if it or s >= RING:
                        load_unit(it, KV0 + s, s % RING)
                sp.wait_ge(cs_max, 8 * C_PAIRS * (it + 1))
                sp.dma_start(brope[:, 0, :], rope_cos[half(it)]).then_inc(rope_in, 16)
                sp.dma_start(brope[:, 1, :], rope_sin[half(it)]).then_inc(rope_in, 16)
                with sp.Fori(0, B_TILES) as i:
                    for s in range(U_B):
                        load_unit(it, i * U_B + (B0 + s), s % RING)
                with sp.Fori(0, 2) as m:
                    for s in range(2 * U_N):
                        load_unit(it, m * (2 * U_N) + (O0 + s), s % RING)
                        for gg in range(8):
                            if it + 1 == STEPS or s != (8, 9, 11, 13, 15, 17, 19, 21)[gg]:
                                continue
                            sp.wait_ge(tr_full, m * 8 + (16 * (it + 1) + gg - 1))
                            sp.wait_ge(bt_full, 4 * B_TILES * (it + 1))
                            src = x_rows(it + 1).rearrange("(t p) (k n) -> t k p n", p=P, n=512)
                            sp.dma_start(prob[:, gg % 2, 0:512],
                                         src[ds(2 * m + gg // 4, 1), gg % 4].rearrange("o p n -> (o p) n")
                                         ).then_inc(xin[gg % 2], 16)
                        if s in (14, 30):
                            n = 2 * m + s // 16
                            sp.wait_ge(res_out, n * 16 + (64 * it + 16))
                            src = x_rows(it).rearrange("(t p) (c n) -> c p t n", p=P, n=512)
                            sp.dma_start(res[:], src[ds(n, 1)].rearrange("o p t n -> (o p) t n")).then_inc(res_in, 16)
            for r in range(AHEAD):
                sp.wait_ge(w_lo, STEPS * U_STEP + r + 1)
                sp.dma_start(raw[:, r, :], wall[DEPTH - 1, 0]).then_inc(w_raw[r], 16)
            with sp.Fori(0, 4) as n:
                load_ln(STEPS - 1, n)
                store_ln(STEPS - 1, n)

        @block.tensor
        def _(pe):
            def mm(o, lhsT, rhs, start, stop):
                return nc.tensor.matmul(o, lhsT, rhs, start=start, stop=stop)

            pe.sem_inc(w_used, RING)

            def project(it, r, q, bank, slot):
                pe.wait_ge(w_lo, unit(it, r) + (1 + RING))
                for kk in range(4):
                    k = 4 * q + kk
                    hi, lo = (w[:, slot, kk * P:(kk + 1) * P] for w in (wh, wl))
                    mm(bank, hi, xh[:, k, :], k == 0, False)
                    mm(bank, hi, xl[:, k, :], False, False)
                    last = mm(bank, lo, xh[:, k, :], False, k == KT - 1)
                last.then_inc(w_used, 1)

            def transpose_x(g, bank):
                for b in range(4):
                    last = nc.tensor.transpose(bank[:, b * P:(b + 1) * P], prob[:, g % 2, b * P:(b + 1) * P], ident[:])
                last.then_inc(tr_full, 1)

            def transpose_values(bank):
                for b in range(QT):
                    last = nc.tensor.transpose(bank[:, b * P:(b + 1) * P], tmp[:, b * P:(b + 1) * P], ident[:])
                last.then_inc(vn_full, 1)

            def c_scores(it, p, j):
                c0 = 0 if half(it) else 512 - P * j
                for h in range(2):
                    pe.wait_ge(ct_lo, p * 8 + (8 * C_PAIRS * it + 2 * j + h + 1))
                    rows = slice(HD * h, HD * (h + 1))
                    qs = slice(P * j, P * (j + 1))
                    for a, b in ((c0, 512), (512, C_KEYS)):
                        if a >= b:
                            continue
                        ks = slice(P * j + a, P * j + b)
                        mm(sc[h][:, a:b], cq_h[rows, qs], ck_h[rows, ks], True, False)
                        mm(sc[h][:, a:b], cq_h[rows, qs], ck_l[rows, ks], False, False)
                        last = mm(sc[h][:, a:b], cq_l[rows, qs], ck_h[rows, ks], False, True)
                    last.then_inc(cs_full, 1)

            def c_transpose(it, p, j):
                c0 = 0 if half(it) else 512 - P * j
                for h in range(2):
                    pe.wait_ge(cs_prob, p * 8 + (8 * C_PAIRS * it + 2 * j + h + 1))
                    for b in range(c0 // P, 5):
                        cs = slice(b * P, (b + 1) * P)
                        last = nc.tensor.transpose(sc[h][:, cs], prob[:, h, cs], ident[:])
                    last.then_inc(ct_full, 1)

            def attend(region, values, blocks):
                n = 3 * len(blocks)
                i = 0
                for vb, pb in blocks:
                    for v, pt in ((values[0], pth), (values[0], ptl), (values[1], pth)):
                        last = mm(region, v[:, vb, :], pt[:, pb, :, :].rearrange("p h q -> p (h q)"), i == 0, i == n - 1)
                        i += 1
                return last

            def c_attend(it, p, j):
                if j == 0:
                    pe.wait_ge(prod_ok, p * 2 + (MIXES * it + 2))
                pe.wait_ge(ct_lo, p * 8 + (8 * C_PAIRS * it + 2 * j + 2 + 2))
                v0 = 0 if half(it) else 4 - j
                attend(pv[:, 256 * j:256 * (j + 1)], (cv_h, cv_l), [(j + v, v) for v in range(v0, 5)]
                       ).then_inc(c_pv, 1)

            def b_scores(it, i):
                pe.wait_ge(bq_ok, i + ((B_TILES + 1) * it + 2))
                pe.wait_ge(bt_lo, i * 4 + (4 * B_TILES * it + 4))
                for jj in range(2):
                    for h in range(2):
                        rows = slice(HD * h, HD * (h + 1))
                        for t in range(2):
                            j = 2 * jj + t
                            c0 = HD if half(it) == 0 and j == 0 else 0
                            o = sc[h][:, 512 * jj + 192 * t + c0:512 * jj + 192 * (t + 1)]
                            qs, ks = slice(P * j, P * (j + 1)), slice(P * j + HD + c0, P * j + 2 * P)
                            mm(o, bqh[rows, qs], bkh[rows, ks], True, False)
                            mm(o, bqh[rows, qs], bkl[rows, ks], False, False)
                            last = mm(o, bql[rows, qs], bkh[rows, ks], False, True)
                        last.then_inc(bs_full, 1)

            def b_transpose(it, i, jj):
                for h in range(2):
                    pe.wait_ge(bs_prob, i * 4 + (4 * B_TILES * it + 2 * jj + h + 1))
                    for t in range(2):
                        for b in range(2):
                            if half(it) == 0 and jj == t == b == 0:
                                continue
                            c = 256 * t + P * b
                            last = nc.tensor.transpose(sc[h][:, 512 * jj + c:512 * jj + c + P], prob[:, h, c:c + P], ident[:])
                    last.then_inc(bt_full, 1)

            def b_attend(it, i, jj):
                if jj == 0:
                    pe.wait_ge(prod_ok, i + (MIXES * it + 2 * C_PAIRS + 2))
                pe.wait_ge(bt_lo, i * 4 + (4 * B_TILES * it + 2 * jj + 2 + 4))
                for t in range(2):
                    j = 2 * jj + t
                    bs = [1] if half(it) == 0 and j == 0 else [0, 1]
                    last = attend(pv[:, 256 * j:256 * (j + 1)], (bvh, bvl), [(j + b, 2 * t + b) for b in bs])
                last.then_inc(b_pv, 1)

            pe.wait_ge(ident_ok, 2)
            for g in range(16):
                pe.wait_ge(xin[g % 2], 16 * (g // 2 + 1))
                if g >= 4:
                    pe.wait_ge(xl_ok, g - 3)
                transpose_x(g, odd_banks[g % 4])

            for it in range(STEPS):
                pe.wait_ge(xl_ok, 16 * (it + 1))
                if it:
                    pe.wait_ge(out_free, 16 * it + 8)
                with pe.Fori(0, C_PAIRS) as p:
                    def quarter(s, bank):
                        project(it, p * U_C + s, s % 4, acc[bank][:, :], s % RING)

                    pe.wait_ge(prod_ok, p * 2 + (MIXES * it + 1))
                    for s in range(0, 4):
                        quarter(s, 0)
                    pe.wait_ge(gate_ok, p * 2 + (MIXES * it + 1))
                    for s in range(4, 8):
                        quarter(s, 1)
                    pe.wait_ge(av_ok, p + (C_PAIRS * it + 1))
                    for s in range(8, 10):
                        quarter(s, 0)
                    pe.wait_ge(vt_ok, p + ((C_PAIRS + 1) * it + 1))
                    transpose_values(acc[1])
                    for s in range(10, 12):
                        quarter(s, 0)
                    pe.wait_ge(v_ok, p + ((C_PAIRS + 1) * it + 1))
                    for s in range(12, 16):
                        quarter(s, 1)
                    pe.wait_ge(k_ok, p + (C_PAIRS * it + 1))
                    quarter(16, 0)
                    pe.wait_ge(q_ok, p + (C_PAIRS * it + 1))
                    if half(it):
                        pe.wait_ge(hist_in, p * 32 + (32 * C_PAIRS * layer(it) + 32))
                    c_scores(it, p, 0)
                    quarter(17, 0)
                    c_transpose(it, p, 0)
                    quarter(18, 0)
                    c_scores(it, p, 1)
                    c_attend(it, p, 0)
                    quarter(19, 0)
                    c_transpose(it, p, 1)
                    quarter(20, 1)
                    c_scores(it, p, 2)
                    c_attend(it, p, 1)
                    quarter(21, 1)
                    c_transpose(it, p, 2)
                    pe.wait_ge(gate_ok, p * 2 + (MIXES * it + 2))
                    pe.wait_ge(ayl_ok, p + (C_PAIRS * it + 1))
                    pe.wait_ge(gwl_ok, p + (C_PAIRS * it + 2))
                    mm(acc[0][:, :], gwh[:], ya_h, True, False)
                    mm(acc[0][:, :], gwh[:], ya_l, False, False)
                    mm(acc[0][:, :], gwl[:], ya_h, False, True).then_inc(a_full, 1)
                    quarter(22, 1)
                    c_scores(it, p, 3)
                    c_attend(it, p, 2)
                    quarter(23, 1)
                    c_transpose(it, p, 3)
                    c_attend(it, p, 3)

                pe.wait_ge(prod_ok, MIXES * it + 2 * C_PAIRS - 1 + 2)
                for s in range(4):
                    project(it, KV0 + s, s, acc[0][:, :], s % RING)
                pe.wait_ge(gate_ok, MIXES * it + 2 * C_PAIRS + 1)
                for s in range(4):
                    project(it, KV0 + 4 + s, s, acc[1][:, :], s % RING)
                pe.wait_ge(rope_raw, ROTS * it + 1)
                for s in range(4):
                    project(it, B0 + s, s, acc[0][:, :], s % RING)
                    if s == 1:
                        pe.wait_ge(vt_ok, (C_PAIRS + 1) * (it + 1))
                        transpose_values(acc[1])
                pe.wait_ge(v_ok, (C_PAIRS + 1) * (it + 1))
                for s in range(4):
                    project(it, B0 + 4 + s, s, acc[1][:, :], s % RING)
                with pe.Fori(1, B_TILES) as i:
                    def quarter(s):
                        project(it, i * U_B + (B0 + s), s % 4, acc[s // 4][:, :], s % RING)
                    pe.wait_ge(rope_raw, i + (ROTS * it + 1))
                    quarter(0)
                    b_scores(it, i - 1)
                    quarter(1)
                    quarter(2)
                    b_transpose(it, i - 1, 0)
                    quarter(3)
                    b_attend(it, i - 1, 0)
                    pe.wait_ge(gate_ok, i + (MIXES * it + 2 * C_PAIRS + 1))
                    quarter(4)
                    b_transpose(it, i - 1, 1)
                    quarter(5)
                    b_attend(it, i - 1, 1)
                    quarter(6)
                    quarter(7)
                b_scores(it, B_TILES - 1)
                for jj in range(2):
                    b_transpose(it, B_TILES - 1, jj)
                    b_attend(it, B_TILES - 1, jj)

                pe.wait_ge(rope_raw, ROTS * (it + 1))
                pe.wait_ge(gate_ok, MIXES * (it + 1) + 1)
                pe.wait_ge(bt_lo, 4 * B_TILES * (it + 1) + 4)
                pe.wait_ge(mixl_ok, 16 * it + 16)
                with pe.Fori(0, 2) as m:
                    for n in range(2):
                        banks = (even_banks, odd_banks)[n]
                        if n and it + 1 < STEPS:
                            pe.wait_ge(xl_ok, m * 8 + (16 * (it + 1) + 8))
                        if n:
                            pe.wait_ge(prod_ok, MIXES * (it + 1) + 2)
                        for k in range(KT):
                            u = n * U_N + k
                            pe.wait_ge(w_lo, unit(it, m * (2 * U_N) + (O0 + u)) + (1 + RING))
                            if k == KT - 1:
                                pe.wait_ge(mixl_ok, 16 * (it + 1) + 1)
                            for t in range(QT):
                                if k == 0:
                                    pe.wait_ge(out_free, m * 8 + (16 * it + 4 * n + t + 1))
                                ts = slice(t * P, (t + 1) * P)
                                kt = MIX_ORDER[k]
                                w_h, w_l = wh[:, u % RING, :], wl[:, u % RING, :]
                                mm(banks[t], mixh[:, kt, ts], w_h, k == 0, False)
                                mm(banks[t], mixh[:, kt, ts], w_l, False, False)
                                last = mm(banks[t], mixl[:, kt, ts], w_h, False, k == KT - 1)
                                if k == KT - 1 and t < QT - 1:
                                    last.then_inc(out_full, 1)
                            last.then_inc(w_used, 1)
                            if n == 0 and k % 2 == 1 and it + 1 < STEPS:
                                gg = k // 2
                                pe.wait_ge(prod_ok, MIXES * (it + 1) + 2)
                                if gg >= 4:
                                    pe.wait_ge(xl_ok, m * 8 + (16 * (it + 1) + gg - 3))
                                else:
                                    pe.wait_ge(out_free, m * 8 + (16 * it + gg + 5))
                                pe.wait_ge(xin[gg % 2], m * 64 + (128 * (it + 1) + 16 * (gg // 2 + 1)))
                                transpose_x(gg, odd_banks[gg % 4])

        @block.scalar
        def _(act):
            def copy(o, i, scale=1.0):
                return nc.scalar.activation(o, i, ACT.Copy, scale=scale)

            def split(it, r, slot):
                u = unit(it, r) + AHEAD
                slot = (slot + AHEAD) % RING
                split_at(u, slot)

            def split_at(u, slot):
                act.wait_ge(w_raw[slot], (u - slot) * (16 // RING) + 16)
                act.wait_ge(w_used, u + 1)
                copy(wh[:, slot, :], raw[:, slot, :]).then_inc(w_hi, 1)

            def used(it, r):
                act.wait_ge(w_used, unit(it, r) + (1 + RING))

            def mix_hi(count, tile):
                act.wait_ge(prod_ok, count + 2)
                copy(mixh[:, ds(tile, 1), :].rearrange("p o n -> p (o n)"), tmp[:]).then_inc(mixh_ok, 1)

            def tanh_gate(bank):
                nc.scalar.activation(tmp[:], acc[bank][:, :], ACT.Tanh, scale=0.5).then_inc(tanh_ok, 1)

            def x_hi(idx, gg, bank, t):
                act.wait_ge(tr_full, idx + 1)
                copy(xh[:, 4 * (gg % 4):4 * (gg % 4) + 4, ds(t * P, P)],
                     bank.rearrange("p (k q) -> p k q", k=4)).then_inc(xh_ok, 1)

            for u in range(AHEAD):
                split_at(u, u)
            for g in range(16):
                x_hi(g, g, odd_banks[g % 4], g // 4)

            def c_exp(it, p, j):
                c0 = 0 if half(it) else 512 - P * j
                for h in range(2):
                    act.wait_ge(cs_max, p * 8 + (8 * C_PAIRS * it + 2 * j + h + 1))
                    nc.scalar.activation(prob[:, h, c0:C_KEYS], sc[h][:, c0:C_KEYS], ACT.Exp,
                                         bias=nmax[:, h, 0:1], accum_out=psums[:, h, 0:1]).then_inc(cs_exp, 1)

            def c_hi(it, p, j):
                b0 = 0 if half(it) else 4 - j
                for h in range(2):
                    act.wait_ge(ct_full, p * 8 + (8 * C_PAIRS * it + 2 * j + h + 1))
                    copy(pth[:, b0:5, h, :], sc[h][:, b0 * P:5 * P].rearrange("p (b q) -> p b q", q=P)).then_inc(ct_hi, 1)

            def b_exp(it, i, u):
                jj, h = u // 2, u % 2
                act.wait_ge(bs_max, i * 4 + (4 * B_TILES * it + u + 1))
                if jj:
                    act.wait_ge(bt_full, i * 4 + (4 * B_TILES * it + h + 1))
                for t in range(2):
                    nc.scalar.activation(prob[:, h, 256 * t + HD:256 * (t + 1)], sc[h][:, 512 * jj + 192 * t:512 * jj + 192 * (t + 1)],
                                         ACT.Exp, bias=nmax[:, u, t:t + 1], accum_out=psums[:, u, t:t + 1])
                nc.scalar.activation(esink[:, u, :], nmax[:, u, :], ACT.Exp, bias=sink1[:, 0, h:h + 1]).then_inc(bs_exp, 1)

            def b_hi(it, i, u):
                jj, h = u // 2, u % 2
                b0 = 1 if half(it) == 0 and jj == 0 else 0
                act.wait_ge(bt_full, i * 4 + (4 * B_TILES * it + u + 1))
                copy(pth[:, b0:4, h, :], sc[h][:, 512 * jj + b0 * P:512 * (jj + 1)].rearrange("p (b q) -> p b q", q=P)
                     ).then_inc(bt_hi, 1)

            def rope_copy(it, n, scale):
                if isinstance(n, int) and n == 0:
                    act.wait_ge(ayl_ok, C_PAIRS * (it + 1))
                else:
                    act.wait_ge(bq_ok, n + ROTS * it)
                copy(s0[:, 0:HALF], acc[0][:, :], scale).then_inc(rope_raw, 1)

            for it in range(STEPS):
                nb = 16 * it
                with act.Fori(0, C_PAIRS) as p:
                    def slot(s):
                        split(it, p * U_C + s, s % RING)
                    pc = C_PAIRS * it

                    for s in range(5):
                        slot(s)
                    used(it, p * U_C + 3)
                    copy(av[:, 16:16 + HALF], acc[0][:, :]).then_inc(av_ok, 1)
                    slot(5)
                    slot(6)
                    act.wait_ge(gw_in, p * 16 + (16 * pc + 16))
                    copy(gwh[:], gw[:]).then_inc(gwh_ok, 1)
                    slot(7)
                    act.wait_ge(mixl_ok, p * 2 + (nb + 1))
                    used(it, p * U_C + 7)
                    copy(tmp[:], acc[1][:, :]).then_inc(vt_ok, 1)
                    slot(8)
                    slot(9)
                    act.wait_ge(ay_ok, p + (pc + 1))
                    copy(ya_h, s0[:, 16:16 + HALF]).then_inc(ayh_ok, 1)
                    act.wait_ge(vn_full, p + ((C_PAIRS + 1) * it + 1))
                    copy(cv_h[:, 4:8, :], acc[1][:, :].rearrange("p (b c) -> p b c", c=P)).then_inc(vh_ok, 1)
                    slot(10)
                    slot(11)
                    used(it, p * U_C + 11)
                    copy(ck_h[:, HALF:2 * HALF], acc[0][:, :]).then_inc(kh_ok, 1)
                    slot(12)
                    slot(13)
                    slot(14)
                    slot(15)
                    used(it, p * U_C + 15)
                    copy(cq_h, acc[1][:, :], SCALE).then_inc(qh_ok, 1)
                    slot(16)
                    slot(17)
                    c_exp(it, p, 0)
                    slot(18)
                    c_hi(it, p, 0)
                    slot(19)
                    c_exp(it, p, 1)
                    slot(20)
                    c_hi(it, p, 1)
                    used(it, p * U_C + 19)
                    tanh_gate(0)
                    slot(21)
                    c_exp(it, p, 2)
                    slot(22)
                    c_hi(it, p, 2)
                    mix_hi(p * 2 + (nb + 1), p + MIX_A)
                    slot(23)
                    c_exp(it, p, 3)
                    c_hi(it, p, 3)
                    used(it, p * U_C + 23)
                    act.wait_ge(mixl_ok, p * 2 + (nb + 1 + 1))
                    tanh_gate(1)
                    mix_hi(p * 2 + (nb + 2), p + MIX_C)
                    if not half(it):
                        act.wait_ge(hist_out, p * 32 + (32 * C_PAIRS * layer(it) + 32))

                for s in range(4):
                    split(it, KV0 + s, s % RING)
                split(it, KV0 + 4, 0)
                used(it, KV0 + 3)
                rope_copy(it, 0, 1.0)
                split(it, KV0 + 5, 1)
                if half(it):
                    act.wait_ge(hist_mv, layer(it) + 1)
                act.wait_ge(rope_ok, (B_TILES + 1) * it + 1)
                copy(bkh[:, P:], s0[:, 0:HALF]).then_inc(qh_ok, 1)
                split(it, KV0 + 6, 2)
                split(it, KV0 + 7, 3)
                split(it, B0, 0)
                act.wait_ge(mixl_ok, nb + 2 * C_PAIRS + 1)
                used(it, KV0 + 7)
                copy(tmp[:], acc[1][:, :]).then_inc(vt_ok, 1)
                split(it, B0 + 1, 1)
                split(it, B0 + 2, 2)
                act.wait_ge(vn_full, (C_PAIRS + 1) * (it + 1))
                copy(bvh[:, 1:, :], acc[1][:, :].rearrange("p (b c) -> p b c", c=P)).then_inc(vh_ok, 1)
                split(it, B0 + 3, 3)
                split(it, B0 + 4, 0)
                used(it, B0 + 3)
                rope_copy(it, 1, SCALE)
                split(it, B0 + 5, 1)
                split(it, B0 + 6, 2)
                act.wait_ge(rope_ok, (B_TILES + 1) * it + 2)
                copy(bqh[:], s0[:, 0:HALF]).then_inc(qh_ok, 1)
                split(it, B0 + 7, 3)
                used(it, B0 + 7)
                tanh_gate(1)
                with act.Fori(1, B_TILES) as i:
                    def slot(s):
                        split(it, i * U_B + (B0 + s), s % RING)
                    slot(0)
                    b_exp(it, i - 1, 0)
                    b_exp(it, i - 1, 1)
                    slot(1)
                    slot(2)
                    b_hi(it, i - 1, 0)
                    b_hi(it, i - 1, 1)
                    b_exp(it, i - 1, 2)
                    b_exp(it, i - 1, 3)
                    slot(3)
                    slot(4)
                    used(it, i * U_B + (B0 + 3))
                    rope_copy(it, i + 1, SCALE)
                    b_hi(it, i - 1, 2)
                    b_hi(it, i - 1, 3)
                    slot(5)
                    act.wait_ge(rope_ok, i + ((B_TILES + 1) * it + 2))
                    copy(bqh[:], s0[:, 0:HALF]).then_inc(qh_ok, 1)
                    slot(6)
                    mix_hi(i + (nb + 2 * C_PAIRS), i + (MIX_B - 1))
                    slot(7)
                    used(it, i * U_B + (B0 + 7))
                    act.wait_ge(mixl_ok, i + (nb + 2 * C_PAIRS + 1))
                    tanh_gate(1)
                last = B_TILES - 1
                for jj in range(2):
                    b_exp(it, last, 2 * jj)
                    b_exp(it, last, 2 * jj + 1)
                    b_hi(it, last, 2 * jj)
                    b_hi(it, last, 2 * jj + 1)
                mix_hi(nb + 16, MIX_B + last)

                with act.Fori(0, 2) as m:
                    for s in range(2 * U_N):
                        split(it, m * (2 * U_N) + (O0 + s), s % RING)
                        if s < U_N and s % 2 == 1 and it + 1 < STEPS:
                            gg = s // 2
                            x_hi(m * 8 + (16 * (it + 1) + gg), gg, odd_banks[gg % 4], 2 * m + gg // 4)
                        if s % U_N == U_N - 1:
                            n = 2 * m + s // U_N
                            act.wait_ge(res_ok, n * 4 + (16 * it + 4))
                            act.dma_start(res_d[ds(n, 1)].rearrange("o p t n -> (o p) t n"), res[:]).then_inc(res_out, 16)
                act.wait_ge(ln_var, it + 1)
                nc.scalar.activation(sq[:], veps[:], ACT.Sqrt).then_inc(ln_sqrt, 1)

        @block.gpsimd
        def _(pool):
            pool.sem_inc(w_lo, RING)
            nc.gpsimd.memset(ident[:], 0.0).then_inc(ident_ok, 1)
            pool.wait_ge(ident_ok, 1)
            nc.gpsimd.affine_select(out=ident[:], in_=ident[:], compare_op=ALU.not_equal, fill=1.0, base=0,
                                    pattern=[[-1, P]], channel_multiplier=1).then_inc(ident_ok, 1)
            with pool.Fori(0, STEPS * U_STEP, RING) as u:
                for s in range(RING):
                    pool.wait_ge(w_hi, u + (s + 1))
                    pool.wait_ge(w_used, u + (s + 1))
                    nc.gpsimd.tensor_tensor(wl[:, s, :], raw[:, s, :], wh[:, s, :].bitcast(F32), ALU.subtract
                                            ).then_inc(w_lo, 1)

        @block.vector
        def _(dv):
            V = nc.vector
            count = [0, 0]

            def section(value):
                count[0], count[1] = value, 0

            def V_(ins):
                count[1] += 1
                ins.then_inc(dve, 1)
                dv.wait_ge(dve, count[0] + count[1])

            dv.sem_inc(gwl_ok, 1)
            dv.sem_inc(bias_ok, 1)
            dv.sem_inc(ct_lo, 2)
            dv.sem_inc(bt_lo, 4)
            dv.sem_inc(prod_ok, 2)
            dv.sem_inc(mixl_ok, 1)
            dv.sem_inc(out_free, 8)
            dv.sem_inc(gate_ok, 1)

            def lo(o, whole, hi):
                return V.tensor_tensor(o, whole, hi.bitcast(F32), ALU.subtract)

            def x_lo(idx, gg, bank, t):
                dv.wait_ge(xh_ok, idx + 1)
                piece = (slice(None), slice(4 * (gg % 4), 4 * (gg % 4) + 4), ds(t * P, P))
                lo(xl[piece], bank.rearrange("p (k q) -> p k q", k=4), xh[piece]).then_inc(xl_ok, 1)

            def gate_ready(n, bank):
                dv.wait_ge(tanh_ok, n)
                V.scalar_tensor_tensor(gate[:], tmp[:], 1.0, acc[bank][:, :], ALU.add, ALU.mult).then_inc(gate_ok, 1)

            def mix_lo(n, tile):
                dv.wait_ge(mixh_ok, n)
                t = mixh[:, ds(tile, 1), :].rearrange("p o n -> p (o n)")
                lo(mixl[:, ds(tile, 1), :].rearrange("p o n -> p (o n)"), tmp[:], t).then_inc(mixl_ok, 1)

            def attention_product(gates):
                dv.wait_ge(gate_ok, gates + 1)
                for h in range(2):
                    rows = slice(HD * h, HD * (h + 1))
                    last = V.scalar_tensor_tensor(tmp[rows, :].rearrange("p (j q) -> p j q", q=P), pv4[rows, :, h, :], 0.5,
                                                  gate[rows, :].rearrange("p (j q) -> p j q", q=P), ALU.mult, ALU.mult)
                last.then_inc(prod_ok, 1)

            def c_max(it, p, j):
                c0 = 0 if half(it) else 512 - P * j
                for h in range(2):
                    s = sc[h]
                    dv.wait_ge(cs_full, p * 8 + (8 * C_PAIRS * it + 2 * j + h + 1))
                    if half(it):
                        V.memset(s[HD:P, 0:CHUNK], NEG_INF)
                    a = max(c0, C_KEYS - NEAR)
                    V_(V.tensor_tensor(s[:, a:C_KEYS], s[:, a:C_KEYS],
                                       brope[:, 1, NEAR * h + a - (C_KEYS - NEAR):NEAR * (h + 1)], ALU.add))
                    V.tensor_reduce(nmax[:, h, 0:1], s[:, c0:C_KEYS], AX, ALU.max, negate=True).then_inc(cs_max, 1)

            def c_normalise(it, p, j):
                c0 = 0 if half(it) else 512 - P * j
                for h in range(2):
                    dv.wait_ge(cs_exp, p * 8 + (8 * C_PAIRS * it + 2 * j + h + 1))
                    V_(V.reciprocal(rinv[:, h, 0:1], psums[:, h, 0:1]))
                    V.tensor_scalar(prob[:, h, c0:C_KEYS], prob[:, h, c0:C_KEYS], rinv[:, h, 0:1], None, ALU.mult
                                    ).then_inc(cs_prob, 1)

            def c_lo(it, p, j):
                b0 = 0 if half(it) else 4 - j
                for h in range(2):
                    dv.wait_ge(ct_hi, p * 8 + (8 * C_PAIRS * it + 2 * j + h + 1))
                    lo(ptl[:, b0:5, h, :], sc[h][:, b0 * P:5 * P].rearrange("p (b q) -> p b q", q=P), pth[:, b0:5, h, :]
                       ).then_inc(ct_lo, 1)

            def b_max(it, i, u):
                jj, h = u // 2, u % 2
                dv.wait_ge(bs_full, i * 4 + (4 * B_TILES * it + u + 1))
                s = sc[h][:, 512 * jj:512 * jj + 384].rearrange("p (t c) -> p t c", t=2)
                if half(it) == 0 and jj == 0:
                    V.memset(s[:, 0, 0:CHUNK], NEG_INF)
                    V.memset(s[HD:P, 1, 0:CHUNK], NEG_INF)
                else:
                    V.memset(s[HD:P, :, 0:CHUNK], NEG_INF)
                V_(V.memset(s[0:HD, :, 2 * CHUNK:3 * CHUNK], NEG_INF))
                V_(V.tensor_reduce(mx[:, u, :], s, AX, ALU.max, negate=True))
                V.tensor_scalar(nmax[:, u, :], mx[:, u, :], sink1[:, 1, h:h + 1], None, ALU.min).then_inc(bs_max, 1)

            def b_normalise(it, i, u):
                h = u % 2
                dv.wait_ge(bs_exp, i * 4 + (4 * B_TILES * it + u + 1))
                V_(V.tensor_tensor(mx[:, u, :], psums[:, u, :], esink[:, u, :], ALU.add))
                V_(V.reciprocal(rinv[:, u, :], mx[:, u, :]))
                for t in range(2):
                    cs = slice(256 * t + HD, 256 * (t + 1))
                    last = V.tensor_scalar(prob[:, h, cs], prob[:, h, cs], rinv[:, u, t:t + 1], None, ALU.mult)
                last.then_inc(bs_prob, 1)

            def b_lo(it, i, u):
                jj, h = u // 2, u % 2
                b0 = 1 if half(it) == 0 and jj == 0 else 0
                dv.wait_ge(bt_hi, i * 4 + (4 * B_TILES * it + u + 1))
                lo(ptl[:, b0:4, h, :], sc[h][:, 512 * jj + b0 * P:512 * (jj + 1)].rearrange("p (b q) -> p b q", q=P),
                   pth[:, b0:4, h, :]).then_inc(bt_lo, 1)

            def sinks_of(it, i):
                V_(V.tensor_copy(sink1[:, 0, :], sink_s[:, layer(it), ds(i, 1), :].rearrange("p o h -> p (o h)")))
                V_(V.tensor_scalar(sink1[:, 1, :], sink1[:, 0, :], -1.0, None, ALU.mult))

            def rotate(n):
                dv.wait_ge(rope_raw, n)
                x_, y_ = s0[:, 0:HALF], s1[:, 0:HALF]
                V.tensor_tensor(y_, x_, brope[:, 0, :], ALU.mult)
                V_(V.stream_shuffle(x_, x_, SWAP))
                V_(V.tensor_tensor(x_, x_, brope[:, 1, :], ALU.mult))
                V.tensor_tensor(x_, x_, y_, ALU.add).then_inc(rope_ok, 1)

            def rotated(o, hi, n):
                dv.wait_ge(qh_ok, n)
                lo(o, s0[:, 0:HALF], hi).then_inc(bq_ok, 1)

            def layer_norm(it, n):
                dv.wait_ge(ln_in, n * 48 + (192 * it + 48))
                for t in range(QT):
                    last = V.tensor_scalar(res[:, t, :], res[:, t, :], mv[:, t, 0:1], rstd[:, t:t + 1],
                                           ALU.subtract, ALU.mult)
                V_(last)
                for slot, op in ((0, ALU.mult), (1, ALU.add)):
                    v = prob[:, slot, 0:512].rearrange("p (o n) -> p o n", o=1).to_broadcast([P, QT, 512])
                    last = V.tensor_tensor(res[:], res[:], v, op)
                    if slot == 0:
                        V_(last)
                last.then_inc(ln_ok, 1)

            dv.wait_ge(tzr_in, 16)
            section(0)
            V.tensor_copy(tmp[0:DEPTH * 8, 0:127], tmp[0:DEPTH * 8, 127:128].to_broadcast([DEPTH * 8, 127])).then_inc(tzr_ok, 1)
            dv.wait_ge(const_in, 64)
            V_(V.tensor_scalar(scale_s[:], scale_s[:], 0.5, None, ALU.mult))
            for g in range(16):
                x_lo(g, g, odd_banks[g % 4], g // 4)
            dv.wait_ge(tz_out, 16)
            total = count[1]

            for it in range(STEPS):
                pc, nb = C_PAIRS * it, 16 * it
                per_c = 23 + (2 if it else 0) - half(it)
                with dv.Fori(0, C_PAIRS) as p:
                    section(p * per_c + total)
                    V.tensor_copy(coef1[:], coef[:, ds(p, 1), :].rearrange("p o n -> p (o n)"))
                    V.tensor_copy(inv1[:], inv16[:, ds(p, 1), :].rearrange("p o n -> p (o n)"))
                    V.tensor_copy(scale1[:], scale_s[:, layer(it), ds(p, 1)])
                    if half(it):
                        V_(V.tensor_copy(av[:, 0:16], a_tail[:, ds(p, 1), :].rearrange("p o n -> p (o n)")))
                    else:
                        V_(V.memset(av[:, 0:16], 0.0))
                    dv.wait_ge(av_ok, p + (pc + 1))
                    N = 16 + HALF
                    V_(V.tensor_tensor(s0[:, 1:N], av[:, 1:N], av[:, 0:N - 1], ALU.add))
                    V_(V.scalar_tensor_tensor(s1[:, 3:N], s0[:, 1:N - 2], coef1[:, 0:1], s0[:, 3:N], ALU.mult, ALU.add))
                    V_(V.scalar_tensor_tensor(s0[:, 7:N], s1[:, 3:N - 4], coef1[:, 1:2], s1[:, 7:N], ALU.mult, ALU.add))
                    V_(V.scalar_tensor_tensor(s1[:, 15:N], s0[:, 7:N - 8], coef1[:, 2:3], s0[:, 15:N], ALU.mult, ALU.add))
                    if half(it):
                        V.scalar_tensor_tensor(s0[:, 16:N], s1[:, 16:N], coef1[:, 3:4], av[:, 16:N], ALU.mult, ALU.subtract
                                               ).then_inc(ay_ok, 1)
                    else:
                        V.tensor_copy(a_tail[:, ds(p, 1), :].rearrange("p o n -> p (o n)"), av[:, HALF:N])
                        V_(V.tensor_tensor(s1[:, 16:32], s1[:, 16:32], inv1[:], ALU.mult))
                        V.tensor_tensor(s0[:, 16:32], s1[:, 16:32], av[:, 16:32], ALU.subtract)
                        V.scalar_tensor_tensor(s0[:, 32:N], s1[:, 32:N], coef1[:, 3:4], av[:, 32:N], ALU.mult, ALU.subtract
                                               ).then_inc(ay_ok, 1)
                    dv.wait_ge(gwh_ok, p + (pc + 1))
                    lo(gwl[:], gw[:], gwh[:]).then_inc(gwl_ok, 1)
                    dv.wait_ge(ayh_ok, p + (pc + 1))
                    lo(ya_l, s0[:, 16:N], ya_h).then_inc(ayl_ok, 1)
                    dv.wait_ge(vh_ok, p + ((C_PAIRS + 1) * it + 1))
                    lo(cv_l[:, 4:8, :], acc[1][:, :].rearrange("p (b c) -> p b c", c=P), cv_h[:, 4:8, :])\
                        .then_inc(v_ok, 1)
                    dv.wait_ge(bias_in, p * 16 + (16 * pc + 16))
                    for h in range(2):
                        cs = slice(NEAR * h, NEAR * (h + 1))
                        last = V.tensor_scalar(brope[:, 1, cs], brope[:, 0, cs], brope[:, 0, NEAR * h:NEAR * h + 1], None, ALU.subtract)
                    V_(last)
                    for h in range(2):
                        last = V.memset(brope[0:HD, 1, NEAR * (h + 1) - CHUNK:NEAR * (h + 1)], NEG_INF)
                    last.then_inc(bias_ok, 1)
                    dv.wait_ge(kh_ok, p + (pc + 1))
                    lo(ck_l[:, HALF:2 * HALF], acc[0][:, :], ck_h[:, HALF:2 * HALF]).then_inc(k_ok, 1)
                    if it:
                        layer_norm(it - 1, p)
                    dv.wait_ge(qh_ok, p + ((C_PAIRS + B_TILES + 1) * it + 1))
                    V.scalar_tensor_tensor(cq_l, acc[1][:, :], SCALE, cq_h.bitcast(F32), ALU.mult, ALU.subtract).then_inc(q_ok, 1)
                    dv.wait_ge(bias_ok, p + (pc + 2))
                    c_max(it, p, 0)
                    c_normalise(it, p, 0)
                    c_lo(it, p, 0)
                    c_max(it, p, 1)
                    c_normalise(it, p, 1)
                    c_lo(it, p, 1)
                    gate_ready(p * 2 + ((2 * C_PAIRS + B_TILES) * it + 1), 0)
                    c_max(it, p, 2)
                    c_normalise(it, p, 2)
                    c_lo(it, p, 2)
                    dv.wait_ge(a_full, p + (pc + 1))
                    V.scalar_tensor_tensor(tmp[:], acc[0][:, :], scale1[:], gate[:], ALU.mult, ALU.mult).then_inc(prod_ok, 1)
                    mix_lo(p * 2 + (nb + 1), p + MIX_A)
                    c_max(it, p, 3)
                    c_normalise(it, p, 3)
                    c_lo(it, p, 3)
                    gate_ready(p * 2 + ((2 * C_PAIRS + B_TILES) * it + 2), 1)
                    dv.wait_ge(c_pv, p * 4 + (4 * pc + 4))
                    attention_product(p * 2 + (MIXES * it + 2))
                    mix_lo(p * 2 + (nb + 2), p + MIX_C)
                    if not half(it):
                        dv.wait_ge(hist_out, p * 32 + (32 * C_PAIRS * layer(it) + 32))
                    assert count[1] == per_c, (it, count[1])
                total += C_PAIRS * per_c

                section(total)
                dv.wait_ge(rope_raw, ROTS * it + 1)
                if half(it):
                    for t in (bkh, bkl):
                        V.tensor_copy(t[:, 0:P], t[:, HALF:HALF + P])
                    V.tensor_copy(bvh[:, 0, :], bvh[:, QT, :])
                    V.tensor_copy(bvl[:, 0, :], bvl[:, QT, :]).then_inc(hist_mv, 1)
                V.memset(prob[:, :, 0:512].rearrange("p s (t c) -> p s t c", t=2)[:, :, :, 0:HD], 0.0)
                dv.wait_ge(rope_in, 32 * (it + 1))
                rotate(ROTS * it + 1)
                if half(it):
                    dv.wait_ge(hist_mv, layer(it) + 1)
                rotated(bkl[:, P:], bkh[:, P:], QS * it + C_PAIRS + 1)
                dv.wait_ge(vh_ok, (C_PAIRS + 1) * (it + 1))
                lo(bvl[:, 1:, :], acc[1][:, :].rearrange("p (b c) -> p b c", c=P), bvh[:, 1:, :]).then_inc(v_ok, 1)
                rotate(ROTS * it + 2)
                rotated(bql[:], bqh[:], QS * it + C_PAIRS + 2)
                gate_ready(MIXES * it + 2 * C_PAIRS + 1, 1)
                total += count[1]

                per_b = 2 + 2 * 4 + 2 * 4 + 2
                with dv.Fori(1, B_TILES) as i:
                    section((i - 1) * per_b + total)
                    sinks_of(it, i - 1)
                    for u in (0, 1):
                        b_max(it, i - 1, u)
                    for u in (0, 1):
                        b_normalise(it, i - 1, u)
                    for u in (2, 3):
                        b_max(it, i - 1, u)
                    for u in (0, 1):
                        b_lo(it, i - 1, u)
                    for u in (2, 3):
                        b_normalise(it, i - 1, u)
                    rotate(i + (ROTS * it + 2))
                    for u in (2, 3):
                        b_lo(it, i - 1, u)
                    rotated(bql[:], bqh[:], i + (QS * it + C_PAIRS + 2))
                    dv.wait_ge(b_pv, i * 2 + 2 * B_TILES * it)
                    attention_product(i + (MIXES * it + 2 * C_PAIRS))
                    mix_lo(i + (nb + 2 * C_PAIRS), i + (MIX_B - 1))
                    gate_ready(i + (MIXES * it + 2 * C_PAIRS + 1), 1)
                    assert count[1] == per_b, count[1]
                total += (B_TILES - 1) * per_b

                section(total)
                last_tile = B_TILES - 1
                sinks_of(it, last_tile)
                for jj in range(2):
                    for u in (2 * jj, 2 * jj + 1):
                        b_max(it, last_tile, u)
                    for u in (2 * jj, 2 * jj + 1):
                        b_normalise(it, last_tile, u)
                    for u in (2 * jj, 2 * jj + 1):
                        b_lo(it, last_tile, u)
                dv.wait_ge(b_pv, 2 * B_TILES * (it + 1))
                attention_product(MIXES * (it + 1))
                mix_lo(nb + 16, MIX_B + last_tile)
                total += count[1]

                with dv.Fori(0, 2) as m:
                    for n in range(2):
                        if n == 0 and it + 1 < STEPS:
                            for gg in range(8):
                                x_lo(m * 8 + (16 * (it + 1) + gg), gg, odd_banks[gg % 4], 2 * m + gg // 4)
                        c = 2 * m + n
                        dv.wait_ge(res_in, c * 16 + (64 * it + 16))
                        for t in range(QT):
                            if t < QT - 1:
                                dv.wait_ge(out_full, c * 3 + (12 * it + t + 1))
                            else:
                                dv.wait_ge(w_used, unit(it, c * U_N + (O0 + U_N)) + RING)
                            V.scalar_tensor_tensor(res[:, t, :], res[:, t, :], ALPHA, (even_banks, odd_banks)[n][t],
                                                   ALU.mult, ALU.add).then_inc(out_free, 1)
                        dv.wait_ge(out_free, c * 4 + (16 * it + 4 + 8))
                        for t in range(QT):
                            V.bn_stats(stats[:, t, ds(c, 1), :].rearrange("p o s -> p (o s)"), res[:, t, :]).then_inc(res_ok, 1)
                section(total)
                dv.wait_ge(res_ok, 16 * (it + 1))
                for t in range(QT):
                    last = V.bn_aggr(mv[:, t, :], stats[:, t, :, :].rearrange("p n s -> p (n s)"))
                V_(last)
                V.tensor_scalar(veps[:], mv[:, :, 1], LN_EPS, None, ALU.add).then_inc(ln_var, 1)
                dv.wait_ge(ln_sqrt, it + 1)
                V_(V.reciprocal(sq2[:], sq[:]))
                V_(V.tensor_tensor(sq2[:], sq2[:], veps[:], ALU.mult))
                V_(V.tensor_tensor(sq2[:], sq2[:], sq[:], ALU.add))
                V_(V.reciprocal(rstd[:], sq2[:]))
                V_(V.tensor_scalar(rstd[:], rstd[:], 2.0, None, ALU.mult))
                total += count[1]

            with dv.Fori(0, 4) as n:
                section(n * 2 + total)
                layer_norm(STEPS - 1, n)


def laid_out(x, w_in, a_group_w, a_scale, b_sinks, c_rel_bias, w_out, ln_gain, ln_bias):
    cols = np.split(np.arange(w_in.shape[2]),
                    np.cumsum([A_WIDTH, A_WIDTH, B_WIDTH, P, P, B_WIDTH, C_WIDTH, C_WIDTH, C_WIDTH])) 
    a_v, a_g, b_q, b_k, b_v, b_g, c_q, c_k, c_v, c_g = cols

    def tile(v, i):
        return v[i * P:(i + 1) * P]

    def heads(v, i):
        return np.concatenate([v[i * HD:(i + 1) * HD], v[(i + B_TILES) * HD:(i + B_TILES + 1) * HD]])

    order = []
    for p in range(C_PAIRS):
        order += [tile(v, p) for v in (a_v, c_v, c_k, c_q, a_g, c_g)]
    order += [b_k, b_v]
    for i in range(B_TILES):
        order += [heads(b_q, i), heads(b_g, i)]
    order = np.concatenate(order)
    w1 = w_in[:, :, order].reshape(DEPTH, 4, 4, P, len(order) // P, P)
    w1 = w1.transpose(0, 4, 1, 3, 2, 5).reshape(DEPTH, O0, P, UNIT)
    chan = np.arange(D)
    mix = [tile(chan, g) for g in range(A_GROUPS)] + [heads(A_WIDTH + np.arange(B_WIDTH), i) for i in range(B_TILES)] \
        + [tile(A_WIDTH + B_WIDTH + np.arange(C_WIDTH), p) for p in range(C_PAIRS)]
    w2 = w_out[:, np.concatenate([mix[k] for k in MIX_ORDER]), :].reshape(DEPTH, KT, P, 4, UNIT)
    w2 = w2.transpose(0, 3, 1, 2, 4).reshape(DEPTH, 4 * U_N, P, UNIT)
    wall = np.concatenate([w1, w2], axis=1)

    t = np.arange(SEQ, dtype=np.float32)
    j = np.arange(ROPE_DIM // 2, dtype=np.float32)
    inv = (np.float32(ROPE_THETA) ** (-j / np.float32(ROPE_DIM // 2))).astype(np.float32)
    ang = (inv[:, None] * t[None, :]).astype(np.float32)
    cos = np.ones((2, HD, SEQ), np.float32)
    sin = np.zeros((2, HD, SEQ), np.float32)
    cos[:, 0:8] = cos[:, 8:16] = np.cos(ang)
    sin[:, 0:8], sin[:, 8:16] = -np.sin(ang), np.sin(ang)
    by_half = [np.ascontiguousarray(a.reshape(P, 2, HALF).transpose(1, 0, 2)) for a in (cos, sin)]
    coef = np.array([[w >= 4, w >= 8, w >= 16, 1.0 / w] for w in WINDOWS], np.float32)
    first = np.array([1.0 / np.minimum(np.arange(16) + 1.0, w) for w in WINDOWS], np.float32)
    return {
        "x": x[0],
        "wall": wall,
        "a_gw": a_group_w,
        "a_scale": a_scale.reshape(DEPTH, A_GROUPS, P).transpose(2, 0, 1),
        "sinks": b_sinks.reshape(DEPTH, 2, B_TILES).transpose(0, 2, 1).reshape(1, -1),
        "rel_rev": c_rel_bias.reshape(DEPTH * 8, 2 * MAX_REL + 1)[:, ::-1],
        "ln_gain": ln_gain.reshape(DEPTH, 4, 512),
        "ln_bias": ln_bias.reshape(DEPTH, 4, 512),
        "rope_cos": by_half[0],
        "rope_sin": by_half[1],
        "pool_coef": np.broadcast_to(coef, (P,) + coef.shape),
        "pool_inv": np.broadcast_to(first, (P,) + first.shape),
    }


def kernel(x, w_in, a_group_w, a_scale, b_sinks, c_rel_bias, w_out, ln_gain, ln_bias):
    import concourse.bacc as bacc
    from concourse.bass_utils import run_bass_kernel_spmd

    given = laid_out(*(np.asarray(a) for a in (x, w_in, a_group_w, a_scale, b_sinks, c_rel_bias, w_out,
                                               ln_gain, ln_bias)))
    nc = bacc.Bacc("TRN2", target_bir_lowering=False, num_devices=1)
    arrays, args = {}, {}
    for name, a in given.items():
        a = np.ascontiguousarray(a)
        arrays[f"in_{name}"] = a
        args[name] = nc.dram_tensor(f"in_{name}", a.shape, mybir.dt.from_np(a.dtype), kind="ExternalInput").ap()
    out = nc.dram_tensor("out", (SEQ, D), F32, kind="ExternalOutput").ap()
    build(nc, out=out, **args)
    r = run_bass_kernel_spmd(nc, [arrays], core_ids=[0])
    return r.results[0]["out"].reshape(1, SEQ, D)
```

```python
from contextlib import ExitStack

import numpy as np

import concourse.bass as bass
from concourse import mybir

F32 = mybir.dt.float32
F32R = mybir.dt.float32r
ALU = mybir.AluOpType
ACT = mybir.ActivationFunctionType
AX = mybir.AxisListType.X
ds = bass.ds

P = 128
D = 2048
SEQ = 1024
DEPTH = 2
HALF = 512
STEPS = DEPTH * (SEQ // HALF)
KT = D // P
HD = 64
A_WIDTH = D // 4
A_GROUPS = 4
WINDOWS = (2, 4, 8, 16)
B_WIDTH = D // 2
B_HEADS = B_WIDTH // HD
B_TILES = B_HEADS // 2
C_WIDTH = D - A_WIDTH - B_WIDTH
C_PAIRS = C_WIDTH // P
CHUNK = 64
C_KEYS = 640
NEAR = 256
MAX_REL = 128
ROPE_DIM = HD // 4
ROPE_THETA = 500000.0
SCALE = float(HD) ** -0.5
ALPHA = (2.0 * DEPTH) ** 0.25
LN_EPS = 1e-5
NEG_INF = -1e30
QT = HALF // P

UNIT = 512
RING = 4
AHEAD = 3
U_C = 24
U_KV = 8
U_B = 8
U_N = 16
KV0 = C_PAIRS * U_C
B0 = KV0 + U_KV
O0 = B0 + B_TILES * U_B
U_STEP = O0 + 4 * U_N

MIX_A, MIX_B, MIX_C = 0, A_GROUPS, A_GROUPS + B_TILES
MIX_ORDER = list(range(MIX_B)) + list(range(MIX_C, KT)) + list(range(MIX_B, MIX_C))

MIXES = 2 * C_PAIRS + B_TILES
ROTS = 1 + B_TILES
QS = C_PAIRS + ROTS
TZ = 384

X_AT = (1, 3, 5, 7, 9, 11, 13, 14)
X_LOAD = (7, 7, 9, 11, 13, 15, 17, 19)

LN_V = 1408

SWAP = [i + 8 if i < 8 else i - 8 if i < 16 else i for i in range(32)]


def build(nc, x, x_t, wall, a_gw, a_scale, sinks, rel_rev, ln_gain, ln_bias, rope_cos, rope_sin,
          pool_coef, pool_inv, out):
    with ExitStack() as ctx:
        def sb(name, shape, dt=F32):
            return ctx.enter_context(nc.sbuf_tensor(name, shape, dt))

        def psum(name, shape):
            return ctx.enter_context(nc.psum_tensor(name, shape, F32))

        def sem(name):
            return ctx.enter_context(nc.semaphore(name))

        x1 = nc.dram_tensor("x1_scratch", (SEQ, D), F32, kind="Internal").ap()
        res_d = nc.dram_tensor("res_scratch", (4, P, QT, 512), F32, kind="Internal").ap()
        hist_d = nc.dram_tensor("hist_scratch", (C_PAIRS, P, 4, 512), F32, kind="Internal").ap()
        tz_d = nc.dram_tensor("bias_rows_scratch", (DEPTH * 8, P * TZ), F32, kind="Internal").ap()

        x_at = -(-nc.sbuf_base // 32) * 32
        xh = sb("xh", [P, KT, HALF], F32R)
        xl = sb("xl", [P, KT, HALF], F32R)
        mixh = sb("mixh", [P, KT, HALF], F32R)
        mixl = sb("mixl", [P, KT, HALF], F32R)
        raw = sb("raw", [P, RING, UNIT])
        wh = sb("wh", [P, RING, UNIT], F32R)
        wl = sb("wl", [P, RING, UNIT], F32R)
        bkh = sb("bkh", [P, P + HALF], F32R)
        bkl = sb("bkl", [P, P + HALF], F32R)
        bvh = sb("bvh", [P, 1 + QT, P], F32R)
        bvl = sb("bvl", [P, 1 + QT, P], F32R)
        bqh = sb("bqh", [P, HALF], F32R)
        bql = sb("bql", [P, HALF], F32R)
        pth = sb("pth", [P, 5, 2, P], F32R)
        ptl = sb("ptl", [P, 5, 2, P], F32R)
        prob = sb("prob", [P, 2, C_KEYS])
        res = sb("res", [P, QT, 512])
        gate = sb("gate", [P, HALF])
        tmp = sb("tmp", [P, HALF])
        av = sb("av", [P, 16 + HALF])
        s0 = sb("s0", [P, 16 + HALF])
        s1 = sb("s1", [P, 16 + HALF])
        brope = sb("brope", [P, 2, 512])
        gw = sb("gw", [P, P])
        gwh = sb("gwh", [P, P], F32R)
        gwl = sb("gwl", [P, P], F32R)
        ident = sb("ident", [P, P])
        a_tail = sb("a_tail", [P, A_GROUPS, 16])
        coef = sb("coef", [P, A_GROUPS, 4])
        inv16 = sb("inv16", [P, A_GROUPS, 16])
        coef1 = sb("coef1", [P, 4])
        inv1 = sb("inv1", [P, 16])
        scale_s = sb("scale_s", [P, DEPTH, A_GROUPS])
        scale1 = sb("scale1", [P, 1])
        sink_s = sb("sink_s", [P, DEPTH, B_TILES, 2])
        sink1 = sb("sink1", [P, 2, 2])
        nmax = sb("nmax", [P, 4, 2])
        mx = sb("mx", [P, 4, 2])
        psums = sb("psums", [P, 4, 2])
        esink = sb("esink", [P, 4, 2])
        rinv = sb("rinv", [P, 4, 2])
        stats = sb("stats", [P, QT, 4, 6])
        mv = sb("mv", [P, QT, 2])
        veps = sb("veps", [P, QT])
        sq = sb("sq", [P, QT])
        sq2 = sb("sq2", [P, QT])
        rstd = sb("rstd", [P, QT])
        shift = sb("shift", [P, QT])

        ck_h, ck_l = (m[:, MIX_B:MIX_B + 2, :].rearrange("p a n -> p (a n)") for m in (mixh, mixl))
        cv_h, cv_l = (m[:, MIX_B + 2:MIX_B + 4, :].rearrange("p a (b n) -> p (a b) n", n=P) for m in (mixh, mixl))
        cq_h, cq_l = (m[:, MIX_B + 4, :] for m in (mixh, mixl))
        ya_h, ya_l = (m[:, MIX_B + 5, :] for m in (mixh, mixl))

        x_in = nc.alloc_sbuf_tensor_at("first_x", [P, KT, HALF], F32, offset=x_at + 2 * 4 * KT * HALF)
        sums = nc.alloc_sbuf_tensor_at("last_sums", [P, KT, HALF], F32, offset=x_at)
        gain_bias = nc.alloc_sbuf_tensor_at("last_gain_bias", [P, 2, D], F32, offset=x_at + 4 * KT * HALF)
        gain_all, bias_all = gain_bias[:, 0, :], gain_bias[:, 1, :]

        acc = [psum("acc0", [P, 512]), psum("acc1", [P, 512])]
        sc = [psum("sc0", [P, 1024]), psum("sc1", [P, 1024])]
        pv = psum("pv", [P, 1024])
        pv4 = pv[:, :].rearrange("p (j h q) -> p j h q", j=QT, h=2)
        even_banks = [acc[0][:, :], sc[0][:, 0:512], sc[0][:, 512:1024], acc[1][:, :]]
        odd_banks = [sc[1][:, 0:512], sc[1][:, 512:1024], pv[:, 0:512], pv[:, 512:1024]]

        w_raw = [sem(f"w_raw{i}") for i in range(RING)]
        w_hi = sem("w_hi")
        w_lo = sem("w_lo")
        w_used = sem("w_used")
        vn_full = sem("vn_full")
        a_full = sem("a_full")
        ident_ok = sem("ident_ok")
        const_in = sem("const_in")
        xin = [sem("xin0"), sem("xin1")]
        x0_in = [sem(f"x0_in{q}") for q in range(4)]
        tr_full = sem("tr_full")
        xh_ok = sem("xh_ok")
        xl_ok = sem("xl_ok")
        av_ok = sem("av_ok")
        ay_ok = sem("ay_ok")
        ayh_ok = sem("ayh_ok")
        ayl_ok = sem("ayl_ok")
        gw_in = sem("gw_in")
        gwh_ok = sem("gwh_ok")
        gwl_ok = sem("gwl_ok")
        vt_ok = sem("vt_ok")
        vh_ok = sem("vh_ok")
        v_ok = sem("v_ok")
        kh_ok = sem("kh_ok")
        k_ok = sem("k_ok")
        qh_ok = sem("qh_ok")
        q_ok = sem("q_ok")
        bq_ok = sem("bq_ok")
        rope_raw = sem("rope_raw")
        rope_ok = sem("rope_ok")
        hist_out = sem("hist_out")
        hist_in = sem("hist_in")
        bias_in = sem("bias_in")
        bias_ok = sem("bias_ok")
        rope_in = sem("rope_in")
        cs_full = sem("cs_full")
        cs_max = sem("cs_max")
        cs_exp = sem("cs_exp")
        cs_prob = sem("cs_prob")
        ct_full = sem("ct_full")
        ct_hi = sem("ct_hi")
        ct_lo = sem("ct_lo")
        c_pv = sem("c_pv")
        bs_full = sem("bs_full")
        bs_max = sem("bs_max")
        bs_exp = sem("bs_exp")
        bs_prob = sem("bs_prob")
        bt_full = sem("bt_full")
        bt_hi = sem("bt_hi")
        bt_lo = sem("bt_lo")
        b_pv = sem("b_pv")
        tanh_ok = sem("tanh_ok")
        gate_ok = sem("gate_ok")
        prod_ok = sem("prod_ok")
        mixh_ok = sem("mixh_ok")
        mixl_ok = sem("mixl_ok")
        out_full = sem("out_full")
        out_free = sem("out_free")
        res_in = sem("res_in")
        res_out = sem("res_out")
        res_ok = sem("res_ok")
        ln_var = sem("ln_var")
        ln_sqrt = sem("ln_sqrt")
        ln_in = sem("ln_in")
        ln_rstd = sem("ln_rstd")
        ln_unit = sem("ln_unit")
        ln_end_v = sem("ln_end_v")
        ln_end_p = sem("ln_end_p")
        pool_step = sem("pool_step")
        ln_ok = sem("ln_ok")
        ln_out = sem("ln_out")
        tzr_in = sem("tzr_in")
        tzr_ok = sem("tzr_ok")
        tz_out = sem("tz_out")
        hist_mv = sem("hist_mv")
        sp_step = sem("sp_step")
        dve = sem("dve_step")


        def layer(it):
            return it // 2

        def half(it):
            return it % 2

        def x_rows(it):
            src = x if layer(it) == 0 else x1
            return src[half(it) * HALF:(half(it) + 1) * HALF, :]

        def x_taken(it, n):
            return (xl_ok, n + 16 * (it + 1)) if layer(it + 1) == 0 else (tr_full, n + (16 * (it + 1 - 2) + 2))

        def last_rows(t, a, b):
            return sums[:, 4 * t:4 * t + 4, :].rearrange("p c n -> p (c n)")[:, a:b]

        def unit(it, r):
            return r + it * U_STEP

        block = ctx.enter_context(nc.Block())

        @block.sync
        def _(sp):
            sp.sem_inc(res_out, 16)

            def wait_alone(semaphore, value):
                sp.wait_ge(semaphore, value)
                sp.sem_inc(sp_step, 1)

            def load_unit(it, r, slot):
                sp.wait_ge(w_lo, unit(it, r) + 1)
                sp.dma_start(raw[:, slot, :], wall[layer(it), ds(r, 1)].rearrange("o p n -> (o p) n")
                             ).then_inc(w_raw[slot], 16)

            def load_ln(it, n):
                sp.wait_ge(res_out, 64 * (it + 1) + 16)
                sp.dma_start(res[:], res_d[ds(n, 1)].rearrange("o p t n -> (o p) t n")).then_inc(ln_in, 16)
                for slot, v in enumerate((ln_gain, ln_bias)):
                    sp.dma_start(prob[:, slot, 0:512], v[layer(it), ds(n, 1), :].to_broadcast([P, 512])
                                 ).then_inc(ln_in, 16)

            def store_ln(it, n):
                wait_alone(ln_ok, n + (4 * it + 1))
                dst = (x1 if layer(it) == 0 else out)[half(it) * HALF:(half(it) + 1) * HALF, :]
                sp.dma_start(dst.rearrange("(t p) (c n) -> c p t n", p=P, n=512)[ds(n, 1)]
                             .rearrange("o p t n -> (o p) t n"), res[:]).then_inc(ln_out, 16)
                wait_alone(ln_out, n * 16 + (64 * it + 16))

            for q in range(4):
                load_unit(0, q, q)
                sp.dma_start(x_in[:, 4 * q:4 * q + 4, :],
                             x_t[4 * q * P:4 * (q + 1) * P, 0:HALF].rearrange("(k p) n -> p k n", p=P)
                             ).then_inc(x0_in[q], 16)
                if q == 0:
                    sp.dma_start(tmp[0:DEPTH * 8, 127:127 + 257], rel_rev).then_inc(tzr_in, 16)
                    sp.dma_start(coef[:], pool_coef).then_inc(const_in, 16)
                    sp.dma_start(inv16[:], pool_inv).then_inc(const_in, 16)
                    sp.dma_start(scale_s[:], a_scale).then_inc(const_in, 16)
                    sp.dma_start(sink_s[:].rearrange("p a b c -> p (a b c)"),
                                 sinks.to_broadcast([P, DEPTH * B_HEADS])).then_inc(const_in, 16)
            sp.wait_ge(tzr_ok, 1)
            sp.dma_start(tz_d.rearrange("h (q c) -> h q c", c=TZ),
                         tmp[0:DEPTH * 8, 0:TZ].rearrange("h (o c) -> h o c", o=1).to_broadcast([DEPTH * 8, P, TZ])
                         ).then_inc(tz_out, 16)

            for it in range(STEPS):
                with sp.Fori(0, C_PAIRS) as p:
                    for s in range(U_C):
                        if s == 4:
                            sp.wait_ge(gwl_ok, p + (C_PAIRS * it + 1))
                            sp.dma_start(gw[:], a_gw[layer(it), ds(p, 1)].rearrange("o c d -> (o c) d")
                                         ).then_inc(gw_in, 16)
                        if s == 9 and half(it):
                            sp.wait_ge(w_used, unit(it, p * U_C) + (2 + RING))
                            for n, m in enumerate((mixh, mixl)):
                                sp.dma_start(m[:, MIX_B:MIX_B + 3:2, :].bitcast(F32),
                                             hist_d[ds(p, 1), :, 2 * n:2 * n + 2, :].rearrange("o p a n -> (o p) a n")
                                             ).then_inc(hist_in, 16)
                        if s == 10:
                            sp.wait_ge(bias_ok, p + (C_PAIRS * it + 1))
                            if it:
                                sp.wait_ge(rope_ok, (B_TILES + 1) * it)
                            else:
                                sp.wait_ge(tz_out, 16)
                            sp.dma_start(brope[:, 0, :].rearrange("p (h n) -> p h n", h=2),
                                         tz_d[ds(2 * p + 8 * layer(it), 2), 127:127 + P * (TZ - 1)]
                                         .rearrange("h (q c) -> q h c", c=TZ - 1)[:, :, 0:NEAR]).then_inc(bias_in, 16)
                        if s == 12 and it:
                            sp.wait_ge(w_used, unit(it, p * U_C) + (1 + RING))
                            load_ln(it - 1, p)
                        if s == 22 and it:
                            store_ln(it - 1, p)
                        if s == 23 and not half(it):
                            wait_alone(k_ok, p + (C_PAIRS * it + 1))
                            wait_alone(v_ok, p + ((C_PAIRS + 1) * it + 1))
                            for n, m in enumerate((mixh, mixl)):
                                sp.dma_start(hist_d[ds(p, 1), :, 2 * n:2 * n + 2, :].rearrange("o p a n -> (o p) a n"),
                                             m[:, MIX_B + 1:MIX_B + 4:2, :].bitcast(F32)).then_inc(hist_out, 16)
                        if it == 0:
                            load_unit(it, p * U_C + (s + RING), s % RING)
                        else:
                            load_unit(it, p * U_C + s, s % RING)
                for s in range(U_KV):
                    if it or s >= RING:
                        load_unit(it, KV0 + s, s % RING)
                sp.wait_ge(cs_max, 8 * C_PAIRS * (it + 1))
                sp.dma_start(brope[:, 0, :], rope_cos[half(it)]).then_inc(rope_in, 16)
                sp.dma_start(brope[:, 1, :], rope_sin[half(it)]).then_inc(rope_in, 16)
                with sp.Fori(0, B_TILES) as i:
                    for s in range(U_B):
                        load_unit(it, i * U_B + (B0 + s), s % RING)
                with sp.Fori(0, 2) as m:
                    for s in range(2 * U_N):
                        load_unit(it, m * (2 * U_N) + (O0 + s), s % RING)
                        for gg in range(8):
                            if it + 1 == STEPS or s != X_LOAD[gg]:
                                continue
                            sp.wait_ge(bt_full, 4 * B_TILES * (it + 1))
                            sp.wait_ge(*x_taken(it, m * 8 + gg - 1))
                            if layer(it + 1) == 0:
                                src = x_t.rearrange("(k p) n -> k p n", p=P)[ds(m * 8 + gg, 1), :, HALF:2 * HALF]
                            else:
                                src = x_rows(it + 1).rearrange("(t p) (k n) -> t k p n", p=P, n=512)
                                src = src[ds(2 * m + gg // 4, 1), gg % 4]
                            sp.dma_start(prob[:, gg % 2, 0:512], src.rearrange("o p n -> (o p) n")
                                         ).then_inc(xin[gg % 2], 16)
                        if s in (14, 30):
                            n = 2 * m + s // 16
                            if it + 1 < STEPS:
                                sp.wait_ge(res_out, n * 16 + (64 * it + 16))
                            else:
                                sp.wait_ge(out_free, n * 4 + (16 * it + 8))
                            src = x_rows(it).rearrange("(t p) (c n) -> c p t n", p=P, n=512)
                            sp.dma_start(res[:], src[ds(n, 1)].rearrange("o p t n -> (o p) t n")).then_inc(res_in, 16)
            for r in range(AHEAD):
                sp.wait_ge(w_lo, STEPS * U_STEP + r + 1)
                sp.dma_start(raw[:, r, :], wall[DEPTH - 1, 0]).then_inc(w_raw[r], 16)
            sp.wait_ge(w_used, unit(STEPS - 1, O0) + RING)
            for o, v in ((gain_all, ln_gain), (bias_all, ln_bias)):
                sp.dma_start(o, v[DEPTH - 1].rearrange("c n -> (c n)").rearrange("(o n) -> o n", o=1)
                             .to_broadcast([P, D])).then_inc(ln_in, 16)
            rows = out[HALF:2 * HALF, :].rearrange("(t p) n -> t p n", p=P)
            for t in range(QT):
                sp.wait_ge(ln_end_v, t + 1)
                sp.dma_start(rows[t, :, 0:LN_V], last_rows(t, 0, LN_V)).then_inc(ln_out, 16)
                sp.wait_ge(ln_end_p, t + 1)
                sp.dma_start(rows[t, :, LN_V:D], last_rows(t, LN_V, D)).then_inc(ln_out, 16)
            sp.wait_ge(ln_out, 16 * 4 * (STEPS - 1) + 32 * QT)

        @block.tensor
        def _(pe):
            def mm(o, lhsT, rhs, start, stop):
                return nc.tensor.matmul(o, lhsT, rhs, start=start, stop=stop)

            pe.sem_inc(w_used, RING)
            pe.sem_inc(tr_full, 2)

            def project(it, r, q, bank, slot):
                pe.wait_ge(w_lo, unit(it, r) + (1 + RING))
                for kk in range(4):
                    k = 4 * q + kk
                    hi, lo = (w[:, slot, kk * P:(kk + 1) * P] for w in (wh, wl))
                    mm(bank, hi, xh[:, k, :], k == 0, False)
                    mm(bank, hi, xl[:, k, :], False, False)
                    last = mm(bank, lo, xh[:, k, :], False, k == KT - 1)
                last.then_inc(w_used, 1)

            def transpose_x(g, bank):
                for b in range(4):
                    last = nc.tensor.transpose(bank[:, b * P:(b + 1) * P], prob[:, g % 2, b * P:(b + 1) * P], ident[:])
                last.then_inc(tr_full, 1)

            def transpose_values(bank):
                for b in range(QT):
                    last = nc.tensor.transpose(bank[:, b * P:(b + 1) * P], tmp[:, b * P:(b + 1) * P], ident[:])
                last.then_inc(vn_full, 1)

            def c_scores(it, p, j):
                c0 = 0 if half(it) else 512 - P * j
                for h in range(2):
                    pe.wait_ge(ct_lo, p * 8 + (8 * C_PAIRS * it + 2 * j + h + 1))
                    rows = slice(HD * h, HD * (h + 1))
                    qs = slice(P * j, P * (j + 1))
                    for a, b in ((c0, 512), (512, C_KEYS)):
                        if a >= b:
                            continue
                        ks = slice(P * j + a, P * j + b)
                        mm(sc[h][:, a:b], cq_h[rows, qs], ck_h[rows, ks], True, False)
                        mm(sc[h][:, a:b], cq_h[rows, qs], ck_l[rows, ks], False, False)
                        last = mm(sc[h][:, a:b], cq_l[rows, qs], ck_h[rows, ks], False, True)
                    last.then_inc(cs_full, 1)

            def c_transpose(it, p, j):
                c0 = 0 if half(it) else 512 - P * j
                for h in range(2):
                    pe.wait_ge(cs_prob, p * 8 + (8 * C_PAIRS * it + 2 * j + h + 1))
                    for b in range(c0 // P, 5):
                        cs = slice(b * P, (b + 1) * P)
                        last = nc.tensor.transpose(sc[h][:, cs], prob[:, h, cs], ident[:])
                    last.then_inc(ct_full, 1)

            def attend(region, values, blocks):
                n = 3 * len(blocks)
                i = 0
                for vb, pb in blocks:
                    for v, pt in ((values[0], pth), (values[0], ptl), (values[1], pth)):
                        last = mm(region, v[:, vb, :], pt[:, pb, :, :].rearrange("p h q -> p (h q)"), i == 0, i == n - 1)
                        i += 1
                return last

            def c_attend(it, p, j):
                if j == 0:
                    pe.wait_ge(prod_ok, p * 2 + (MIXES * it + 2))
                pe.wait_ge(ct_lo, p * 8 + (8 * C_PAIRS * it + 2 * j + 2 + 2))
                v0 = 0 if half(it) else 4 - j
                attend(pv[:, 256 * j:256 * (j + 1)], (cv_h, cv_l), [(j + v, v) for v in range(v0, 5)]
                       ).then_inc(c_pv, 1)

            def b_scores(it, i):
                pe.wait_ge(bq_ok, i + ((B_TILES + 1) * it + 2))
                pe.wait_ge(bt_lo, i * 4 + (4 * B_TILES * it + 4))
                for jj in range(2):
                    for h in range(2):
                        rows = slice(HD * h, HD * (h + 1))
                        for t in range(2):
                            j = 2 * jj + t
                            c0 = HD if half(it) == 0 and j == 0 else 0
                            o = sc[h][:, 512 * jj + 192 * t + c0:512 * jj + 192 * (t + 1)]
                            qs, ks = slice(P * j, P * (j + 1)), slice(P * j + HD + c0, P * j + 2 * P)
                            mm(o, bqh[rows, qs], bkh[rows, ks], True, False)
                            mm(o, bqh[rows, qs], bkl[rows, ks], False, False)
                            last = mm(o, bql[rows, qs], bkh[rows, ks], False, True)
                        last.then_inc(bs_full, 1)

            def b_transpose(it, i, jj):
                for h in range(2):
                    pe.wait_ge(bs_prob, i * 4 + (4 * B_TILES * it + 2 * jj + h + 1))
                    for t in range(2):
                        for b in range(2):
                            if half(it) == 0 and jj == t == b == 0:
                                continue
                            c = 256 * t + P * b
                            last = nc.tensor.transpose(sc[h][:, 512 * jj + c:512 * jj + c + P], prob[:, h, c:c + P], ident[:])
                    last.then_inc(bt_full, 1)

            def b_attend(it, i, jj):
                if jj == 0:
                    pe.wait_ge(prod_ok, i + (MIXES * it + 2 * C_PAIRS + 2))
                pe.wait_ge(bt_lo, i * 4 + (4 * B_TILES * it + 2 * jj + 2 + 4))
                for t in range(2):
                    j = 2 * jj + t
                    bs = [1] if half(it) == 0 and j == 0 else [0, 1]
                    last = attend(pv[:, 256 * j:256 * (j + 1)], (bvh, bvl), [(j + b, 2 * t + b) for b in bs])
                last.then_inc(b_pv, 1)

            pe.wait_ge(ident_ok, 2)
            for it in range(STEPS):
                pe.wait_ge(xl_ok, 16 * it + (16 if it else 4))
                if it:
                    pe.wait_ge(out_free, 16 * it + 8)
                pe.wait_ge(prod_ok, MIXES * it + 1)
                project(it, 0, 0, acc[0][:, :], 0)
                with pe.Fori(0, C_PAIRS) as p:
                    def quarter(s, bank):
                        project(it, p * U_C + s, s % 4, acc[bank][:, :], s % RING)

                    for s in range(1, 4):
                        if it == 0:
                            pe.wait_ge(xl_ok, 4 * (s + 1))
                        quarter(s, 0)
                    pe.wait_ge(gate_ok, p * 2 + (MIXES * it + 1))
                    for s in range(4, 8):
                        quarter(s, 1)
                    pe.wait_ge(av_ok, p + (C_PAIRS * it + 1))
                    for s in range(8, 10):
                        quarter(s, 0)
                    pe.wait_ge(vt_ok, p + ((C_PAIRS + 1) * it + 1))
                    transpose_values(acc[1])
                    for s in range(10, 12):
                        quarter(s, 0)
                    pe.wait_ge(v_ok, p + ((C_PAIRS + 1) * it + 1))
                    for s in range(12, 16):
                        quarter(s, 1)
                    pe.wait_ge(k_ok, p + (C_PAIRS * it + 1))
                    quarter(16, 0)
                    pe.wait_ge(q_ok, p + (C_PAIRS * it + 1))
                    if half(it):
                        pe.wait_ge(hist_in, p * 32 + (32 * C_PAIRS * layer(it) + 32))
                    c_scores(it, p, 0)
                    quarter(17, 0)
                    c_transpose(it, p, 0)
                    quarter(18, 0)
                    c_scores(it, p, 1)
                    c_attend(it, p, 0)
                    quarter(19, 0)
                    c_transpose(it, p, 1)
                    quarter(20, 1)
                    c_scores(it, p, 2)
                    c_attend(it, p, 1)
                    quarter(21, 1)
                    c_transpose(it, p, 2)
                    pe.wait_ge(gate_ok, p * 2 + (MIXES * it + 2))
                    pe.wait_ge(ayl_ok, p + (C_PAIRS * it + 1))
                    pe.wait_ge(gwl_ok, p + (C_PAIRS * it + 2))
                    mm(acc[0][:, :], gwh[:], ya_h, True, False)
                    mm(acc[0][:, :], gwh[:], ya_l, False, False)
                    mm(acc[0][:, :], gwl[:], ya_h, False, True).then_inc(a_full, 1)
                    quarter(22, 1)
                    c_scores(it, p, 3)
                    c_attend(it, p, 2)
                    quarter(23, 1)
                    c_transpose(it, p, 3)
                    pe.wait_ge(prod_ok, p * 2 + (MIXES * it + 3))
                    quarter(24, 0)
                    c_attend(it, p, 3)

                for s in range(1, 4):
                    project(it, KV0 + s, s, acc[0][:, :], s % RING)
                pe.wait_ge(gate_ok, MIXES * it + 2 * C_PAIRS + 1)
                for s in range(4):
                    project(it, KV0 + 4 + s, s, acc[1][:, :], s % RING)
                pe.wait_ge(rope_raw, ROTS * it + 1)
                for s in range(4):
                    project(it, B0 + s, s, acc[0][:, :], s % RING)
                    if s == 1:
                        pe.wait_ge(vt_ok, (C_PAIRS + 1) * (it + 1))
                        transpose_values(acc[1])
                pe.wait_ge(v_ok, (C_PAIRS + 1) * (it + 1))
                with pe.Fori(1, B_TILES) as i:
                    def quarter(s):
                        project(it, i * U_B + (B0 - 4 + s), s % 4, acc[s // 4][:, :], s % RING)
                    pe.wait_ge(rope_raw, i + (ROTS * it + 1))
                    quarter(0)
                    b_scores(it, i - 1)
                    quarter(1)
                    quarter(2)
                    b_transpose(it, i - 1, 0)
                    quarter(3)
                    b_attend(it, i - 1, 0)
                    pe.wait_ge(gate_ok, i + (MIXES * it + 2 * C_PAIRS))
                    quarter(4)
                    b_transpose(it, i - 1, 1)
                    quarter(5)
                    b_attend(it, i - 1, 1)
                    quarter(6)
                    quarter(7)
                b_scores(it, B_TILES - 1)
                pe.wait_ge(gate_ok, MIXES * (it + 1))
                for s in range(4):
                    project(it, O0 - 4 + s, s, acc[1][:, :], s % RING)
                    if s in (2, 3):
                        b_attend(it, B_TILES - 1, s - 2)
                    if s in (1, 2):
                        b_transpose(it, B_TILES - 1, s - 1)

                pe.wait_ge(rope_raw, ROTS * (it + 1))
                pe.wait_ge(bt_lo, 4 * B_TILES * (it + 1) + 4)
                pe.wait_ge(mixl_ok, 16 * it + 16)
                with pe.Fori(0, 2) as m:
                    for n in range(2):
                        banks = (even_banks, odd_banks)[n]
                        if n and 2 <= it + 1 < STEPS:
                            pe.wait_ge(xl_ok, m * 8 + (16 * (it + 1) + 8))
                        if n:
                            pe.wait_ge(prod_ok, MIXES * (it + 1) + 2)
                        for k in range(KT):
                            u = n * U_N + k
                            pe.wait_ge(w_lo, unit(it, m * (2 * U_N) + (O0 + u)) + (1 + RING))
                            if k == KT - 1:
                                pe.wait_ge(mixl_ok, 16 * (it + 1) + 1)
                            for t in range(QT):
                                if k == 0:
                                    pe.wait_ge(out_free, m * 8 + (16 * it + 4 * n + t + 1))
                                    if n == 0 and t == QT - 1:
                                        pe.wait_ge(gate_ok, MIXES * (it + 1) + 1)
                                ts = slice(t * P, (t + 1) * P)
                                kt = MIX_ORDER[k]
                                w_h, w_l = wh[:, u % RING, :], wl[:, u % RING, :]
                                mm(banks[t], mixh[:, kt, ts], w_h, k == 0, False)
                                mm(banks[t], mixh[:, kt, ts], w_l, False, False)
                                last = mm(banks[t], mixl[:, kt, ts], w_h, False, k == KT - 1)
                                if k == KT - 1 and t < QT - 1:
                                    last.then_inc(out_full, 1)
                            last.then_inc(w_used, 1)
                            if n == 0 and k in X_AT and 2 <= it + 1 < STEPS:
                                gg = X_AT.index(k)
                                pe.wait_ge(prod_ok, MIXES * (it + 1) + 2)
                                if gg >= 4:
                                    pe.wait_ge(xl_ok, m * 8 + (16 * (it + 1) + gg - 3))
                                else:
                                    pe.wait_ge(out_free, m * 8 + (16 * it + gg + 5))
                                pe.wait_ge(xin[gg % 2], m * 64 + (128 * it + 16 * (gg // 2 + 1)))
                                transpose_x(gg, odd_banks[gg % 4])

        @block.scalar
        def _(act):
            def copy(o, i, scale=1.0):
                return nc.scalar.activation(o, i, ACT.Copy, scale=scale)

            def split(it, r, slot):
                u = unit(it, r) + AHEAD
                slot = (slot + AHEAD) % RING
                split_at(u, slot)

            def split_at(u, slot):
                act.wait_ge(w_raw[slot], (u - slot) * (16 // RING) + 16)
                act.wait_ge(w_used, u + 1)
                copy(wh[:, slot, :], raw[:, slot, :]).then_inc(w_hi, 1)

            def used(it, r):
                act.wait_ge(w_used, unit(it, r) + (1 + RING))

            def mix_hi(count, tile):
                act.wait_ge(prod_ok, count + 2)
                copy(mixh[:, ds(tile, 1), :].rearrange("p o n -> p (o n)"), tmp[:]).then_inc(mixh_ok, 1)

            def tanh_gate(bank):
                nc.scalar.activation(tmp[:], acc[bank][:, :], ACT.Tanh, scale=0.5).then_inc(tanh_ok, 1)

            def x_hi_tile(tile, source):
                copy(xh[:, ds(tile, 1), :].rearrange("p o n -> p (o n)"), source).then_inc(xh_ok, 1)

            def x_hi(idx, gg, bank, t):
                act.wait_ge(tr_full, idx + (1 + 2 - 32))
                copy(xh[:, 4 * (gg % 4):4 * (gg % 4) + 4, ds(t * P, P)],
                     bank.rearrange("p (k q) -> p k q", k=4)).then_inc(xh_ok, 1)

            for q in range(4):
                if q < AHEAD:
                    split_at(q, q)
                act.wait_ge(x0_in[q], 16)
                for k in range(4 * q, 4 * q + 4):
                    copy(xh[:, k, :], x_in[:, k, :]).then_inc(xh_ok, 1)

            def c_exp(it, p, j):
                c0 = 0 if half(it) else 512 - P * j
                for h in range(2):
                    act.wait_ge(cs_max, p * 8 + (8 * C_PAIRS * it + 2 * j + h + 1))
                    nc.scalar.activation(prob[:, h, c0:C_KEYS], sc[h][:, c0:C_KEYS], ACT.Exp,
                                         bias=nmax[:, h, 0:1], accum_out=psums[:, h, 0:1]).then_inc(cs_exp, 1)

            def c_hi(it, p, j):
                b0 = 0 if half(it) else 4 - j
                for h in range(2):
                    act.wait_ge(ct_full, p * 8 + (8 * C_PAIRS * it + 2 * j + h + 1))
                    copy(pth[:, b0:5, h, :], sc[h][:, b0 * P:5 * P].rearrange("p (b q) -> p b q", q=P)).then_inc(ct_hi, 1)

            def b_exp(it, i, u):
                jj, h = u // 2, u % 2
                act.wait_ge(bs_max, i * 4 + (4 * B_TILES * it + u + 1))
                if jj:
                    act.wait_ge(bt_full, i * 4 + (4 * B_TILES * it + h + 1))
                for t in range(2):
                    nc.scalar.activation(prob[:, h, 256 * t + HD:256 * (t + 1)], sc[h][:, 512 * jj + 192 * t:512 * jj + 192 * (t + 1)],
                                         ACT.Exp, bias=nmax[:, u, t:t + 1], accum_out=psums[:, u, t:t + 1])
                nc.scalar.activation(esink[:, u, :], nmax[:, u, :], ACT.Exp, bias=sink1[:, 0, h:h + 1]).then_inc(bs_exp, 1)

            def b_hi(it, i, u):
                jj, h = u // 2, u % 2
                b0 = 1 if half(it) == 0 and jj == 0 else 0
                act.wait_ge(bt_full, i * 4 + (4 * B_TILES * it + u + 1))
                copy(pth[:, b0:4, h, :], sc[h][:, 512 * jj + b0 * P:512 * (jj + 1)].rearrange("p (b q) -> p b q", q=P)
                     ).then_inc(bt_hi, 1)

            def rope_copy(it, n, scale):
                if isinstance(n, int) and n == 0:
                    act.wait_ge(ayl_ok, C_PAIRS * (it + 1))
                else:
                    act.wait_ge(bq_ok, n + ROTS * it)
                copy(s0[:, 0:HALF], acc[0][:, :], scale).then_inc(rope_raw, 1)

            for it in range(STEPS):
                nb = 16 * it
                split(it, 0, 0)
                split(it, 1, 1)
                if 0 < it:
                    act.wait_ge(ln_var, it)
                    nc.scalar.activation(sq[:], veps[:], ACT.Sqrt).then_inc(ln_sqrt, 1)
                with act.Fori(0, C_PAIRS) as p:
                    def slot(s):
                        split(it, p * U_C + s, s % RING)
                    pc = C_PAIRS * it

                    for s in range(2, 5):
                        slot(s)
                    used(it, p * U_C + 3)
                    copy(av[:, 16:16 + HALF], acc[0][:, :]).then_inc(av_ok, 1)
                    slot(5)
                    slot(6)
                    act.wait_ge(gw_in, p * 16 + (16 * pc + 16))
                    copy(gwh[:], gw[:]).then_inc(gwh_ok, 1)
                    slot(7)
                    act.wait_ge(mixl_ok, p * 2 + (nb + 1))
                    if it == 0:
                        act.wait_ge(tz_out, 16)
                    used(it, p * U_C + 7)
                    copy(tmp[:], acc[1][:, :]).then_inc(vt_ok, 1)
                    slot(8)
                    slot(9)
                    act.wait_ge(ay_ok, p + (pc + 1))
                    copy(ya_h, s0[:, 16:16 + HALF]).then_inc(ayh_ok, 1)
                    act.wait_ge(vn_full, p + ((C_PAIRS + 1) * it + 1))
                    copy(cv_h[:, 4:8, :], acc[1][:, :].rearrange("p (b c) -> p b c", c=P)).then_inc(vh_ok, 1)
                    slot(10)
                    slot(11)
                    used(it, p * U_C + 11)
                    copy(ck_h[:, HALF:2 * HALF], acc[0][:, :]).then_inc(kh_ok, 1)
                    slot(12)
                    slot(13)
                    slot(14)
                    slot(15)
                    used(it, p * U_C + 15)
                    copy(cq_h, acc[1][:, :], SCALE).then_inc(qh_ok, 1)
                    slot(16)
                    slot(17)
                    c_exp(it, p, 0)
                    slot(18)
                    c_hi(it, p, 0)
                    slot(19)
                    c_exp(it, p, 1)
                    slot(20)
                    c_hi(it, p, 1)
                    used(it, p * U_C + 19)
                    tanh_gate(0)
                    slot(21)
                    c_exp(it, p, 2)
                    slot(22)
                    c_hi(it, p, 2)
                    mix_hi(p * 2 + (nb + 1), p + MIX_A)
                    slot(23)
                    c_exp(it, p, 3)
                    c_hi(it, p, 3)
                    used(it, p * U_C + 23)
                    act.wait_ge(mixl_ok, p * 2 + (nb + 1 + 1))
                    tanh_gate(1)
                    mix_hi(p * 2 + (nb + 2), p + MIX_C)
                    if not half(it):
                        act.wait_ge(hist_out, p * 32 + (32 * C_PAIRS * layer(it) + 32))
                    slot(24)
                    slot(25)

                for s in range(2, 4):
                    split(it, KV0 + s, s % RING)
                split(it, KV0 + 4, 0)
                used(it, KV0 + 3)
                rope_copy(it, 0, 1.0)
                split(it, KV0 + 5, 1)
                if half(it):
                    act.wait_ge(hist_mv, layer(it) + 1)
                act.wait_ge(rope_ok, (B_TILES + 1) * it + 1)
                copy(bkh[:, P:], s0[:, 0:HALF]).then_inc(qh_ok, 1)
                split(it, KV0 + 6, 2)
                split(it, KV0 + 7, 3)
                split(it, B0, 0)
                act.wait_ge(mixl_ok, nb + 2 * C_PAIRS + 1)
                used(it, KV0 + 7)
                copy(tmp[:], acc[1][:, :]).then_inc(vt_ok, 1)
                split(it, B0 + 1, 1)
                split(it, B0 + 2, 2)
                act.wait_ge(vn_full, (C_PAIRS + 1) * (it + 1))
                copy(bvh[:, 1:, :], acc[1][:, :].rearrange("p (b c) -> p b c", c=P)).then_inc(vh_ok, 1)
                split(it, B0 + 3, 3)
                used(it, B0 + 3)
                rope_copy(it, 1, SCALE)
                act.wait_ge(rope_ok, (B_TILES + 1) * it + 2)
                copy(bqh[:], s0[:, 0:HALF]).then_inc(qh_ok, 1)
                with act.Fori(1, B_TILES) as i:
                    def slot(s):
                        split(it, i * U_B + (B0 - 4 + s), s % RING)
                    slot(0)
                    b_exp(it, i - 1, 0)
                    b_exp(it, i - 1, 1)
                    slot(1)
                    slot(2)
                    b_hi(it, i - 1, 0)
                    b_hi(it, i - 1, 1)
                    b_exp(it, i - 1, 2)
                    b_exp(it, i - 1, 3)
                    slot(3)
                    slot(4)
                    used(it, i * U_B + (B0 - 4 + 3))
                    rope_copy(it, i + 1, SCALE)
                    b_hi(it, i - 1, 2)
                    b_hi(it, i - 1, 3)
                    slot(5)
                    act.wait_ge(rope_ok, i + ((B_TILES + 1) * it + 2))
                    copy(bqh[:], s0[:, 0:HALF]).then_inc(qh_ok, 1)
                    slot(6)
                    slot(7)
                    used(it, i * U_B + (B0 - 4 + 7))
                    tanh_gate(1)
                    mix_hi(i + (nb + 2 * C_PAIRS), i + (MIX_B - 1))
                    act.wait_ge(mixl_ok, i + (nb + 2 * C_PAIRS + 1))
                last = B_TILES - 1
                split(it, O0 - 4, 0)
                b_exp(it, last, 0)
                b_exp(it, last, 1)
                split(it, O0 - 3, 1)
                split(it, O0 - 2, 2)
                b_hi(it, last, 0)
                b_hi(it, last, 1)
                b_exp(it, last, 2)
                b_exp(it, last, 3)
                split(it, O0 - 1, 3)
                b_hi(it, last, 2)
                b_hi(it, last, 3)
                used(it, O0 - 1)
                tanh_gate(1)
                mix_hi(nb + 16, MIX_B + last)

                with act.Fori(0, 2) as m:
                    for s in range(2 * U_N):
                        split(it, m * (2 * U_N) + (O0 + s), s % RING)
                        if s in X_AT and it + 1 < STEPS:
                            gg = X_AT.index(s)
                            if layer(it + 1) == 0:
                                act.wait_ge(xin[gg % 2], m * 64 + (128 * it + 16 * (gg // 2 + 1)))
                                x_hi_tile(m * 8 + gg, prob[:, gg % 2, 0:512])
                            else:
                                x_hi(m * 8 + (16 * (it + 1) + gg), gg, odd_banks[gg % 4], 2 * m + gg // 4)
                        if s % U_N == U_N - 1 and it + 1 < STEPS:
                            n = 2 * m + s // U_N
                            act.wait_ge(res_ok, n * 4 + (16 * it + 4))
                            act.dma_start(res_d[ds(n, 1)].rearrange("o p t n -> (o p) t n"), res[:]).then_inc(res_out, 16)

            nc.scalar.activation(sq2[:], ident[:, 0:QT], ACT.Sqrt)
            act.wait_ge(ln_var, STEPS)
            nc.scalar.activation(sq[:], veps[:], ACT.Sqrt).then_inc(ln_sqrt, 1)
            act.wait_ge(ln_rstd, 1)
            for t in range(QT):
                cols = last_rows(t, LN_V, D)
                nc.scalar.activation(cols, cols, ACT.Identity, scale=rstd[:, t:t + 1], bias=shift[:, t:t + 1]
                                     ).then_inc(ln_unit, 1)

        @block.gpsimd
        def _(pool):
            pool.sem_inc(w_lo, RING)
            nc.gpsimd.memset(ident[:], 0.0).then_inc(ident_ok, 1)
            pool.wait_ge(ident_ok, 1)
            nc.gpsimd.affine_select(out=ident[:], in_=ident[:], compare_op=ALU.not_equal, fill=1.0, base=0,
                                    pattern=[[-1, P]], channel_multiplier=1).then_inc(ident_ok, 1)
            with pool.Fori(0, STEPS * U_STEP, RING) as u:
                for s in range(RING):
                    pool.wait_ge(w_hi, u + (s + 1))
                    pool.wait_ge(w_used, u + (s + 1))
                    nc.gpsimd.tensor_tensor(wl[:, s, :], raw[:, s, :], wh[:, s, :].bitcast(F32), ALU.subtract
                                            ).then_inc(w_lo, 1)
            pool.wait_ge(ln_in, 48 * 4 * (STEPS - 1) + 32)
            for t in range(QT):
                cols = last_rows(t, LN_V, D)
                pool.wait_ge(ln_unit, t + 1)
                nc.gpsimd.tensor_tensor(cols, cols, gain_all[:, LN_V:D], ALU.mult).then_inc(pool_step, 1)
                pool.wait_ge(pool_step, t + 1)
                nc.gpsimd.tensor_tensor(cols, cols, bias_all[:, LN_V:D], ALU.add).then_inc(ln_end_p, 1)

        @block.vector
        def _(dv):
            V = nc.vector
            count = [0, 0]

            def section(value):
                count[0], count[1] = value, 0

            def V_(ins):
                count[1] += 1
                ins.then_inc(dve, 1)
                dv.wait_ge(dve, count[0] + count[1])

            dv.sem_inc(gwl_ok, 1)
            dv.sem_inc(bias_ok, 1)
            dv.sem_inc(ct_lo, 2)
            dv.sem_inc(bt_lo, 4)
            dv.sem_inc(prod_ok, 2)
            dv.sem_inc(mixl_ok, 1)
            dv.sem_inc(out_free, 8)
            dv.sem_inc(gate_ok, 1)

            def lo(o, whole, hi):
                return V.tensor_tensor(o, whole, hi.bitcast(F32), ALU.subtract)

            def x_lo(idx, gg, bank, t):
                dv.wait_ge(xh_ok, idx + 1)
                piece = (slice(None), slice(4 * (gg % 4), 4 * (gg % 4) + 4), ds(t * P, P))
                lo(xl[piece], bank.rearrange("p (k q) -> p k q", k=4), xh[piece]).then_inc(xl_ok, 1)

            def gate_ready(n, bank):
                dv.wait_ge(tanh_ok, n)
                V.scalar_tensor_tensor(gate[:], tmp[:], 1.0, acc[bank][:, :], ALU.add, ALU.mult).then_inc(gate_ok, 1)

            def mix_lo(n, tile):
                dv.wait_ge(mixh_ok, n)
                t = mixh[:, ds(tile, 1), :].rearrange("p o n -> p (o n)")
                lo(mixl[:, ds(tile, 1), :].rearrange("p o n -> p (o n)"), tmp[:], t).then_inc(mixl_ok, 1)

            def attention_product(gates):
                dv.wait_ge(gate_ok, gates + 1)
                for h in range(2):
                    rows = slice(HD * h, HD * (h + 1))
                    last = V.scalar_tensor_tensor(tmp[rows, :].rearrange("p (j q) -> p j q", q=P), pv4[rows, :, h, :], 0.5,
                                                  gate[rows, :].rearrange("p (j q) -> p j q", q=P), ALU.mult, ALU.mult)
                last.then_inc(prod_ok, 1)

            def c_max(it, p, j):
                c0 = 0 if half(it) else 512 - P * j
                for h in range(2):
                    s = sc[h]
                    dv.wait_ge(cs_full, p * 8 + (8 * C_PAIRS * it + 2 * j + h + 1))
                    if half(it):
                        V.memset(s[HD:P, 0:CHUNK], NEG_INF)
                    a = max(c0, C_KEYS - NEAR)
                    V_(V.tensor_tensor(s[:, a:C_KEYS], s[:, a:C_KEYS],
                                       brope[:, 1, NEAR * h + a - (C_KEYS - NEAR):NEAR * (h + 1)], ALU.add))
                    V.tensor_reduce(nmax[:, h, 0:1], s[:, c0:C_KEYS], AX, ALU.max, negate=True).then_inc(cs_max, 1)

            def c_normalise(it, p, j):
                c0 = 0 if half(it) else 512 - P * j
                for h in range(2):
                    dv.wait_ge(cs_exp, p * 8 + (8 * C_PAIRS * it + 2 * j + h + 1))
                    V_(V.reciprocal(rinv[:, h, 0:1], psums[:, h, 0:1]))
                    V.tensor_scalar(prob[:, h, c0:C_KEYS], prob[:, h, c0:C_KEYS], rinv[:, h, 0:1], None, ALU.mult
                                    ).then_inc(cs_prob, 1)

            def c_lo(it, p, j):
                b0 = 0 if half(it) else 4 - j
                for h in range(2):
                    dv.wait_ge(ct_hi, p * 8 + (8 * C_PAIRS * it + 2 * j + h + 1))
                    lo(ptl[:, b0:5, h, :], sc[h][:, b0 * P:5 * P].rearrange("p (b q) -> p b q", q=P), pth[:, b0:5, h, :]
                       ).then_inc(ct_lo, 1)

            def b_max(it, i, u):
                jj, h = u // 2, u % 2
                dv.wait_ge(bs_full, i * 4 + (4 * B_TILES * it + u + 1))
                s = sc[h][:, 512 * jj:512 * jj + 384].rearrange("p (t c) -> p t c", t=2)
                if half(it) == 0 and jj == 0:
                    V.memset(s[:, 0, 0:CHUNK], NEG_INF)
                    V.memset(s[HD:P, 1, 0:CHUNK], NEG_INF)
                else:
                    V.memset(s[HD:P, :, 0:CHUNK], NEG_INF)
                V_(V.memset(s[0:HD, :, 2 * CHUNK:3 * CHUNK], NEG_INF))
                V_(V.tensor_reduce(mx[:, u, :], s, AX, ALU.max, negate=True))
                V.tensor_scalar(nmax[:, u, :], mx[:, u, :], sink1[:, 1, h:h + 1], None, ALU.min).then_inc(bs_max, 1)

            def b_normalise(it, i, u):
                h = u % 2
                dv.wait_ge(bs_exp, i * 4 + (4 * B_TILES * it + u + 1))
                V_(V.tensor_tensor(mx[:, u, :], psums[:, u, :], esink[:, u, :], ALU.add))
                V_(V.reciprocal(rinv[:, u, :], mx[:, u, :]))
                for t in range(2):
                    cs = slice(256 * t + HD, 256 * (t + 1))
                    last = V.tensor_scalar(prob[:, h, cs], prob[:, h, cs], rinv[:, u, t:t + 1], None, ALU.mult)
                last.then_inc(bs_prob, 1)

            def b_lo(it, i, u):
                jj, h = u // 2, u % 2
                b0 = 1 if half(it) == 0 and jj == 0 else 0
                dv.wait_ge(bt_hi, i * 4 + (4 * B_TILES * it + u + 1))
                lo(ptl[:, b0:4, h, :], sc[h][:, 512 * jj + b0 * P:512 * (jj + 1)].rearrange("p (b q) -> p b q", q=P),
                   pth[:, b0:4, h, :]).then_inc(bt_lo, 1)

            def sinks_of(it, i):
                V_(V.tensor_copy(sink1[:, 0, :], sink_s[:, layer(it), ds(i, 1), :].rearrange("p o h -> p (o h)")))
                V_(V.tensor_scalar(sink1[:, 1, :], sink1[:, 0, :], -1.0, None, ALU.mult))

            def rotate(n):
                dv.wait_ge(rope_raw, n)
                x_, y_ = s0[:, 0:HALF], s1[:, 0:HALF]
                V.tensor_tensor(y_, x_, brope[:, 0, :], ALU.mult)
                V_(V.stream_shuffle(x_, x_, SWAP))
                V_(V.tensor_tensor(x_, x_, brope[:, 1, :], ALU.mult))
                V.tensor_tensor(x_, x_, y_, ALU.add).then_inc(rope_ok, 1)

            def rotated(o, hi, n):
                dv.wait_ge(qh_ok, n)
                lo(o, s0[:, 0:HALF], hi).then_inc(bq_ok, 1)

            def layer_norm(it, n):
                dv.wait_ge(ln_in, n * 48 + (192 * it + 48))
                for t in range(QT):
                    last = V.tensor_scalar(res[:, t, :], res[:, t, :], mv[:, t, 0:1], rstd[:, t:t + 1],
                                           ALU.subtract, ALU.mult)
                V_(last)
                for slot, op in ((0, ALU.mult), (1, ALU.add)):
                    v = prob[:, slot, 0:512].rearrange("p (o n) -> p o n", o=1).to_broadcast([P, QT, 512])
                    last = V.tensor_tensor(res[:], res[:], v, op)
                    if slot == 0:
                        V_(last)
                last.then_inc(ln_ok, 1)

            def first_lo(k):
                dv.wait_ge(xh_ok, k + 1)
                lo(xl[:, k, :], x_in[:, k, :], xh[:, k, :]).then_inc(xl_ok, 1)

            for k in range(4):
                first_lo(k)
            dv.wait_ge(tzr_in, 16)
            section(0)
            V.tensor_copy(tmp[0:DEPTH * 8, 0:127], tmp[0:DEPTH * 8, 127:128].to_broadcast([DEPTH * 8, 127])).then_inc(tzr_ok, 1)
            for k in range(4, KT):
                first_lo(k)
            dv.wait_ge(const_in, 64)
            V_(V.tensor_scalar(scale_s[:], scale_s[:], 0.5, None, ALU.mult))
            total = count[1]

            for it in range(STEPS):
                pc, nb = C_PAIRS * it, 16 * it
                per_c = 23 + (2 if it else 0) - half(it)
                with dv.Fori(0, C_PAIRS) as p:
                    section(p * per_c + total)
                    V.tensor_copy(coef1[:], coef[:, ds(p, 1), :].rearrange("p o n -> p (o n)"))
                    V.tensor_copy(inv1[:], inv16[:, ds(p, 1), :].rearrange("p o n -> p (o n)"))
                    V.tensor_copy(scale1[:], scale_s[:, layer(it), ds(p, 1)])
                    if half(it):
                        V_(V.tensor_copy(av[:, 0:16], a_tail[:, ds(p, 1), :].rearrange("p o n -> p (o n)")))
                    else:
                        V_(V.memset(av[:, 0:16], 0.0))
                    dv.wait_ge(av_ok, p + (pc + 1))
                    N = 16 + HALF
                    V_(V.tensor_tensor(s0[:, 1:N], av[:, 1:N], av[:, 0:N - 1], ALU.add))
                    V_(V.scalar_tensor_tensor(s1[:, 3:N], s0[:, 1:N - 2], coef1[:, 0:1], s0[:, 3:N], ALU.mult, ALU.add))
                    V_(V.scalar_tensor_tensor(s0[:, 7:N], s1[:, 3:N - 4], coef1[:, 1:2], s1[:, 7:N], ALU.mult, ALU.add))
                    V_(V.scalar_tensor_tensor(s1[:, 15:N], s0[:, 7:N - 8], coef1[:, 2:3], s0[:, 15:N], ALU.mult, ALU.add))
                    if half(it):
                        V.scalar_tensor_tensor(s0[:, 16:N], s1[:, 16:N], coef1[:, 3:4], av[:, 16:N], ALU.mult, ALU.subtract
                                               ).then_inc(ay_ok, 1)
                    else:
                        V.tensor_copy(a_tail[:, ds(p, 1), :].rearrange("p o n -> p (o n)"), av[:, HALF:N])
                        V_(V.tensor_tensor(s1[:, 16:32], s1[:, 16:32], inv1[:], ALU.mult))
                        V.tensor_tensor(s0[:, 16:32], s1[:, 16:32], av[:, 16:32], ALU.subtract)
                        V.scalar_tensor_tensor(s0[:, 32:N], s1[:, 32:N], coef1[:, 3:4], av[:, 32:N], ALU.mult, ALU.subtract
                                               ).then_inc(ay_ok, 1)
                    dv.wait_ge(gwh_ok, p + (pc + 1))
                    lo(gwl[:], gw[:], gwh[:]).then_inc(gwl_ok, 1)
                    dv.wait_ge(ayh_ok, p + (pc + 1))
                    lo(ya_l, s0[:, 16:N], ya_h).then_inc(ayl_ok, 1)
                    dv.wait_ge(vh_ok, p + ((C_PAIRS + 1) * it + 1))
                    lo(cv_l[:, 4:8, :], acc[1][:, :].rearrange("p (b c) -> p b c", c=P), cv_h[:, 4:8, :])\
                        .then_inc(v_ok, 1)
                    dv.wait_ge(bias_in, p * 16 + (16 * pc + 16))
                    for h in range(2):
                        cs = slice(NEAR * h, NEAR * (h + 1))
                        last = V.tensor_scalar(brope[:, 1, cs], brope[:, 0, cs], brope[:, 0, NEAR * h:NEAR * h + 1], None, ALU.subtract)
                    V_(last)
                    for h in range(2):
                        last = V.memset(brope[0:HD, 1, NEAR * (h + 1) - CHUNK:NEAR * (h + 1)], NEG_INF)
                    last.then_inc(bias_ok, 1)
                    dv.wait_ge(kh_ok, p + (pc + 1))
                    lo(ck_l[:, HALF:2 * HALF], acc[0][:, :], ck_h[:, HALF:2 * HALF]).then_inc(k_ok, 1)
                    if it:
                        layer_norm(it - 1, p)
                    dv.wait_ge(qh_ok, p + ((C_PAIRS + B_TILES + 1) * it + 1))
                    V.scalar_tensor_tensor(cq_l, acc[1][:, :], SCALE, cq_h.bitcast(F32), ALU.mult, ALU.subtract).then_inc(q_ok, 1)
                    dv.wait_ge(bias_ok, p + (pc + 2))
                    c_max(it, p, 0)
                    c_normalise(it, p, 0)
                    c_lo(it, p, 0)
                    c_max(it, p, 1)
                    c_normalise(it, p, 1)
                    c_lo(it, p, 1)
                    gate_ready(p * 2 + ((2 * C_PAIRS + B_TILES) * it + 1), 0)
                    c_max(it, p, 2)
                    c_normalise(it, p, 2)
                    c_lo(it, p, 2)
                    dv.wait_ge(a_full, p + (pc + 1))
                    V.scalar_tensor_tensor(tmp[:], acc[0][:, :], scale1[:], gate[:], ALU.mult, ALU.mult).then_inc(prod_ok, 1)
                    mix_lo(p * 2 + (nb + 1), p + MIX_A)
                    c_max(it, p, 3)
                    c_normalise(it, p, 3)
                    c_lo(it, p, 3)
                    gate_ready(p * 2 + ((2 * C_PAIRS + B_TILES) * it + 2), 1)
                    dv.wait_ge(c_pv, p * 4 + (4 * pc + 4))
                    attention_product(p * 2 + (MIXES * it + 2))
                    mix_lo(p * 2 + (nb + 2), p + MIX_C)
                    if not half(it):
                        dv.wait_ge(hist_out, p * 32 + (32 * C_PAIRS * layer(it) + 32))
                    assert count[1] == per_c, (it, count[1])
                total += C_PAIRS * per_c

                section(total)
                dv.wait_ge(rope_raw, ROTS * it + 1)
                if half(it):
                    for t in (bkh, bkl):
                        V.tensor_copy(t[:, 0:P], t[:, HALF:HALF + P])
                    V.tensor_copy(bvh[:, 0, :], bvh[:, QT, :])
                    V.tensor_copy(bvl[:, 0, :], bvl[:, QT, :]).then_inc(hist_mv, 1)
                V.memset(prob[:, :, 0:512].rearrange("p s (t c) -> p s t c", t=2)[:, :, :, 0:HD], 0.0)
                dv.wait_ge(rope_in, 32 * (it + 1))
                rotate(ROTS * it + 1)
                if half(it):
                    dv.wait_ge(hist_mv, layer(it) + 1)
                rotated(bkl[:, P:], bkh[:, P:], QS * it + C_PAIRS + 1)
                dv.wait_ge(vh_ok, (C_PAIRS + 1) * (it + 1))
                lo(bvl[:, 1:, :], acc[1][:, :].rearrange("p (b c) -> p b c", c=P), bvh[:, 1:, :]).then_inc(v_ok, 1)
                rotate(ROTS * it + 2)
                rotated(bql[:], bqh[:], QS * it + C_PAIRS + 2)
                total += count[1]

                per_b = 2 + 2 * 4 + 2 * 4 + 2
                with dv.Fori(1, B_TILES) as i:
                    section((i - 1) * per_b + total)
                    sinks_of(it, i - 1)
                    for u in (0, 1):
                        b_max(it, i - 1, u)
                    for u in (0, 1):
                        b_normalise(it, i - 1, u)
                    for u in (2, 3):
                        b_max(it, i - 1, u)
                    for u in (0, 1):
                        b_lo(it, i - 1, u)
                    for u in (2, 3):
                        b_normalise(it, i - 1, u)
                    rotate(i + (ROTS * it + 2))
                    for u in (2, 3):
                        b_lo(it, i - 1, u)
                    rotated(bql[:], bqh[:], i + (QS * it + C_PAIRS + 2))
                    gate_ready(i + (MIXES * it + 2 * C_PAIRS), 1)
                    dv.wait_ge(b_pv, i * 2 + 2 * B_TILES * it)
                    attention_product(i + (MIXES * it + 2 * C_PAIRS))
                    mix_lo(i + (nb + 2 * C_PAIRS), i + (MIX_B - 1))
                    assert count[1] == per_b, count[1]
                total += (B_TILES - 1) * per_b

                section(total)
                last_tile = B_TILES - 1
                sinks_of(it, last_tile)
                for u in (0, 1):
                    b_max(it, last_tile, u)
                for u in (0, 1):
                    b_normalise(it, last_tile, u)
                for u in (2, 3):
                    b_max(it, last_tile, u)
                for u in (0, 1):
                    b_lo(it, last_tile, u)
                for u in (2, 3):
                    b_normalise(it, last_tile, u)
                for u in (2, 3):
                    b_lo(it, last_tile, u)
                gate_ready(MIXES * (it + 1), 1)
                dv.wait_ge(b_pv, 2 * B_TILES * (it + 1))
                attention_product(MIXES * (it + 1))
                mix_lo(nb + 16, MIX_B + last_tile)
                total += count[1]

                def summed(t, c):
                    return res[:, t, :] if it + 1 < STEPS else sums[:, ds(4 * t + c, 1), :].rearrange("p o n -> p (o n)")

                with dv.Fori(0, 2) as m:
                    for n in range(2):
                        if n == 0 and it + 1 < STEPS:
                            for gg in range(8):
                                if layer(it + 1) == 0:
                                    dv.wait_ge(xh_ok, m * 8 + (16 * (it + 1) + gg + 1))
                                    o, hi = (v[:, ds(m * 8 + gg, 1), :].rearrange("p o n -> p (o n)") for v in (xl, xh))
                                    lo(o, prob[:, gg % 2, 0:512], hi).then_inc(xl_ok, 1)
                                else:
                                    x_lo(m * 8 + (16 * (it + 1) + gg), gg, odd_banks[gg % 4], 2 * m + gg // 4)
                        c = 2 * m + n
                        dv.wait_ge(res_in, c * 16 + (64 * it + 16))
                        for t in range(QT):
                            if t < QT - 1:
                                dv.wait_ge(out_full, c * 3 + (12 * it + t + 1))
                            else:
                                dv.wait_ge(w_used, unit(it, c * U_N + (O0 + U_N)) + RING)
                            V.scalar_tensor_tensor(summed(t, c), res[:, t, :], ALPHA, (even_banks, odd_banks)[n][t],
                                                   ALU.mult, ALU.add).then_inc(out_free, 1)
                        dv.wait_ge(out_free, c * 4 + (16 * it + 4 + 8))
                        for t in range(QT):
                            V.bn_stats(stats[:, t, ds(c, 1), :].rearrange("p o s -> p (o s)"), summed(t, c)).then_inc(res_ok, 1)
                section(total)
                dv.wait_ge(res_ok, 16 * (it + 1))
                for t in range(QT):
                    last = V.bn_aggr(mv[:, t, :], stats[:, t, :, :].rearrange("p n s -> p (n s)"))
                V_(last)
                V.tensor_scalar(veps[:], mv[:, :, 1], LN_EPS, None, ALU.add).then_inc(ln_var, 1)
                dv.wait_ge(ln_sqrt, it + 1)
                V_(V.reciprocal(sq2[:], sq[:]))
                V_(V.tensor_tensor(sq2[:], sq2[:], veps[:], ALU.mult))
                V_(V.tensor_tensor(sq2[:], sq2[:], sq[:], ALU.add))
                V_(V.reciprocal(rstd[:], sq2[:]))
                V_(V.tensor_scalar(rstd[:], rstd[:], 2.0, None, ALU.mult))
                total += count[1]

            section(total)
            V.scalar_tensor_tensor(shift[:], mv[:, :, 0], -1.0, rstd[:], ALU.mult, ALU.mult).then_inc(ln_rstd, 1)
            dv.wait_ge(ln_in, 48 * 4 * (STEPS - 1) + 32)
            for t in range(QT):
                cols = last_rows(t, 0, LN_V)
                V_(V.scalar_tensor_tensor(cols, cols, mv[:, t, 0:1], gain_all[:, 0:LN_V], ALU.subtract, ALU.mult))
                V.scalar_tensor_tensor(cols, cols, rstd[:, t:t + 1], bias_all[:, 0:LN_V], ALU.mult, ALU.add
                                       ).then_inc(ln_end_v, 1)


def laid_out(x, w_in, a_group_w, a_scale, b_sinks, c_rel_bias, w_out, ln_gain, ln_bias):
    cols = np.split(np.arange(w_in.shape[2]),
                    np.cumsum([A_WIDTH, A_WIDTH, B_WIDTH, P, P, B_WIDTH, C_WIDTH, C_WIDTH, C_WIDTH])) 
    a_v, a_g, b_q, b_k, b_v, b_g, c_q, c_k, c_v, c_g = cols

    def tile(v, i):
        return v[i * P:(i + 1) * P]

    def heads(v, i):
        return np.concatenate([v[i * HD:(i + 1) * HD], v[(i + B_TILES) * HD:(i + B_TILES + 1) * HD]])

    order = []
    for p in range(C_PAIRS):
        order += [tile(v, p) for v in (a_v, c_v, c_k, c_q, a_g, c_g)]
    order += [b_k, b_v]
    order += [heads(b_q, 0)]
    for i in range(1, B_TILES):
        order += [heads(b_q, i), heads(b_g, i - 1)]
    order += [heads(b_g, B_TILES - 1)]
    order = np.concatenate(order)
    w1 = w_in[:, :, order].reshape(DEPTH, 4, 4, P, len(order) // P, P)
    w1 = w1.transpose(0, 4, 1, 3, 2, 5).reshape(DEPTH, O0, P, UNIT)
    chan = np.arange(D)
    mix = [tile(chan, g) for g in range(A_GROUPS)] + [heads(A_WIDTH + np.arange(B_WIDTH), i) for i in range(B_TILES)] \
        + [tile(A_WIDTH + B_WIDTH + np.arange(C_WIDTH), p) for p in range(C_PAIRS)]
    w2 = w_out[:, np.concatenate([mix[k] for k in MIX_ORDER]), :].reshape(DEPTH, KT, P, 4, UNIT)
    w2 = w2.transpose(0, 3, 1, 2, 4).reshape(DEPTH, 4 * U_N, P, UNIT)
    wall = np.concatenate([w1, w2], axis=1)

    t = np.arange(SEQ, dtype=np.float32)
    j = np.arange(ROPE_DIM // 2, dtype=np.float32)
    inv = (np.float32(ROPE_THETA) ** (-j / np.float32(ROPE_DIM // 2))).astype(np.float32)
    ang = (inv[:, None] * t[None, :]).astype(np.float32)
    cos = np.ones((2, HD, SEQ), np.float32)
    sin = np.zeros((2, HD, SEQ), np.float32)
    cos[:, 0:8] = cos[:, 8:16] = np.cos(ang)
    sin[:, 0:8], sin[:, 8:16] = -np.sin(ang), np.sin(ang)
    by_half = [np.ascontiguousarray(a.reshape(P, 2, HALF).transpose(1, 0, 2)) for a in (cos, sin)]
    coef = np.array([[w >= 4, w >= 8, w >= 16, 1.0 / w] for w in WINDOWS], np.float32)
    first = np.array([1.0 / np.minimum(np.arange(16) + 1.0, w) for w in WINDOWS], np.float32)
    return {
        "x": x[0],
        "x_t": x[0].T,
        "wall": wall,
        "a_gw": a_group_w,
        "a_scale": a_scale.reshape(DEPTH, A_GROUPS, P).transpose(2, 0, 1),
        "sinks": b_sinks.reshape(DEPTH, 2, B_TILES).transpose(0, 2, 1).reshape(1, -1),
        "rel_rev": c_rel_bias.reshape(DEPTH * 8, 2 * MAX_REL + 1)[:, ::-1],
        "ln_gain": ln_gain.reshape(DEPTH, 4, 512),
        "ln_bias": ln_bias.reshape(DEPTH, 4, 512),
        "rope_cos": by_half[0],
        "rope_sin": by_half[1],
        "pool_coef": np.broadcast_to(coef, (P,) + coef.shape),
        "pool_inv": np.broadcast_to(first, (P,) + first.shape),
    }


def kernel(x, w_in, a_group_w, a_scale, b_sinks, c_rel_bias, w_out, ln_gain, ln_bias):
    import concourse.bacc as bacc
    from concourse.bass_utils import run_bass_kernel_spmd

    given = laid_out(*(np.asarray(a) for a in (x, w_in, a_group_w, a_scale, b_sinks, c_rel_bias, w_out,
                                               ln_gain, ln_bias)))
    nc = bacc.Bacc("TRN2", target_bir_lowering=False, num_devices=1)
    arrays, args = {}, {}
    for name, a in given.items():
        a = np.ascontiguousarray(a)
        arrays[f"in_{name}"] = a
        args[name] = nc.dram_tensor(f"in_{name}", a.shape, mybir.dt.from_np(a.dtype), kind="ExternalInput").ap()
    out = nc.dram_tensor("out", (SEQ, D), F32, kind="ExternalOutput").ap()
    build(nc, out=out, **args)
    r = run_bass_kernel_spmd(nc, [arrays], core_ids=[0])
    return r.results[0]["out"].reshape(1, SEQ, D)
```

```python
from contextlib import ExitStack

import numpy as np

import concourse.bass as bass
from concourse import mybir

F32 = mybir.dt.float32
F32R = mybir.dt.float32r
ALU = mybir.AluOpType
ACT = mybir.ActivationFunctionType
AX = mybir.AxisListType.X
ds = bass.ds

P = 128
D = 2048
SEQ = 1024
DEPTH = 2
HALF = 512
STEPS = DEPTH * (SEQ // HALF)
KT = D // P
HD = 64
A_WIDTH = D // 4
A_GROUPS = 4
WINDOWS = (2, 4, 8, 16)
B_WIDTH = D // 2
B_HEADS = B_WIDTH // HD
B_TILES = B_HEADS // 2
C_WIDTH = D - A_WIDTH - B_WIDTH
C_PAIRS = C_WIDTH // P
CHUNK = 64
C_KEYS = 640
NEAR = 256
MAX_REL = 128
ROPE_DIM = HD // 4
ROPE_THETA = 500000.0
SCALE = float(HD) ** -0.5
ALPHA = (2.0 * DEPTH) ** 0.25
LN_EPS = 1e-5
NEG_INF = -1e30
QT = HALF // P

UNIT = 512
RING = 4
FIRST = 7
AHEAD = 3
U_C = 24
U_KV = 8
U_B = 8
U_N = 16
KV0 = C_PAIRS * U_C
B0 = KV0 + U_KV
O0 = B0 + B_TILES * U_B
U_STEP = O0 + 4 * U_N

MIX_A, MIX_B, MIX_C = 0, A_GROUPS, A_GROUPS + B_TILES
MIX_ORDER = list(range(MIX_B)) + list(range(MIX_C, KT)) + list(range(MIX_B, MIX_C))

MIXES = 2 * C_PAIRS + B_TILES
ROTS = 1 + B_TILES
QS = C_PAIRS + ROTS
TZ = 384

X_AT = (1, 3, 5, 7, 9, 11, 13, 14)
X_LOAD = (6, 6, 9, 11, 13, 15, 17, 19)

LN_V = 1408

SWAP = [i + 8 if i < 8 else i - 8 if i < 16 else i for i in range(32)]


def build(nc, x, x_t, wall, a_gw, a_scale, sinks, rel_rev, ln_gain, ln_bias, rope_cos, rope_sin,
          pool_coef, pool_inv, out):
    with ExitStack() as ctx:
        def sb(name, shape, dt=F32):
            return ctx.enter_context(nc.sbuf_tensor(name, shape, dt))

        def next_address():
            return -(-nc.sbuf_base // 32) * 32

        def psum(name, shape):
            return ctx.enter_context(nc.psum_tensor(name, shape, F32))

        def sem(name):
            return ctx.enter_context(nc.semaphore(name))

        x1 = nc.dram_tensor("x1_scratch", (SEQ, D), F32, kind="Internal").ap()
        res_d = nc.dram_tensor("res_scratch", (4, P, QT, 512), F32, kind="Internal").ap()
        hist_d = nc.dram_tensor("hist_scratch", (C_PAIRS, P, 5, 512), F32, kind="Internal").ap()
        rel_d = nc.dram_tensor("bias_row_scratch", (DEPTH * 8, TZ), F32, kind="Internal").ap()
        tz_d = nc.dram_tensor("bias_rows_scratch", (DEPTH * 8, P * TZ), F32, kind="Internal").ap()

        x_at = next_address()
        xh = sb("xh", [P, KT, HALF], F32R)
        xl = sb("xl", [P, KT, HALF], F32R)
        mixh = sb("mixh", [P, KT, HALF], F32R)
        mixl = sb("mixl", [P, KT, HALF], F32R)
        raw = sb("raw", [P, RING, UNIT])
        wh = sb("wh", [P, RING, UNIT], F32R)
        wl = sb("wl", [P, RING, UNIT], F32R)
        bk = [sb("bk0", [P, HD + HALF], F32R), sb("bk1", [P, HD + HALF], F32R)]
        bkl = sb("bkl", [P, HD + HALF], F32R)
        bvh = sb("bvh", [P, 6, P], F32R)
        bvl = sb("bvl", [P, 6, P], F32R)
        bq_at = next_address()
        bq = [sb("bq0", [P, HALF], F32R), sb("bq1", [P, HALF], F32R)]
        pth = sb("pth", [P, 5, 2, P], F32R)
        ptl = sb("ptl", [P, 5, 2, P], F32R)
        prob = sb("prob", [P, 2, C_KEYS])
        res = sb("res", [P, QT, 512])
        gate = sb("gate", [P, HALF])
        tmp = sb("tmp", [P, HALF])
        av = sb("av", [P, 16 + HALF])
        s0 = sb("s0", [P, 16 + HALF])
        s1 = sb("s1", [P, 16 + HALF])
        brope = sb("brope", [P, 2, 512])
        ident = sb("ident", [P, P])
        a_tail = sb("a_tail", [P, A_GROUPS, 16])
        coef = sb("coef", [P, A_GROUPS, 4])
        inv16 = sb("inv16", [P, A_GROUPS, 16])
        coef1 = sb("coef1", [P, 4])
        inv1 = sb("inv1", [P, 16])
        scale_s = sb("scale_s", [P, DEPTH, A_GROUPS])
        scale1 = sb("scale1", [P, 1])
        sink_s = sb("sink_s", [P, DEPTH, B_TILES, 2])
        sink1 = sb("sink1", [P, 2, 2])
        nmax = sb("nmax", [P, 4, 2])
        mx = sb("mx", [P, 4, 2])
        psums = sb("psums", [P, 4, 2])
        esink = sb("esink", [P, 4, 2])
        rinv = sb("rinv", [P, 4, 2])
        mv = sb("mv", [P, QT, 2])
        veps = sb("veps", [P, QT])
        sq = sb("sq", [P, QT])
        sq2 = sb("sq2", [P, QT])
        rstd = sb("rstd", [P, QT])
        shift = sb("shift", [P, QT])

        ck = [m[:, MIX_B:MIX_B + 2, :].rearrange("p a n -> p (a n)") for m in (mixh, mixl)]
        ck_l = mixh[:, MIX_B + 4:MIX_B + 6, :].rearrange("p a n -> p (a n)")
        cv_h, cv_l = (m[:, MIX_B + 2:MIX_B + 4, :].rearrange("p a (b n) -> p (a b) n", n=P) for m in (mixh, mixl))
        cq = [m[:, MIX_B + 6, :] for m in (mixh, mixl)]
        ya_h, ya_l = (m[:, MIX_B + 7, :] for m in (mixh, mixl))
        gw = nc.alloc_sbuf_tensor_at("gw", [P, P], F32, offset=bq_at)
        gwh, gwl = (bq[1][:, P * n:P * (n + 1)] for n in range(2))
        stats = av[:, 0:QT * 4 * 6].rearrange("p (t c s) -> p t c s", t=QT, c=4)
        ROWS = [slice(HD * h, HD * (h + 1)) for h in range(2)]

        x_in = nc.alloc_sbuf_tensor_at("first_x", [P, KT, HALF], F32, offset=x_at + 2 * 4 * KT * HALF)
        sums = nc.alloc_sbuf_tensor_at("last_sums", [P, KT, HALF], F32, offset=x_at)
        gain_bias = nc.alloc_sbuf_tensor_at("last_gain_bias", [P, 2, D], F32, offset=x_at + 4 * KT * HALF)
        gain_all, bias_all = gain_bias[:, 0, :], gain_bias[:, 1, :]

        acc = [psum("acc0", [P, 512]), psum("acc1", [P, 512])]
        sc = [psum("sc0", [P, 1024]), psum("sc1", [P, 1024])]
        pv = psum("pv", [P, 1024])
        pv5 = pv[:, :].rearrange("p (t i h q) -> p i t h q", t=2, i=2, h=2)
        v_bank = sc[0][:, 0:512]
        v_blocks = prob[:, :, :].rearrange("p s c -> p (s c)")[:, 0:6 * P]
        vn_bank = sc[1][:, 0:6 * P].rearrange("p (b c) -> p b c", c=P)
        even_banks = [acc[0][:, :], sc[0][:, 0:512], sc[0][:, 512:1024], acc[1][:, :]]
        odd_banks = [sc[1][:, 0:512], sc[1][:, 512:1024], pv[:, 0:512], pv[:, 512:1024]]

        w_raw = [sem(f"w_raw{i}") for i in range(RING)]
        w_hi = sem("w_hi")
        w_lo = sem("w_lo")
        w_used = sem("w_used")
        vn_full = sem("vn_full")
        a_full = sem("a_full")
        ident_ok = sem("ident_ok")
        const_in = sem("const_in")
        xin = [sem("xin0"), sem("xin1")]
        x0_in = [sem(f"x0_in{k}") for k in range(KT)]
        tr_full = sem("tr_full")
        xh_ok = sem("xh_ok")
        xl_ok = sem("xl_ok")
        av_ok = sem("av_ok")
        ay_ok = sem("ay_ok")
        ayh_ok = sem("ayh_ok")
        ayl_ok = sem("ayl_ok")
        gw_in = sem("gw_in")
        gwh_ok = sem("gwh_ok")
        gwl_ok = sem("gwl_ok")
        vt_ok = sem("vt_ok")
        vh_ok = sem("vh_ok")
        v_ok = sem("v_ok")
        kh_ok = sem("kh_ok")
        k_ok = sem("k_ok")
        qh_ok = sem("qh_ok")
        q_ok = sem("q_ok")
        bq_ok = sem("bq_ok")
        rope_raw = sem("rope_raw")
        rope_ok = sem("rope_ok")
        hist_out = sem("hist_out")
        hist_in = sem("hist_in")
        bias_in = sem("bias_in")
        bias_ok = sem("bias_ok")
        rope_in = sem("rope_in")
        cs_full = sem("cs_full")
        cs_max = sem("cs_max")
        cs_exp = sem("cs_exp")
        cs_prob = sem("cs_prob")
        ct_full = sem("ct_full")
        ct_hi = sem("ct_hi")
        ct_lo = sem("ct_lo")
        c_pv = sem("c_pv")
        bs_full = sem("bs_full")
        bs_max = sem("bs_max")
        bs_exp = sem("bs_exp")
        bs_prob = sem("bs_prob")
        bt_full = sem("bt_full")
        bt_hi = sem("bt_hi")
        bt_lo = sem("bt_lo")
        b_pv = sem("b_pv")
        tanh_ok = sem("tanh_ok")
        gate_ok = sem("gate_ok")
        prod_ok = sem("prod_ok")
        mixh_ok = sem("mixh_ok")
        mixl_ok = sem("mixl_ok")
        out_full = sem("out_full")
        out_free = sem("out_free")
        res_in = sem("res_in")
        res_out = sem("res_out")
        res_ok = sem("res_ok")
        ln_var = sem("ln_var")
        ln_sqrt = sem("ln_sqrt")
        ln_in = sem("ln_in")
        ln_rstd = sem("ln_rstd")
        ln_unit = sem("ln_unit")
        ln_end_v = sem("ln_end_v")
        ln_end_p = sem("ln_end_p")
        pool_step = sem("pool_step")
        ln_ok = sem("ln_ok")
        ln_out = sem("ln_out")
        rel_in = sem("rel_in")
        rel_ok = sem("rel_ok")
        rel_out = sem("rel_out")
        tz_out = sem("tz_out")
        hist_mv = sem("hist_mv")
        sp_step = sem("sp_step")
        dve = sem("dve_step")


        def layer(it):
            return it // 2

        def half(it):
            return it % 2

        def x_rows(it):
            src = x if layer(it) == 0 else x1
            return src[half(it) * HALF:(half(it) + 1) * HALF, :]

        def transposed(it, n):
            return n + (16 * (it - 2) + 2)

        def x_taken(it, n):
            return (xl_ok, n + 16 * (it + 1)) if layer(it + 1) == 0 else (tr_full, transposed(it + 1, n))

        def last_rows(t, a, b):
            return sums[:, 4 * t:4 * t + 4, :].rearrange("p c n -> p (c n)")[:, a:b]

        def c_seen(it, j):
            return (0, 512 - C_KEYS // 2) if half(it) else (512 - P * j, 0)

        def unit(it, r):
            return r + it * U_STEP

        block = ctx.enter_context(nc.Block())

        @block.sync
        def _(sp):
            sp.sem_inc(res_out, 16)

            def wait_alone(semaphore, value):
                sp.wait_ge(semaphore, value)
                sp.sem_inc(sp_step, 1)

            def load_unit(it, r, slot):
                sp.wait_ge(w_lo, unit(it, r) + 1)
                sp.dma_start(raw[:, slot, :], wall[layer(it), ds(r, 1)].rearrange("o p n -> (o p) n")
                             ).then_inc(w_raw[slot], 16)

            def load_ln(it, n):
                sp.wait_ge(res_out, 64 * (it + 1) + 16)
                sp.dma_start(res[:], res_d[ds(n, 1)].rearrange("o p t n -> (o p) t n")).then_inc(ln_in, 16)
                for slot, v in enumerate((ln_gain, ln_bias)):
                    sp.dma_start(prob[:, slot, 0:512], v[layer(it), ds(n, 1), :].to_broadcast([P, 512])
                                 ).then_inc(ln_in, 16)

            def store_ln(it, n):
                wait_alone(ln_ok, n + (4 * it + 1))
                dst = (x1 if layer(it) == 0 else out)[half(it) * HALF:(half(it) + 1) * HALF, :]
                sp.dma_start(dst.rearrange("(t p) (c n) -> c p t n", p=P, n=512)[ds(n, 1)]
                             .rearrange("o p t n -> (o p) t n"), res[:]).then_inc(ln_out, 16)
                wait_alone(ln_out, n * 16 + (64 * it + 16))

            for q in range(4):
                load_unit(0, q, q)
                for k in range(4 * q, 4 * q + 4):
                    sp.dma_start(x_in[:, k, :], x_t[k * P:(k + 1) * P, 0:HALF]).then_inc(x0_in[k], 16)
                if q == 0:
                    sp.dma_start(tmp[0:DEPTH * 8, 127:127 + 257], rel_rev).then_inc(rel_in, 16)
                    sp.dma_start(coef[:], pool_coef).then_inc(const_in, 16)
                    sp.dma_start(inv16[:], pool_inv).then_inc(const_in, 16)
                    sp.dma_start(scale_s[:], a_scale).then_inc(const_in, 16)
                    sp.dma_start(sink_s[:].rearrange("p a b c -> p (a b c)"),
                                 sinks.to_broadcast([P, DEPTH * B_HEADS])).then_inc(const_in, 16)
            for r in range(RING, FIRST):
                load_unit(0, r, r % RING)
            sp.wait_ge(rel_ok, 1)
            sp.dma_start(rel_d, tmp[0:DEPTH * 8, 0:TZ]).then_inc(rel_out, 16)

            for it in range(STEPS):
                with sp.Fori(0, C_PAIRS) as p:
                    for s in range(U_C):
                        if s == (4 if it else 0):
                            sp.wait_ge(gwl_ok, p + (C_PAIRS * it + 1))
                            sp.dma_start(gw[:], a_gw[layer(it), ds(p, 1)].rearrange("o c d -> (o c) d")
                                         ).then_inc(gw_in, 16)
                        if s == 9 and half(it):
                            sp.wait_ge(w_used, unit(it, p * U_C) + (2 + RING))
                            for m, a, b in ((mixh, 0, 3), (mixl, 3, 5)):
                                sp.dma_start(m[:, MIX_B:MIX_B + 2 * (b - a) - 1:2, :].bitcast(F32),
                                             hist_d[ds(p, 1), :, a:b, :].rearrange("o p a n -> (o p) a n")
                                             ).then_inc(hist_in, 16)
                        if s == 2 and it == 0:
                            sp.wait_ge(rel_out, 16)
                            for first in range(0, DEPTH * 8, 8):
                                heads = ds(2 * p + first, 2)
                                sp.dma_start(tz_d[heads].rearrange("h (q c) -> h q c", c=TZ),
                                             rel_d[heads].rearrange("h (o c) -> h o c", o=1).to_broadcast([2, P, TZ])
                                             ).then_inc(tz_out, 16)
                        if s == (10 if it else 5):
                            sp.wait_ge(bias_ok, p + (C_PAIRS * it + 1))
                            if it:
                                sp.wait_ge(rope_ok, (B_TILES + 1) * it)
                            else:
                                sp.wait_ge(tz_out, p * (16 * DEPTH) + 16 * DEPTH)
                            sp.dma_start(brope[:, 0, :].rearrange("p (h n) -> p h n", h=2),
                                         tz_d[ds(2 * p + 8 * layer(it), 2), 127:127 + P * (TZ - 1)]
                                         .rearrange("h (q c) -> q h c", c=TZ - 1)[:, :, 0:NEAR]).then_inc(bias_in, 16)
                        if s == 12 and it:
                            sp.wait_ge(w_used, unit(it, p * U_C) + (1 + RING))
                            load_ln(it - 1, p)
                        if s == 22 and it:
                            store_ln(it - 1, p)
                        if s == (23 if it else 15) and not half(it):
                            wait_alone(k_ok, p + (C_PAIRS * it + 1))
                            wait_alone(v_ok, p + ((C_PAIRS + 1) * it + 1))
                            for m, a, b in ((mixh, 0, 3), (mixl, 3, 5)):
                                sp.dma_start(hist_d[ds(p, 1), :, a:b, :].rearrange("o p a n -> (o p) a n"),
                                             m[:, MIX_B + 1:MIX_B + 2 * (b - a):2, :].bitcast(F32)).then_inc(hist_out, 16)
                        if it == 0:
                            load_unit(it, p * U_C + (s + FIRST), (s + FIRST) % RING)
                        else:
                            load_unit(it, p * U_C + s, s % RING)
                for s in range(U_KV):
                    if it or s >= FIRST:
                        load_unit(it, KV0 + s, s % RING)
                sp.wait_ge(cs_max, 8 * C_PAIRS * (it + 1))
                sp.dma_start(brope[:, 0, :], rope_cos[half(it)]).then_inc(rope_in, 16)
                sp.dma_start(brope[:, 1, :], rope_sin[half(it)]).then_inc(rope_in, 16)
                with sp.Fori(0, B_TILES) as i:
                    for s in range(U_B):
                        load_unit(it, i * U_B + (B0 + s), s % RING)
                with sp.Fori(0, 2) as m:
                    for s in range(2 * U_N):
                        load_unit(it, m * (2 * U_N) + (O0 + s), s % RING)
                        for gg in range(8):
                            if it + 1 == STEPS or s != X_LOAD[gg]:
                                continue
                            sp.wait_ge(bt_full, 4 * B_TILES * (it + 1))
                            sp.wait_ge(*x_taken(it, m * 8 + gg - 1))
                            if layer(it + 1) == 0:
                                src = x_t.rearrange("(k p) n -> k p n", p=P)[ds(m * 8 + gg, 1), :, HALF:2 * HALF]
                            else:
                                src = x_rows(it + 1).rearrange("(t p) (k n) -> t k p n", p=P, n=512)
                                src = src[ds(2 * m + gg // 4, 1), gg % 4]
                            sp.dma_start(prob[:, gg % 2, 0:512], src.rearrange("o p n -> (o p) n")
                                         ).then_inc(xin[gg % 2], 16)
                        if s in (14, 30):
                            n = 2 * m + s // 16
                            if it + 1 < STEPS:
                                sp.wait_ge(res_out, n * 16 + (64 * it + 16))
                            else:
                                sp.wait_ge(out_free, n * 4 + (16 * it + 8))
                            src = x_rows(it).rearrange("(t p) (c n) -> c p t n", p=P, n=512)
                            sp.dma_start(res[:], src[ds(n, 1)].rearrange("o p t n -> (o p) t n")).then_inc(res_in, 16)
            for r in range(AHEAD):
                sp.wait_ge(w_lo, STEPS * U_STEP + r + 1)
                sp.dma_start(raw[:, r, :], wall[DEPTH - 1, 0]).then_inc(w_raw[r], 16)
            sp.wait_ge(w_used, unit(STEPS - 1, O0) + RING)
            for o, v in ((gain_all, ln_gain), (bias_all, ln_bias)):
                sp.dma_start(o, v[DEPTH - 1].rearrange("c n -> (c n)").rearrange("(o n) -> o n", o=1)
                             .to_broadcast([P, D])).then_inc(ln_in, 16)
            rows = out[HALF:2 * HALF, :].rearrange("(t p) n -> t p n", p=P)
            for t in range(QT):
                sp.wait_ge(ln_end_v, t + 1)
                sp.dma_start(rows[t, :, 0:LN_V], last_rows(t, 0, LN_V)).then_inc(ln_out, 16)
                sp.wait_ge(ln_end_p, t + 1)
                sp.dma_start(rows[t, :, LN_V:D], last_rows(t, LN_V, D)).then_inc(ln_out, 16)
            sp.wait_ge(ln_out, 16 * 4 * (STEPS - 1) + 32 * QT)

        @block.tensor
        def _(pe):
            def mm(o, lhsT, rhs, start, stop):
                return nc.tensor.matmul(o, lhsT, rhs, start=start, stop=stop)

            pe.sem_inc(w_used, RING)
            pe.sem_inc(tr_full, 2)

            def project(it, r, q, bank, slot, part=range(4), x_first=False):
                if part[0] == 0:
                    pe.wait_ge(w_lo, unit(it, r) + (1 + RING))
                for kk in part:
                    k = 4 * q + kk
                    if x_first:
                        pe.wait_ge(xl_ok, k + 1)
                    hi, lo = (w[:, slot, kk * P:(kk + 1) * P] for w in (wh, wl))
                    mm(bank, hi, xh[:, k, :], k == 0, False)
                    mm(bank, hi, xl[:, k, :], False, False)
                    last = mm(bank, lo, xh[:, k, :], False, k == KT - 1)
                if kk == 3:
                    last.then_inc(w_used, 1)

            def transpose_x(g, bank):
                for b in range(4):
                    last = nc.tensor.transpose(bank[:, b * P:(b + 1) * P], prob[:, g % 2, b * P:(b + 1) * P], ident[:])
                last.then_inc(tr_full, 1)

            def transpose_values(bank):
                for b in range(QT):
                    last = nc.tensor.transpose(bank[:, b * P:(b + 1) * P], tmp[:, b * P:(b + 1) * P], ident[:])
                last.then_inc(vn_full, 1)

            def b_transpose_values():
                for b in range(6):
                    last = nc.tensor.transpose(vn_bank[:, b, :], v_blocks[:, b * P:(b + 1) * P], ident[:])
                last.then_inc(vn_full, 1)

            def c_scores(it, p, j):
                c0, at = c_seen(it, j)
                end = at + C_KEYS - c0
                pe.wait_ge(ct_lo, p * 8 + (8 * C_PAIRS * it + 2 * j + 2))
                qs = slice(P * j, P * (j + 1))
                for a, b in ((at, 512), (512, end)) if end > 512 else ((at, end),):
                    ks = slice(P * j + c0 + a - at, P * j + c0 + b - at)
                    for h in range(2):
                        mm(sc[h][:, a:b], cq[h][:, qs], ck[h][:, ks], True, False)
                    for h in range(2):
                        last = mm(sc[h][:, a:b], cq[h][ROWS[h], qs], ck_l[ROWS[h], ks], False, True)
                        if b == end:
                            last.then_inc(cs_full, 1)

            def c_transpose(it, p, j):
                c0 = 0 if half(it) else 512 - P * j
                for h in range(2):
                    pe.wait_ge(cs_prob, p * 8 + (8 * C_PAIRS * it + 2 * j + h + 1))
                    for b in range(c0 // P, 5):
                        cs = slice(b * P, (b + 1) * P)
                        last = nc.tensor.transpose(sc[h][:, cs], prob[:, h, cs], ident[:])
                    last.then_inc(ct_full, 1)

            def outputs(j):
                return pv[:, 512 * (j % 2) + 256 * (j // 2):512 * (j % 2) + 256 * (j // 2) + 256]

            def attend(region, values, block, probs, rows, start, stop):
                for i, (v, pt) in enumerate(((values[0], pth), (values[0], ptl), (values[1], pth))):
                    yield mm(region, v[rows, block, :], pt[rows, probs, :, :].rearrange("p h q -> p (h q)"),
                             start and i == 0, stop and i == 2)

            def c_attend(it, p, j):
                if j == 0:
                    pe.wait_ge(prod_ok, p * 2 + (MIXES * it + 2))
                pe.wait_ge(ct_lo, p * 8 + (8 * C_PAIRS * it + 2 * j + 2 + 2))
                v0 = 0 if half(it) else 4 - j
                for v in range(v0, 5):
                    *_, last = attend(outputs(j), (cv_h, cv_l), j + v, v, slice(0, P), v == v0, v == 4)
                last.then_inc(c_pv, 1)

            def b_scores(it, i):
                pe.wait_ge(v_ok, (C_PAIRS + 1) * (it + 1))
                pe.wait_ge(bq_ok, i + ((B_TILES + 1) * it + 2))
                pe.wait_ge(bt_lo, i * 4 + (4 * B_TILES * it + 4))
                for jj in range(2):
                    for t in range(2):
                        j = 2 * jj + t
                        c0 = HD if half(it) == 0 and j == 0 else 0
                        cs = slice(512 * jj + 192 * t + c0, 512 * jj + 192 * (t + 1))
                        qs, ks = slice(P * j, P * (j + 1)), slice(P * j + c0, P * j + 192)
                        for h in range(2):
                            mm(sc[h][:, cs], bq[h][:, qs], bk[h][:, ks], True, False)
                        for h in range(2):
                            last = mm(sc[h][:, cs], bq[h][ROWS[h], qs], bkl[ROWS[h], ks], False, True)
                            if t:
                                last.then_inc(bs_full, 1)

            def b_transpose(it, i, jj):
                for h in range(2):
                    pe.wait_ge(bs_prob, i * 4 + (4 * B_TILES * it + 2 * jj + h + 1))
                    for b in range(3):
                        c = P * b
                        last = nc.tensor.transpose(sc[h][:, 512 * jj + c:512 * jj + c + P], prob[:, h, c:c + P], ident[:])
                    last.then_inc(bt_full, 1)

            def b_attend(it, i, jj):
                if jj == 0:
                    pe.wait_ge(prod_ok, i + (MIXES * it + 2 * C_PAIRS + 2))
                pe.wait_ge(bt_lo, i * 4 + (4 * B_TILES * it + 2 * jj + 2 + 4))
                values, o = (bvh, bvl), [outputs(2 * jj + t) for t in range(2)]
                for t, block in ((0, 0), (1, 2)):
                    list(attend(o[t], values, 3 * jj + block, block, slice(0, P), True, False))
                for both in zip(*(attend(o[t], values, 3 * jj + 1, 1, ROWS[t], False, True) for t in range(2))):
                    last = both[1]
                last.then_inc(b_pv, 1)

            pe.wait_ge(ident_ok, 2)
            for it in range(STEPS):
                if it:
                    pe.wait_ge(xl_ok, 16 * (it + 1))
                if it:
                    pe.wait_ge(out_free, 16 * it + 8)
                pe.wait_ge(prod_ok, MIXES * it + 1)
                project(it, 0, 0, acc[0][:, :], 0, x_first=it == 0)
                with pe.Fori(0, C_PAIRS) as p:
                    def quarter(s, bank, **how):
                        project(it, p * U_C + s, s % 4, acc[bank][:, :], s % RING, **how)

                    for s in range(1, 4):
                        quarter(s, 0, x_first=it == 0)
                    pe.wait_ge(gate_ok, p * 2 + (MIXES * it + 1))
                    for s in range(4, 8):
                        quarter(s, 1)
                    pe.wait_ge(av_ok, p + (C_PAIRS * it + 1))
                    for s in range(8, 10):
                        quarter(s, 0)
                    pe.wait_ge(vt_ok, p + ((C_PAIRS + 1) * it + 1))
                    transpose_values(acc[1])
                    for s in range(10, 12):
                        quarter(s, 0)
                    pe.wait_ge(v_ok, p + ((C_PAIRS + 1) * it + 1))
                    for s in range(12, 16):
                        quarter(s, 1)
                    pe.wait_ge(k_ok, p + (C_PAIRS * it + 1))
                    quarter(16, 0)
                    pe.wait_ge(q_ok, p + (C_PAIRS * it + 1))
                    if half(it):
                        pe.wait_ge(hist_in, p * 32 + (32 * C_PAIRS * layer(it) + 32))
                    c_scores(it, p, 0)
                    quarter(17, 0)
                    quarter(18, 0, part=range(0, 1))
                    c_transpose(it, p, 0)
                    quarter(18, 0, part=range(1, 4))
                    c_scores(it, p, 1)
                    c_attend(it, p, 0)
                    quarter(19, 0)
                    c_transpose(it, p, 1)
                    quarter(20, 1)
                    c_scores(it, p, 2)
                    c_attend(it, p, 1)
                    quarter(21, 1)
                    c_transpose(it, p, 2)
                    pe.wait_ge(gate_ok, p * 2 + (MIXES * it + 2))
                    pe.wait_ge(ayl_ok, p + (C_PAIRS * it + 1))
                    pe.wait_ge(gwl_ok, p + (C_PAIRS * it + 2))
                    mm(acc[0][:, :], gwh, ya_h, True, False)
                    mm(acc[0][:, :], gwh, ya_l, False, False)
                    mm(acc[0][:, :], gwl, ya_h, False, True).then_inc(a_full, 1)
                    quarter(22, 1)
                    c_scores(it, p, 3)
                    c_attend(it, p, 2)
                    quarter(23, 1)
                    c_transpose(it, p, 3)
                    pe.wait_ge(prod_ok, p * 2 + (MIXES * it + 3))
                    quarter(24, 0)
                    c_attend(it, p, 3)

                for s in range(1, 4):
                    project(it, KV0 + s, s, acc[0][:, :], s % RING)
                pe.wait_ge(gate_ok, MIXES * it + 2 * C_PAIRS + 1)
                for s in range(4):
                    project(it, KV0 + 4 + s, s, acc[1][:, :], s % RING)
                for s in range(4):
                    project(it, KV0 + 8 + s, s, v_bank, s % RING)
                pe.wait_ge(vt_ok, (C_PAIRS + 1) * (it + 1))
                b_transpose_values()
                with pe.Fori(1, B_TILES) as i:
                    def quarter(s):
                        project(it, i * U_B + (B0 - 4 + s), s % 4, acc[s // 4][:, :], s % RING)
                    pe.wait_ge(rope_raw, i + ROTS * it)
                    quarter(0)
                    b_scores(it, i - 1)
                    quarter(1)
                    quarter(2)
                    b_transpose(it, i - 1, 0)
                    quarter(3)
                    b_attend(it, i - 1, 0)
                    pe.wait_ge(gate_ok, i + (MIXES * it + 2 * C_PAIRS))
                    quarter(4)
                    b_transpose(it, i - 1, 1)
                    quarter(5)
                    b_attend(it, i - 1, 1)
                    quarter(6)
                    quarter(7)
                b_scores(it, B_TILES - 1)
                pe.wait_ge(gate_ok, MIXES * (it + 1))
                for s in range(4):
                    def gate_unit(part):
                        project(it, O0 - 4 + s, s, acc[1][:, :], s % RING, part)
                    gate_unit(range(0, 1))
                    if s >= 2:
                        b_transpose(it, B_TILES - 1, s - 2)
                    gate_unit(range(1, 4))
                    if s >= 2:
                        b_attend(it, B_TILES - 1, s - 2)

                pe.wait_ge(rope_raw, ROTS * (it + 1))
                pe.wait_ge(bt_lo, 4 * B_TILES * (it + 1) + 4)
                pe.wait_ge(mixl_ok, 16 * it + 16)
                with pe.Fori(0, 2) as m:
                    for n in range(2):
                        banks = (even_banks, odd_banks)[n]
                        if n and 2 <= it + 1 < STEPS:
                            pe.wait_ge(xl_ok, m * 8 + (16 * (it + 1) + 8))
                        if n:
                            pe.wait_ge(prod_ok, MIXES * (it + 1) + 2)
                        for k in range(KT):
                            u = n * U_N + k
                            pe.wait_ge(w_lo, unit(it, m * (2 * U_N) + (O0 + u)) + (1 + RING))
                            if k == KT - 1:
                                pe.wait_ge(mixl_ok, 16 * (it + 1) + 1)
                            for t in range(QT):
                                if k == 0:
                                    pe.wait_ge(out_free, m * 8 + (16 * it + 4 * n + t + 1))
                                    if n == 0 and t == QT - 1:
                                        pe.wait_ge(gate_ok, MIXES * (it + 1) + 1)
                                ts = slice(t * P, (t + 1) * P)
                                kt = MIX_ORDER[k]
                                w_h, w_l = wh[:, u % RING, :], wl[:, u % RING, :]
                                mm(banks[t], mixh[:, kt, ts], w_h, k == 0, False)
                                mm(banks[t], mixh[:, kt, ts], w_l, False, False)
                                last = mm(banks[t], mixl[:, kt, ts], w_h, False, k == KT - 1)
                                if k == KT - 1 and t < QT - 1:
                                    last.then_inc(out_full, 1)
                            last.then_inc(w_used, 1)
                            if n == 0 and k in X_AT and 2 <= it + 1 < STEPS:
                                gg = X_AT.index(k)
                                pe.wait_ge(prod_ok, MIXES * (it + 1) + 2)
                                if gg >= 4:
                                    pe.wait_ge(xl_ok, m * 8 + (16 * (it + 1) + gg - 3))
                                else:
                                    pe.wait_ge(out_free, m * 8 + (16 * it + gg + 5))
                                pe.wait_ge(xin[gg % 2], m * 64 + (128 * it + 16 * (gg // 2 + 1)))
                                transpose_x(gg, odd_banks[gg % 4])

        @block.scalar
        def _(act):
            def copy(o, i, scale=1.0):
                return nc.scalar.activation(o, i, ACT.Copy, scale=scale)

            def split(it, r, slot):
                u = unit(it, r) + AHEAD
                slot = (slot + AHEAD) % RING
                split_at(u, slot)

            def split_at(u, slot):
                act.wait_ge(w_raw[slot], (u - slot) * (16 // RING) + 16)
                act.wait_ge(w_used, u + 1)
                copy(wh[:, slot, :], raw[:, slot, :]).then_inc(w_hi, 1)

            def used(it, r):
                act.wait_ge(w_used, unit(it, r) + (1 + RING))

            def mix_hi(count, tile):
                act.wait_ge(prod_ok, count + 2)
                copy(mixh[:, ds(tile, 1), :].rearrange("p o n -> p (o n)"), tmp[:]).then_inc(mixh_ok, 1)

            def tanh_gate(bank):
                nc.scalar.activation(tmp[:], acc[bank][:, :], ACT.Tanh, scale=0.5).then_inc(tanh_ok, 1)

            def x_hi_tile(tile, source):
                copy(xh[:, ds(tile, 1), :].rearrange("p o n -> p (o n)"), source).then_inc(xh_ok, 1)

            def x_hi(it, m, gg):
                bank, t = odd_banks[gg % 4], 2 * m + gg // 4
                act.wait_ge(tr_full, transposed(it, m * 8 + gg + 1))
                copy(xh[:, 4 * (gg % 4):4 * (gg % 4) + 4, ds(t * P, P)],
                     bank.rearrange("p (k q) -> p k q", k=4)).then_inc(xh_ok, 1)

            for q in range(4):
                split_at(q, q)
                for k in range(4 * q, 4 * q + 4):
                    act.wait_ge(x0_in[k], 16)
                    copy(xh[:, k, :], x_in[:, k, :]).then_inc(xh_ok, 1)

            def queries_hi(q, source, scale=1.0):
                for h in range(2):
                    last = copy(q[h][ROWS[h], :], source[ROWS[h], :], scale)
                return last

            def keys_hi(k, source):
                for h in range(2):
                    for rows in ROWS:
                        last = copy(k[h][rows, :], source[ROWS[h], :])
                return last

            def c_exp(it, p, j):
                c0, at = c_seen(it, j)
                for h in range(2):
                    act.wait_ge(cs_max, p * 8 + (8 * C_PAIRS * it + 2 * j + h + 1))
                    nc.scalar.activation(prob[:, h, c0:C_KEYS], sc[h][:, at:at + C_KEYS - c0], ACT.Exp,
                                         bias=nmax[:, h, 0:1], accum_out=psums[:, h, 0:1]).then_inc(cs_exp, 1)

            def c_hi(it, p, j):
                b0 = 0 if half(it) else 4 - j
                for h in range(2):
                    act.wait_ge(ct_full, p * 8 + (8 * C_PAIRS * it + 2 * j + h + 1))
                    copy(pth[:, b0:5, h, :], sc[h][:, b0 * P:5 * P].rearrange("p (b q) -> p b q", q=P)).then_inc(ct_hi, 1)

            def b_exp(it, i, u):
                jj, h = u // 2, u % 2
                act.wait_ge(bs_max, i * 4 + (4 * B_TILES * it + u + 1))
                if jj:
                    act.wait_ge(bt_full, i * 4 + (4 * B_TILES * it + h + 1))
                for t in range(2):
                    nc.scalar.activation(prob[:, h, 192 * t:192 * (t + 1)], sc[h][:, 512 * jj + 192 * t:512 * jj + 192 * (t + 1)],
                                         ACT.Exp, bias=nmax[:, u, t:t + 1], accum_out=psums[:, u, t:t + 1])
                nc.scalar.activation(esink[:, u, :], nmax[:, u, :], ACT.Exp, bias=sink1[:, 0, h:h + 1]).then_inc(bs_exp, 1)

            def b_hi(it, i, u):
                jj, h = u // 2, u % 2
                act.wait_ge(bt_full, i * 4 + (4 * B_TILES * it + u + 1))
                copy(pth[:, 0:3, h, :], sc[h][:, 512 * jj:512 * jj + 384].rearrange("p (b q) -> p b q", q=P)
                     ).then_inc(bt_hi, 1)

            def rope_copy(it, n, scale):
                if isinstance(n, int) and n == 0:
                    act.wait_ge(ayl_ok, C_PAIRS * (it + 1))
                else:
                    act.wait_ge(bq_ok, n + ROTS * it)
                bank = acc[1] if isinstance(n, int) and n == 1 else acc[0]
                copy(s0[:, 0:HALF], bank[:, :], scale).then_inc(rope_raw, 1)

            for it in range(STEPS):
                nb = 16 * it
                if it:
                    split(it, 0, 0)
                split(it, 1, 1)
                if 0 < it:
                    act.wait_ge(ln_var, it)
                    nc.scalar.activation(sq[:], veps[:], ACT.Sqrt).then_inc(ln_sqrt, 1)
                with act.Fori(0, C_PAIRS) as p:
                    def slot(s):
                        split(it, p * U_C + s, s % RING)
                    pc = C_PAIRS * it

                    for s in range(2, 5):
                        slot(s)
                    used(it, p * U_C + 3)
                    copy(av[:, 16:16 + HALF], acc[0][:, :]).then_inc(av_ok, 1)
                    slot(5)
                    slot(6)
                    act.wait_ge(gw_in, p * 16 + (16 * pc + 16))
                    copy(gwh, gw[:]).then_inc(gwh_ok, 1)
                    slot(7)
                    act.wait_ge(mixl_ok, p * 2 + (nb + 1))
                    if it == 0:
                        act.wait_ge(rel_out, 16)
                    used(it, p * U_C + 7)
                    copy(tmp[:], acc[1][:, :]).then_inc(vt_ok, 1)
                    slot(8)
                    slot(9)
                    act.wait_ge(ay_ok, p + (pc + 1))
                    copy(ya_h, s0[:, 16:16 + HALF]).then_inc(ayh_ok, 1)
                    act.wait_ge(vn_full, p + ((C_PAIRS + 1) * it + 1))
                    copy(cv_h[:, 4:8, :], acc[1][:, :].rearrange("p (b c) -> p b c", c=P)).then_inc(vh_ok, 1)
                    slot(10)
                    slot(11)
                    used(it, p * U_C + 11)
                    keys_hi([k[:, HALF:2 * HALF] for k in ck], acc[0]).then_inc(kh_ok, 1)
                    slot(12)
                    slot(13)
                    slot(14)
                    slot(15)
                    used(it, p * U_C + 15)
                    queries_hi(cq, acc[1], SCALE).then_inc(qh_ok, 1)
                    slot(16)
                    slot(17)
                    c_exp(it, p, 0)
                    slot(18)
                    c_hi(it, p, 0)
                    slot(19)
                    c_exp(it, p, 1)
                    slot(20)
                    c_hi(it, p, 1)
                    used(it, p * U_C + 19)
                    tanh_gate(0)
                    slot(21)
                    c_exp(it, p, 2)
                    slot(22)
                    c_hi(it, p, 2)
                    mix_hi(p * 2 + (nb + 1), p + MIX_A)
                    slot(23)
                    c_exp(it, p, 3)
                    c_hi(it, p, 3)
                    used(it, p * U_C + 23)
                    act.wait_ge(mixl_ok, p * 2 + (nb + 1 + 1))
                    tanh_gate(1)
                    mix_hi(p * 2 + (nb + 2), p + MIX_C)
                    if not half(it):
                        act.wait_ge(hist_out, p * 32 + (32 * C_PAIRS * layer(it) + 32))
                    slot(24)
                    slot(25)

                for s in range(2, 5):
                    split(it, KV0 + s, s % RING)
                used(it, KV0 + 3)
                rope_copy(it, 0, SCALE)
                split(it, KV0 + 5, 1)
                act.wait_ge(rope_ok, (B_TILES + 1) * it + 1)
                queries_hi(bq, s0[:, 0:HALF]).then_inc(qh_ok, 1)
                for s in range(6, 9):
                    split(it, KV0 + s, s % RING)
                used(it, KV0 + 7)
                rope_copy(it, 1, 1.0)
                split(it, KV0 + 9, 1)
                if half(it):
                    act.wait_ge(hist_mv, layer(it) + 1)
                act.wait_ge(rope_ok, (B_TILES + 1) * it + 2)
                keys_hi([k[:, HD:] for k in bk], s0[:, 0:HALF]).then_inc(qh_ok, 1)
                split(it, KV0 + 10, 2)
                split(it, KV0 + 11, 3)
                used(it, KV0 + 11)
                for b, token, n in ((0, 0, 2), (2, P, 0), (3, 2 * P - HD, 0), (4, 3 * P - HD, 1), (5, 3 * P, 0)):
                    o = v_blocks[:, b * P:(b + max(n, 1)) * P]
                    if n:
                        o = o.rearrange("p (n d c) -> p n d c", n=n, d=2)
                        i = v_bank[:, token:token + n * HD].rearrange("p (n o c) -> p n o c", n=n, o=1)\
                            .to_broadcast([P, n, 2, HD])
                    else:
                        i = v_bank[:, token:token + P]
                    last = copy(o, i)
                last.then_inc(vt_ok, 1)
                act.wait_ge(vn_full, (C_PAIRS + 1) * (it + 1))
                copy(bvh[ROWS[1], 0, :], vn_bank[ROWS[1], 0, :])
                copy(bvh[:, 1:, :], vn_bank[:, 1:, :]).then_inc(vh_ok, 1)
                with act.Fori(1, B_TILES) as i:
                    def slot(s):
                        split(it, i * U_B + (B0 - 4 + s), s % RING)
                    slot(0)
                    b_exp(it, i - 1, 0)
                    b_exp(it, i - 1, 1)
                    slot(1)
                    slot(2)
                    b_hi(it, i - 1, 0)
                    b_hi(it, i - 1, 1)
                    b_exp(it, i - 1, 2)
                    b_exp(it, i - 1, 3)
                    slot(3)
                    slot(4)
                    used(it, i * U_B + (B0 - 4 + 3))
                    rope_copy(it, i + 1, SCALE)
                    b_hi(it, i - 1, 2)
                    b_hi(it, i - 1, 3)
                    slot(5)
                    act.wait_ge(rope_ok, i + ((B_TILES + 1) * it + 2))
                    queries_hi(bq, s0[:, 0:HALF]).then_inc(qh_ok, 1)
                    slot(6)
                    slot(7)
                    used(it, i * U_B + (B0 - 4 + 7))
                    act.wait_ge(mixl_ok, i + (nb + 2 * C_PAIRS))
                    tanh_gate(1)
                    mix_hi(i + (nb + 2 * C_PAIRS), i + (MIX_B - 1))
                last = B_TILES - 1
                split(it, O0 - 4, 0)
                b_exp(it, last, 0)
                b_exp(it, last, 1)
                split(it, O0 - 3, 1)
                split(it, O0 - 2, 2)
                b_hi(it, last, 0)
                b_hi(it, last, 1)
                b_exp(it, last, 2)
                b_exp(it, last, 3)
                split(it, O0 - 1, 3)
                b_hi(it, last, 2)
                b_hi(it, last, 3)
                used(it, O0 - 1)
                act.wait_ge(mixl_ok, nb + 2 * C_PAIRS + B_TILES)
                tanh_gate(1)
                mix_hi(nb + 16, MIX_B + last)

                with act.Fori(0, 2) as m:
                    for s in range(2 * U_N):
                        split(it, m * (2 * U_N) + (O0 + s), s % RING)
                        if s in X_AT and it + 1 < STEPS:
                            gg = X_AT.index(s)
                            if layer(it + 1) == 0:
                                act.wait_ge(xin[gg % 2], m * 64 + (128 * it + 16 * (gg // 2 + 1)))
                                x_hi_tile(m * 8 + gg, prob[:, gg % 2, 0:512])
                            else:
                                x_hi(it + 1, m, gg)
                        if s % U_N == U_N - 1 and it + 1 < STEPS:
                            n = 2 * m + s // U_N
                            act.wait_ge(res_ok, n * 4 + (16 * it + 4))
                            act.dma_start(res_d[ds(n, 1)].rearrange("o p t n -> (o p) t n"), res[:]).then_inc(res_out, 16)

            nc.scalar.activation(sq2[:], ident[:, 0:QT], ACT.Sqrt)
            act.wait_ge(ln_var, STEPS)
            nc.scalar.activation(sq[:], veps[:], ACT.Sqrt).then_inc(ln_sqrt, 1)
            act.wait_ge(ln_rstd, 1)
            for t in range(QT):
                cols = last_rows(t, LN_V, D)
                nc.scalar.activation(cols, cols, ACT.Identity, scale=rstd[:, t:t + 1], bias=shift[:, t:t + 1]
                                     ).then_inc(ln_unit, 1)

        @block.gpsimd
        def _(pool):
            pool.sem_inc(w_lo, RING)
            nc.gpsimd.memset(ident[:], 0.0).then_inc(ident_ok, 1)
            pool.wait_ge(ident_ok, 1)
            nc.gpsimd.affine_select(out=ident[:], in_=ident[:], compare_op=ALU.not_equal, fill=1.0, base=0,
                                    pattern=[[-1, P]], channel_multiplier=1).then_inc(ident_ok, 1)
            with pool.Fori(0, STEPS * U_STEP, RING) as u:
                for s in range(RING):
                    pool.wait_ge(w_hi, u + (s + 1))
                    pool.wait_ge(w_used, u + (s + 1))
                    nc.gpsimd.tensor_tensor(wl[:, s, :], raw[:, s, :], wh[:, s, :].bitcast(F32), ALU.subtract
                                            ).then_inc(w_lo, 1)
            pool.wait_ge(ln_in, 48 * 4 * (STEPS - 1) + 32)
            for t in range(QT):
                cols = last_rows(t, LN_V, D)
                pool.wait_ge(ln_unit, t + 1)
                nc.gpsimd.tensor_tensor(cols, cols, gain_all[:, LN_V:D], ALU.mult).then_inc(pool_step, 1)
                pool.wait_ge(pool_step, t + 1)
                nc.gpsimd.tensor_tensor(cols, cols, bias_all[:, LN_V:D], ALU.add).then_inc(ln_end_p, 1)

        @block.vector
        def _(dv):
            V = nc.vector
            count = [0, 0]

            def section(value):
                count[0], count[1] = value, 0

            def V_(ins):
                count[1] += 1
                ins.then_inc(dve, 1)
                dv.wait_ge(dve, count[0] + count[1])

            dv.sem_inc(gwl_ok, 1)
            dv.sem_inc(bias_ok, 1)
            dv.sem_inc(ct_lo, 2)
            dv.sem_inc(bt_lo, 4)
            dv.sem_inc(prod_ok, 2)
            dv.sem_inc(mixl_ok, 1)
            dv.sem_inc(out_free, 8)
            dv.sem_inc(gate_ok, 1)

            def lo(o, whole, hi):
                return V.tensor_tensor(o, whole, hi.bitcast(F32), ALU.subtract)

            def keys_lo(o, whole, hi):
                for h in range(2):
                    last = lo(o[ROWS[h], :], whole[ROWS[h], :], hi[h][ROWS[h], :])
                return last

            def queries_lo(q, whole, scale):
                for h in range(2):
                    last = V.scalar_tensor_tensor(q[h][ROWS[1 - h], :], whole[ROWS[h], :], scale,
                                                  q[h][ROWS[h], :].bitcast(F32), ALU.mult, ALU.subtract)
                return last

            def x_lo(idx, gg, bank, t):
                dv.wait_ge(xh_ok, idx + 1)
                piece = (slice(None), slice(4 * (gg % 4), 4 * (gg % 4) + 4), ds(t * P, P))
                lo(xl[piece], bank.rearrange("p (k q) -> p k q", k=4), xh[piece]).then_inc(xl_ok, 1)

            def gate_ready(n, bank):
                dv.wait_ge(tanh_ok, n)
                V.scalar_tensor_tensor(gate[:], tmp[:], 1.0, acc[bank][:, :], ALU.add, ALU.mult).then_inc(gate_ok, 1)

            def mix_lo(n, tile):
                dv.wait_ge(mixh_ok, n)
                t = mixh[:, ds(tile, 1), :].rearrange("p o n -> p (o n)")
                lo(mixl[:, ds(tile, 1), :].rearrange("p o n -> p (o n)"), tmp[:], t).then_inc(mixl_ok, 1)

            def attention_product(gates):
                dv.wait_ge(gate_ok, gates + 1)
                for h in range(2):
                    rows = slice(HD * h, HD * (h + 1))
                    for t in range(2):
                        o, g = (v[rows, :].rearrange("p (i t q) -> p i t q", i=2, t=2)[:, :, t, :] for v in (tmp, gate))
                        last = V.scalar_tensor_tensor(o, pv5[rows, :, t, h, :], 0.5, g, ALU.mult, ALU.mult)
                last.then_inc(prod_ok, 1)

            def c_max(it, p, j):
                c0, at = c_seen(it, j)
                end = at + C_KEYS - c0
                for h in range(2):
                    s = sc[h]
                    dv.wait_ge(cs_full, p * 8 + (8 * C_PAIRS * it + 2 * j + h + 1))
                    if half(it):
                        V.memset(s[HD:P, at:at + CHUNK], NEG_INF)
                    near = min(NEAR, end - at)
                    V_(V.tensor_tensor(s[:, end - near:end], s[:, end - near:end],
                                       brope[:, 1, NEAR * (h + 1) - near:NEAR * (h + 1)], ALU.add))
                    V.tensor_reduce(nmax[:, h, 0:1], s[:, at:end], AX, ALU.max, negate=True).then_inc(cs_max, 1)

            def c_normalise(it, p, j):
                c0 = 0 if half(it) else 512 - P * j
                for h in range(2):
                    dv.wait_ge(cs_exp, p * 8 + (8 * C_PAIRS * it + 2 * j + h + 1))
                    V_(V.reciprocal(rinv[:, h, 0:1], psums[:, h, 0:1]))
                    V.tensor_scalar(prob[:, h, c0:C_KEYS], prob[:, h, c0:C_KEYS], rinv[:, h, 0:1], None, ALU.mult
                                    ).then_inc(cs_prob, 1)

            def c_lo(it, p, j):
                b0 = 0 if half(it) else 4 - j
                for h in range(2):
                    dv.wait_ge(ct_hi, p * 8 + (8 * C_PAIRS * it + 2 * j + h + 1))
                    lo(ptl[:, b0:5, h, :], sc[h][:, b0 * P:5 * P].rearrange("p (b q) -> p b q", q=P), pth[:, b0:5, h, :]
                       ).then_inc(ct_lo, 1)

            def b_max(it, i, u):
                jj, h = u // 2, u % 2
                dv.wait_ge(bs_full, i * 4 + (4 * B_TILES * it + u + 1))
                s = sc[h][:, 512 * jj:512 * jj + 384].rearrange("p (t c) -> p t c", t=2)
                if half(it) == 0 and jj == 0:
                    V.memset(s[:, 0, 0:CHUNK], NEG_INF)
                    V.memset(s[HD:P, 1, 0:CHUNK], NEG_INF)
                else:
                    V.memset(s[HD:P, :, 0:CHUNK], NEG_INF)
                V_(V.memset(s[0:HD, :, 2 * CHUNK:3 * CHUNK], NEG_INF))
                V_(V.tensor_reduce(mx[:, u, :], s, AX, ALU.max, negate=True))
                V.tensor_scalar(nmax[:, u, :], mx[:, u, :], sink1[:, 1, h:h + 1], None, ALU.min).then_inc(bs_max, 1)

            def b_normalise(it, i, u):
                h = u % 2
                dv.wait_ge(bs_exp, i * 4 + (4 * B_TILES * it + u + 1))
                V_(V.tensor_tensor(mx[:, u, :], psums[:, u, :], esink[:, u, :], ALU.add))
                V_(V.reciprocal(rinv[:, u, :], mx[:, u, :]))
                for t in range(2):
                    cs = slice(192 * t, 192 * (t + 1))
                    last = V.tensor_scalar(prob[:, h, cs], prob[:, h, cs], rinv[:, u, t:t + 1], None, ALU.mult)
                last.then_inc(bs_prob, 1)

            def b_lo(it, i, u):
                jj, h = u // 2, u % 2
                dv.wait_ge(bt_hi, i * 4 + (4 * B_TILES * it + u + 1))
                lo(ptl[:, 0:3, h, :], sc[h][:, 512 * jj:512 * jj + 384].rearrange("p (b q) -> p b q", q=P),
                   pth[:, 0:3, h, :]).then_inc(bt_lo, 1)

            def sinks_of(it, i):
                V_(V.tensor_copy(sink1[:, 0, :], sink_s[:, layer(it), ds(i, 1), :].rearrange("p o h -> p (o h)")))
                V_(V.tensor_scalar(sink1[:, 1, :], sink1[:, 0, :], -1.0, None, ALU.mult))

            def rotate(n):
                dv.wait_ge(rope_raw, n)
                x_, y_ = s0[:, 0:HALF], s1[:, 0:HALF]
                V.tensor_tensor(y_, x_, brope[:, 0, :], ALU.mult)
                V_(V.stream_shuffle(x_, x_, SWAP))
                V_(V.tensor_tensor(x_, x_, brope[:, 1, :], ALU.mult))
                V.tensor_tensor(x_, x_, y_, ALU.add).then_inc(rope_ok, 1)

            def rotated_query(n):
                dv.wait_ge(qh_ok, n)
                queries_lo(bq, s0[:, 0:HALF], 1.0).then_inc(bq_ok, 1)

            def layer_norm(it, n):
                dv.wait_ge(ln_in, n * 48 + (192 * it + 48))
                for t in range(QT):
                    last = V.tensor_scalar(res[:, t, :], res[:, t, :], mv[:, t, 0:1], rstd[:, t:t + 1],
                                           ALU.subtract, ALU.mult)
                V_(last)
                for slot, op in ((0, ALU.mult), (1, ALU.add)):
                    v = prob[:, slot, 0:512].rearrange("p (o n) -> p o n", o=1).to_broadcast([P, QT, 512])
                    last = V.tensor_tensor(res[:], res[:], v, op)
                    if slot == 0:
                        V_(last)
                last.then_inc(ln_ok, 1)

            def first_lo(k):
                dv.wait_ge(xh_ok, k + 1)
                lo(xl[:, k, :], x_in[:, k, :], xh[:, k, :]).then_inc(xl_ok, 1)

            for k in range(4):
                first_lo(k)
            dv.wait_ge(rel_in, 16)
            section(0)
            V.tensor_copy(tmp[0:DEPTH * 8, 0:127], tmp[0:DEPTH * 8, 127:128].to_broadcast([DEPTH * 8, 127])).then_inc(rel_ok, 1)
            for k in range(4, KT):
                first_lo(k)
            dv.wait_ge(const_in, 64)
            V_(V.tensor_scalar(scale_s[:], scale_s[:], 0.5, None, ALU.mult))
            total = count[1]

            for it in range(STEPS):
                pc, nb = C_PAIRS * it, 16 * it
                per_c = 23 + (2 if it else 0) - half(it)
                with dv.Fori(0, C_PAIRS) as p:
                    section(p * per_c + total)
                    V.tensor_copy(coef1[:], coef[:, ds(p, 1), :].rearrange("p o n -> p (o n)"))
                    V.tensor_copy(inv1[:], inv16[:, ds(p, 1), :].rearrange("p o n -> p (o n)"))
                    V.tensor_copy(scale1[:], scale_s[:, layer(it), ds(p, 1)])
                    if half(it):
                        V_(V.tensor_copy(av[:, 0:16], a_tail[:, ds(p, 1), :].rearrange("p o n -> p (o n)")))
                    else:
                        V_(V.memset(av[:, 0:16], 0.0))
                    dv.wait_ge(av_ok, p + (pc + 1))
                    N = 16 + HALF
                    V_(V.tensor_tensor(s0[:, 1:N], av[:, 1:N], av[:, 0:N - 1], ALU.add))
                    V_(V.scalar_tensor_tensor(s1[:, 3:N], s0[:, 1:N - 2], coef1[:, 0:1], s0[:, 3:N], ALU.mult, ALU.add))
                    V_(V.scalar_tensor_tensor(s0[:, 7:N], s1[:, 3:N - 4], coef1[:, 1:2], s1[:, 7:N], ALU.mult, ALU.add))
                    V_(V.scalar_tensor_tensor(s1[:, 15:N], s0[:, 7:N - 8], coef1[:, 2:3], s0[:, 15:N], ALU.mult, ALU.add))
                    if half(it):
                        V.scalar_tensor_tensor(s0[:, 16:N], s1[:, 16:N], coef1[:, 3:4], av[:, 16:N], ALU.mult, ALU.subtract
                                               ).then_inc(ay_ok, 1)
                    else:
                        V.tensor_copy(a_tail[:, ds(p, 1), :].rearrange("p o n -> p (o n)"), av[:, HALF:N])
                        V_(V.tensor_tensor(s1[:, 16:32], s1[:, 16:32], inv1[:], ALU.mult))
                        V.tensor_tensor(s0[:, 16:32], s1[:, 16:32], av[:, 16:32], ALU.subtract)
                        V.scalar_tensor_tensor(s0[:, 32:N], s1[:, 32:N], coef1[:, 3:4], av[:, 32:N], ALU.mult, ALU.subtract
                                               ).then_inc(ay_ok, 1)
                    dv.wait_ge(gwh_ok, p + (pc + 1))
                    lo(gwl, gw[:], gwh).then_inc(gwl_ok, 1)
                    dv.wait_ge(ayh_ok, p + (pc + 1))
                    lo(ya_l, s0[:, 16:N], ya_h).then_inc(ayl_ok, 1)
                    dv.wait_ge(vh_ok, p + ((C_PAIRS + 1) * it + 1))
                    lo(cv_l[:, 4:8, :], acc[1][:, :].rearrange("p (b c) -> p b c", c=P), cv_h[:, 4:8, :])\
                        .then_inc(v_ok, 1)
                    dv.wait_ge(bias_in, p * 16 + (16 * pc + 16))
                    for h in range(2):
                        cs = slice(NEAR * h, NEAR * (h + 1))
                        last = V.tensor_scalar(brope[:, 1, cs], brope[:, 0, cs], brope[:, 0, NEAR * h:NEAR * h + 1], None, ALU.subtract)
                    V_(last)
                    for h in range(2):
                        last = V.memset(brope[0:HD, 1, NEAR * (h + 1) - CHUNK:NEAR * (h + 1)], NEG_INF)
                    last.then_inc(bias_ok, 1)
                    dv.wait_ge(kh_ok, p + (pc + 1))
                    keys_lo(ck_l[:, HALF:2 * HALF], acc[0], [k[:, HALF:2 * HALF] for k in ck]).then_inc(k_ok, 1)
                    if it:
                        layer_norm(it - 1, p)
                    dv.wait_ge(qh_ok, p + ((C_PAIRS + B_TILES + 1) * it + 1))
                    queries_lo(cq, acc[1], SCALE).then_inc(q_ok, 1)
                    dv.wait_ge(bias_ok, p + (pc + 2))
                    c_max(it, p, 0)
                    c_normalise(it, p, 0)
                    c_lo(it, p, 0)
                    c_max(it, p, 1)
                    c_normalise(it, p, 1)
                    c_lo(it, p, 1)
                    gate_ready(p * 2 + ((2 * C_PAIRS + B_TILES) * it + 1), 0)
                    c_max(it, p, 2)
                    c_normalise(it, p, 2)
                    c_lo(it, p, 2)
                    dv.wait_ge(a_full, p + (pc + 1))
                    V.scalar_tensor_tensor(tmp[:], acc[0][:, :], scale1[:], gate[:], ALU.mult, ALU.mult).then_inc(prod_ok, 1)
                    mix_lo(p * 2 + (nb + 1), p + MIX_A)
                    c_max(it, p, 3)
                    c_normalise(it, p, 3)
                    c_lo(it, p, 3)
                    gate_ready(p * 2 + ((2 * C_PAIRS + B_TILES) * it + 2), 1)
                    dv.wait_ge(c_pv, p * 4 + (4 * pc + 4))
                    attention_product(p * 2 + (MIXES * it + 2))
                    mix_lo(p * 2 + (nb + 2), p + MIX_C)
                    if not half(it):
                        dv.wait_ge(hist_out, p * 32 + (32 * C_PAIRS * layer(it) + 32))
                    assert count[1] == per_c, (it, count[1])
                total += C_PAIRS * per_c

                section(total)
                dv.wait_ge(rope_raw, ROTS * it + 1)
                if half(it):
                    for k in (*bk, bkl):
                        V.tensor_copy(k[:, 0:HD], k[:, HALF:HALF + HD])
                    V.tensor_copy(bvh[ROWS[0], 0, :], bvh[ROWS[1], 5, :])
                    V.tensor_copy(bvl[ROWS[0], 0, :], bvl[ROWS[1], 5, :]).then_inc(hist_mv, 1)
                else:
                    for v in (bvh, bvl):
                        V.tensor_scalar(v[ROWS[0], 0, :], ident[ROWS[0], :], 0.0, None, ALU.mult)
                dv.wait_ge(rope_in, 32 * (it + 1))
                rotate(ROTS * it + 1)
                rotated_query(QS * it + C_PAIRS + 1)
                rotate(ROTS * it + 2)
                if half(it):
                    dv.wait_ge(hist_mv, layer(it) + 1)
                dv.wait_ge(qh_ok, QS * it + C_PAIRS + 2)
                keys_lo(bkl[:, HD:], s0[:, 0:HALF], [k[:, HD:] for k in bk]).then_inc(bq_ok, 1)
                dv.wait_ge(vh_ok, (C_PAIRS + 1) * (it + 1))
                lo(bvl[ROWS[1], 0, :], vn_bank[ROWS[1], 0, :], bvh[ROWS[1], 0, :])
                lo(bvl[:, 1:, :], vn_bank[:, 1:, :], bvh[:, 1:, :]).then_inc(v_ok, 1)
                total += count[1]

                per_b = 2 + 2 * 4 + 2 * 4 + 2

                def softmax(i, pending):
                    sinks_of(it, i)
                    for u in (0, 1):
                        b_max(it, i, u)
                    if pending:
                        mix_lo(i + (nb + 2 * C_PAIRS), i + (MIX_B - 1))
                    for u in (0, 1):
                        b_normalise(it, i, u)
                    for u in (2, 3):
                        b_max(it, i, u)
                    for u in (0, 1):
                        b_lo(it, i, u)
                    for u in (2, 3):
                        b_normalise(it, i, u)

                def finish(i):
                    gate_ready(i + (MIXES * it + 2 * C_PAIRS + 1), 1)
                    dv.wait_ge(b_pv, i * 2 + (2 * B_TILES * it + 2))
                    attention_product(i + (MIXES * it + 2 * C_PAIRS + 1))

                def tile_before(i, pending):
                    softmax(i - 1, pending)
                    rotate(i + (ROTS * it + 2))
                    for u in (2, 3):
                        b_lo(it, i - 1, u)
                    rotated_query(i + (QS * it + C_PAIRS + 2))
                    finish(i - 1)

                section(total)
                tile_before(1, False)
                with dv.Fori(2, B_TILES) as i:
                    section((i - 1) * per_b + total)
                    tile_before(i, True)
                    assert count[1] == per_b, count[1]
                total += (B_TILES - 1) * per_b

                section(total)
                softmax(B_TILES - 1, True)
                for u in (2, 3):
                    b_lo(it, B_TILES - 1, u)
                finish(B_TILES - 1)
                mix_lo(nb + 16, MIX_B + B_TILES - 1)
                total += count[1]

                def summed(t, c):
                    return res[:, t, :] if it + 1 < STEPS else sums[:, ds(4 * t + c, 1), :].rearrange("p o n -> p (o n)")

                with dv.Fori(0, 2) as m:
                    for n in range(2):
                        if n == 0 and it + 1 < STEPS:
                            for gg in range(8):
                                if layer(it + 1) == 0:
                                    dv.wait_ge(xh_ok, m * 8 + (16 * (it + 1) + gg + 1))
                                    o, hi = (v[:, ds(m * 8 + gg, 1), :].rearrange("p o n -> p (o n)") for v in (xl, xh))
                                    lo(o, prob[:, gg % 2, 0:512], hi).then_inc(xl_ok, 1)
                                else:
                                    x_lo(m * 8 + (16 * (it + 1) + gg), gg, odd_banks[gg % 4], 2 * m + gg // 4)
                        c = 2 * m + n
                        dv.wait_ge(res_in, c * 16 + (64 * it + 16))

                        def statistics(t):
                            dv.wait_ge(out_free, c * 4 + (16 * it + t + 1 + 8))
                            V.bn_stats(stats[:, t, ds(c, 1), :].rearrange("p o s -> p (o s)"), summed(t, c)).then_inc(res_ok, 1)

                        for t in range(QT):
                            if t < QT - 1:
                                dv.wait_ge(out_full, c * 3 + (12 * it + t + 1))
                            else:
                                dv.wait_ge(w_used, unit(it, c * U_N + (O0 + U_N)) + RING)
                            V.scalar_tensor_tensor(summed(t, c), res[:, t, :], ALPHA, (even_banks, odd_banks)[n][t],
                                                   ALU.mult, ALU.add).then_inc(out_free, 1)
                            if it + 1 == STEPS and t:
                                statistics(t - 1)
                        for t in range(QT - 1 if it + 1 == STEPS else 0, QT):
                            statistics(t)
                section(total)
                dv.wait_ge(res_ok, 16 * (it + 1))
                for t in range(QT):
                    last = V.bn_aggr(mv[:, t, :], stats[:, t, :, :].rearrange("p n s -> p (n s)"))
                V_(last)
                V.tensor_scalar(veps[:], mv[:, :, 1], LN_EPS, None, ALU.add).then_inc(ln_var, 1)
                dv.wait_ge(ln_sqrt, it + 1)
                V_(V.reciprocal(sq2[:], sq[:]))
                V_(V.tensor_tensor(sq2[:], sq2[:], veps[:], ALU.mult))
                V_(V.tensor_tensor(sq2[:], sq2[:], sq[:], ALU.add))
                V_(V.reciprocal(rstd[:], sq2[:]))
                V_(V.tensor_scalar(rstd[:], rstd[:], 2.0, None, ALU.mult))
                total += count[1]

            section(total)
            V.scalar_tensor_tensor(shift[:], mv[:, :, 0], -1.0, rstd[:], ALU.mult, ALU.mult).then_inc(ln_rstd, 1)
            dv.wait_ge(ln_in, 48 * 4 * (STEPS - 1) + 32)
            for t in range(QT):
                cols = last_rows(t, 0, LN_V)
                V_(V.scalar_tensor_tensor(cols, cols, mv[:, t, 0:1], gain_all[:, 0:LN_V], ALU.subtract, ALU.mult))
                V.scalar_tensor_tensor(cols, cols, rstd[:, t:t + 1], bias_all[:, 0:LN_V], ALU.mult, ALU.add
                                       ).then_inc(ln_end_v, 1)


def laid_out(x, w_in, a_group_w, a_scale, b_sinks, c_rel_bias, w_out, ln_gain, ln_bias):
    cols = np.split(np.arange(w_in.shape[2]),
                    np.cumsum([A_WIDTH, A_WIDTH, B_WIDTH, P, P, B_WIDTH, C_WIDTH, C_WIDTH, C_WIDTH])) 
    a_v, a_g, b_q, b_k, b_v, b_g, c_q, c_k, c_v, c_g = cols

    def tile(v, i):
        return v[i * P:(i + 1) * P]

    def heads(v, i):
        return np.concatenate([v[i * HD:(i + 1) * HD], v[(i + B_TILES) * HD:(i + B_TILES + 1) * HD]])

    order = []
    for p in range(C_PAIRS):
        order += [tile(v, p) for v in (a_v, c_v, c_k, c_q, a_g, c_g)]
    order += [heads(b_q, 0), b_k, b_v]
    for i in range(1, B_TILES):
        order += [heads(b_q, i), heads(b_g, i - 1)]
    order += [heads(b_g, B_TILES - 1)]
    order = np.concatenate(order)
    w1 = w_in[:, :, order].reshape(DEPTH, 4, 4, P, len(order) // P, P)
    w1 = w1.transpose(0, 4, 1, 3, 2, 5).reshape(DEPTH, O0, P, UNIT)
    chan = np.arange(D)
    mix = [tile(chan, g) for g in range(A_GROUPS)] + [heads(A_WIDTH + np.arange(B_WIDTH), i) for i in range(B_TILES)] \
        + [tile(A_WIDTH + B_WIDTH + np.arange(C_WIDTH), p) for p in range(C_PAIRS)]
    w2 = w_out[:, np.concatenate([mix[k] for k in MIX_ORDER]), :].reshape(DEPTH, KT, P, 4, UNIT)
    w2 = w2.transpose(0, 3, 1, 2, 4).reshape(DEPTH, 4 * U_N, P, UNIT)
    wall = np.concatenate([w1, w2], axis=1)

    t = np.arange(SEQ, dtype=np.float32)
    j = np.arange(ROPE_DIM // 2, dtype=np.float32)
    inv = (np.float32(ROPE_THETA) ** (-j / np.float32(ROPE_DIM // 2))).astype(np.float32)
    ang = (inv[:, None] * t[None, :]).astype(np.float32)
    cos = np.ones((2, HD, SEQ), np.float32)
    sin = np.zeros((2, HD, SEQ), np.float32)
    cos[:, 0:8] = cos[:, 8:16] = np.cos(ang)
    sin[:, 0:8], sin[:, 8:16] = -np.sin(ang), np.sin(ang)
    by_half = [np.ascontiguousarray(a.reshape(P, 2, HALF).transpose(1, 0, 2)) for a in (cos, sin)]
    coef = np.array([[w >= 4, w >= 8, w >= 16, 1.0 / w] for w in WINDOWS], np.float32)
    first = np.array([1.0 / np.minimum(np.arange(16) + 1.0, w) for w in WINDOWS], np.float32)
    return {
        "x": x[0],
        "x_t": x[0].T,
        "wall": wall,
        "a_gw": a_group_w,
        "a_scale": a_scale.reshape(DEPTH, A_GROUPS, P).transpose(2, 0, 1),
        "sinks": b_sinks.reshape(DEPTH, 2, B_TILES).transpose(0, 2, 1).reshape(1, -1),
        "rel_rev": c_rel_bias.reshape(DEPTH * 8, 2 * MAX_REL + 1)[:, ::-1],
        "ln_gain": ln_gain.reshape(DEPTH, 4, 512),
        "ln_bias": ln_bias.reshape(DEPTH, 4, 512),
        "rope_cos": by_half[0],
        "rope_sin": by_half[1],
        "pool_coef": np.broadcast_to(coef, (P,) + coef.shape),
        "pool_inv": np.broadcast_to(first, (P,) + first.shape),
    }


def kernel(x, w_in, a_group_w, a_scale, b_sinks, c_rel_bias, w_out, ln_gain, ln_bias):
    import concourse.bacc as bacc
    from concourse.bass_utils import run_bass_kernel_spmd

    given = laid_out(*(np.asarray(a) for a in (x, w_in, a_group_w, a_scale, b_sinks, c_rel_bias, w_out,
                                               ln_gain, ln_bias)))
    nc = bacc.Bacc("TRN2", target_bir_lowering=False, num_devices=1)
    arrays, args = {}, {}
    for name, a in given.items():
        a = np.ascontiguousarray(a)
        arrays[f"in_{name}"] = a
        args[name] = nc.dram_tensor(f"in_{name}", a.shape, mybir.dt.from_np(a.dtype), kind="ExternalInput").ap()
    out = nc.dram_tensor("out", (SEQ, D), F32, kind="ExternalOutput").ap()
    build(nc, out=out, **args)
    r = run_bass_kernel_spmd(nc, [arrays], core_ids=[0])
    return r.results[0]["out"].reshape(1, SEQ, D)
```
